# Optimizing a Trainium2 kernel written in Bass

```python
import math
import jax, jax.numpy as jnp
from jax import lax
import numpy as np

D_MODEL = 1024
BATCH = 1
SEQ = 256
DEPTH = 1

N_MEM = 256
D_MIX = D_MODEL
D_MLSTM = D_MIX // 2
N_MLSTM_HEADS = 4
MLSTM_HEAD_DIM = D_MLSTM // N_MLSTM_HEADS
MLSTM_CHUNK = 128
CONV_WIDTH = 5
D_GMLP = D_MIX - D_MLSTM
N_GMLP_GROUPS = 4
GMLP_GROUP_DIM = D_GMLP // N_GMLP_GROUPS
GMLP_CHUNK = 128
N_GATES = 4 * N_MLSTM_HEADS
PROJ_COLS = 4 * D_MLSTM + N_GATES + 2 * D_GMLP
N_XATTN_HEADS = 4
XATTN_HEAD_DIM = D_MODEL // N_XATTN_HEADS
N_EXPERT_GROUPS = 4
EXPERTS_PER_GROUP = 8
N_EXPERTS = N_EXPERT_GROUPS * EXPERTS_PER_GROUP
TOP_K_IN_GROUP = 2
D_EXPERT = D_MODEL // 2
MOE_BLOCK = 128
RMS_EPS = 1e-6
LN_EPS = 1e-5
NEG_INIT = -1e30


def rms_norm(x, g):
    xf = x.astype(jnp.float32)
    y = xf * lax.rsqrt(jnp.mean(xf * xf, axis=-1, keepdims=True) + RMS_EPS)
    return (y * g.astype(jnp.float32)).astype(x.dtype)

def layer_norm(x, g, b):
    xf = x.astype(jnp.float32)
    mu = jnp.mean(xf, axis=-1, keepdims=True)
    xc = xf - mu
    y = xc * lax.rsqrt(jnp.mean(xc * xc, axis=-1, keepdims=True) + LN_EPS)
    return (y * g.astype(jnp.float32) + b.astype(jnp.float32)).astype(x.dtype)

def mlstm_chunkwise(q, k, v, i_pre, f_pre):
    Bq, H, S, dh = q.shape
    L = MLSTM_CHUNK
    NC = S // L
    q = q.reshape(Bq, H, NC, L, dh)
    k = k.reshape(Bq, H, NC, L, dh) * (dh ** -0.5)
    v = v.reshape(Bq, H, NC, L, dh)
    ig = i_pre.reshape(Bq, H, NC, L)
    b = jnp.cumsum(jax.nn.log_sigmoid(f_pre.reshape(Bq, H, NC, L)), axis=-1)
    F = b[..., -1]
    a = F[..., None] - b + ig
    m_loc = jnp.max(a, axis=-1)
    kw = k * jnp.exp(a - m_loc[..., None])[..., None]
    C_loc = jnp.einsum('bhcsd,bhcse->bhcde', kw, v)
    n_loc = jnp.sum(kw, axis=-2)

    def step(carry, inp):
        C, n, m = carry
        F_c, m_c, C_c, n_c = inp
        m_new = jnp.maximum(F_c + m, m_c)
        s_old = jnp.exp(F_c + m - m_new)
        s_new = jnp.exp(m_c - m_new)
        C_new = s_old[..., None, None] * C + s_new[..., None, None] * C_c
        n_new = s_old[..., None] * n + s_new[..., None] * n_c
        return (C_new, n_new, m_new), (C, n, m)

    init = (jnp.zeros((Bq, H, dh, dh), jnp.float32),
            jnp.zeros((Bq, H, dh), jnp.float32),
            jnp.full((Bq, H), NEG_INIT, jnp.float32))
    xs = (jnp.moveaxis(F, 2, 0), jnp.moveaxis(m_loc, 2, 0),
          jnp.moveaxis(C_loc, 2, 0), jnp.moveaxis(n_loc, 2, 0))
    _, (C_prev, n_prev, m_prev) = lax.scan(step, init, xs)
    C_prev = jnp.moveaxis(C_prev, 0, 2)
    n_prev = jnp.moveaxis(n_prev, 0, 2)
    m_prev = jnp.moveaxis(m_prev, 0, 2)

    mask = jnp.tril(jnp.ones((L, L), dtype=bool))
    Dm = jnp.where(mask, b[..., :, None] - b[..., None, :] + ig[..., None, :], -jnp.inf)
    inter = b + m_prev[..., None]
    m_t = jnp.maximum(inter, jnp.max(Dm, axis=-1))
    Wqk = jnp.exp(Dm - m_t[..., None]) * jnp.einsum('bhctd,bhcsd->bhcts', q, k)
    s_inter = jnp.exp(inter - m_t)
    num = (jnp.einsum('bhcts,bhcse->bhcte', Wqk, v)
           + s_inter[..., None] * jnp.einsum('bhctd,bhcde->bhcte', q, C_prev))
    den = jnp.sum(Wqk, axis=-1) + s_inter * jnp.einsum('bhctd,bhcd->bhct', q, n_prev)
    h = num / jnp.maximum(jnp.abs(den), jnp.exp(-m_t))[..., None]
    return h.reshape(Bq, H, S, dh)

def parallel_mixer(h, w_in, conv_w, conv_b, gate_b, g_head, ln_v_g, ln_v_b, w_s, b_s, w_out):
    Bq, S, _ = h.shape
    z = h @ w_in
    cuts = [D_MLSTM, 2 * D_MLSTM, 3 * D_MLSTM, 4 * D_MLSTM,
            4 * D_MLSTM + N_GATES, 4 * D_MLSTM + N_GATES + D_GMLP]
    q, k, v, o, gates, gu, gv = jnp.split(z, cuts, axis=-1)

    qk = lax.conv_general_dilated(jnp.concatenate([q, k], axis=-1), conv_w, (1,), 'SAME',
                                  dimension_numbers=('NWC', 'WIO', 'NWC'),
                                  feature_group_count=2 * D_MLSTM)
    qk = jax.nn.silu(qk + conv_b)
    q, k = qk[..., :D_MLSTM], qk[..., D_MLSTM:]

    def heads(t):
        return t.reshape(Bq, S, N_MLSTM_HEADS, MLSTM_HEAD_DIM).transpose(0, 2, 1, 3).astype(jnp.float32)

    qh, kh, vh = heads(q), heads(k), heads(v)
    g = (gates.astype(jnp.float32) + gate_b.astype(jnp.float32)).reshape(Bq, S, 4, N_MLSTM_HEADS)
    g = g.transpose(2, 0, 3, 1)
    i_f, f_f, i_b, f_b = g[0], g[1], g[2], g[3]

    def flip(t):
        return jnp.flip(t, axis=2)

    h_fwd = mlstm_chunkwise(qh, kh, vh, i_f, f_f)
    h_bwd = flip(mlstm_chunkwise(flip(qh), flip(kh), flip(vh), flip(i_b), flip(f_b)))
    hs = h_fwd + h_bwd
    gh = g_head.astype(jnp.float32).reshape(N_MLSTM_HEADS, 1, MLSTM_HEAD_DIM)
    hs = hs * lax.rsqrt(jnp.mean(hs * hs, axis=-1, keepdims=True) + RMS_EPS) * gh
    hs = hs.transpose(0, 2, 1, 3).reshape(Bq, S, D_MLSTM)
    y_mlstm = (jax.nn.sigmoid(o.astype(jnp.float32)) * hs).astype(h.dtype)

    gu = jax.nn.gelu(gu)
    gv = layer_norm(jax.nn.gelu(gv), ln_v_g, ln_v_b)
    NC = S // GMLP_CHUNK
    gv = gv.reshape(Bq, NC, GMLP_CHUNK, N_GMLP_GROUPS, GMLP_GROUP_DIM)
    sp = jnp.einsum('gts,bcsgd->bctgd', w_s, gv) + b_s.T[:, :, None]
    y_gmlp = gu * sp.reshape(Bq, S, D_GMLP)

    return jnp.concatenate([y_mlstm, y_gmlp], axis=-1) @ w_out

def memory_cross_attention(h, hm, w_q, w_kv, w_o):
    Bq, S, _ = h.shape
    M = hm.shape[1]
    q = (h @ w_q).reshape(Bq, S, N_XATTN_HEADS, XATTN_HEAD_DIM)
    kv = (hm @ w_kv).reshape(Bq, M, 2, N_XATTN_HEADS, XATTN_HEAD_DIM)
    k, v = kv[:, :, 0], kv[:, :, 1]
    s = jnp.einsum('bshd,bmhd->bhsm', q, k).astype(jnp.float32) * (XATTN_HEAD_DIM ** -0.5)
    p = jax.nn.softmax(s, axis=-1).astype(h.dtype)
    o = jnp.einsum('bhsm,bmhd->bshd', p, v).reshape(Bq, S, N_XATTN_HEADS * XATTN_HEAD_DIM)
    return o @ w_o

def hier_moe(h, w_rg, b_rg, w_re, b_re, w_gate, w_up, w_down):
    T, D = h.shape
    g_logits = (h @ w_rg).astype(jnp.float32) + b_rg.astype(jnp.float32)
    p_group = jax.nn.softmax(g_logits, axis=-1)
    p_top, g_idx = lax.top_k(p_group, 1)
    e_logits = ((h @ w_re).astype(jnp.float32) + b_re.astype(jnp.float32)).reshape(
        T, N_EXPERT_GROUPS, EXPERTS_PER_GROUP)
    e_logits = jnp.take_along_axis(e_logits, g_idx[:, :, None], axis=1)[:, 0]
    e_top, e_local = lax.top_k(e_logits, TOP_K_IN_GROUP)
    weights = p_top * jax.nn.softmax(e_top, axis=-1)
    expert_id = g_idx * EXPERTS_PER_GROUP + e_local

    A = T * TOP_K_IN_GROUP
    e_flat = expert_id.reshape(A)
    t_flat = jnp.repeat(jnp.arange(T), TOP_K_IN_GROUP)
    w_flat = weights.reshape(A)
    order = jnp.argsort(e_flat)
    e_sorted, t_sorted, w_sorted = e_flat[order], t_flat[order], w_flat[order]
    counts = jnp.bincount(e_flat, length=N_EXPERTS)
    padded = ((counts + MOE_BLOCK - 1) // MOE_BLOCK) * MOE_BLOCK
    start = jnp.cumsum(counts) - counts
    pend = jnp.cumsum(padded)
    pstart = pend - padded
    dest = pstart[e_sorted] + (jnp.arange(A) - start[e_sorted])
    NB = A // MOE_BLOCK + N_EXPERTS
    P = NB * MOE_BLOCK
    x_disp = jnp.zeros((P, D), h.dtype).at[dest].set(h[t_sorted])
    blk_e = jnp.clip(jnp.searchsorted(pend, jnp.arange(NB) * MOE_BLOCK, side='right'), 0, N_EXPERTS - 1)

    def expert_block(args):
        xb, e = args
        return (jax.nn.silu(xb @ w_gate[e]) * (xb @ w_up[e])) @ w_down[e]

    y_disp = lax.map(expert_block, (x_disp.reshape(NB, MOE_BLOCK, D), blk_e)).reshape(P, D)
    contrib = (w_sorted[:, None] * y_disp[dest].astype(jnp.float32))
    out = jnp.zeros((T, D), jnp.float32).at[t_sorted].add(contrib)
    return out.astype(h.dtype)

def first_inputs(seed: int = 0) -> dict:
    key = jax.random.key(seed)
    ks = jax.random.split(key, 32)

    def nrm(k, shape, scale):
        return jax.random.normal(k, shape, jnp.float32) * scale

    def gain(k, shape):
        return 1.0 + 0.1 * jax.random.normal(k, shape, jnp.float32)

    H = N_MLSTM_HEADS
    f_bias = jnp.linspace(3.0, 6.0, H, dtype=jnp.float32)
    gk = jax.random.split(ks[6], 4)
    gate_b = jnp.concatenate([
        nrm(gk[0], (DEPTH, H), 0.1),
        f_bias + nrm(gk[1], (DEPTH, H), 0.1),
        nrm(gk[2], (DEPTH, H), 0.1),
        f_bias + nrm(gk[3], (DEPTH, H), 0.1)], axis=-1)
    return {
        'x': nrm(ks[0], (BATCH, SEQ, D_MODEL), 1.0),
        'mem': nrm(ks[1], (BATCH, N_MEM, D_MODEL), 1.0),
        'g_mix': gain(ks[2], (DEPTH, D_MODEL)),
        'w_in': nrm(ks[3], (DEPTH, D_MODEL, PROJ_COLS), D_MODEL ** -0.5),
        'conv_w': nrm(ks[4], (DEPTH, CONV_WIDTH, 1, 2 * D_MLSTM), CONV_WIDTH ** -0.5),
        'conv_b': nrm(ks[5], (DEPTH, 2 * D_MLSTM), 0.01),
        'gate_b': gate_b,
        'g_head': gain(ks[7], (DEPTH, D_MLSTM)),
        'ln_v_g': gain(ks[8], (DEPTH, D_GMLP)),
        'ln_v_b': nrm(ks[9], (DEPTH, D_GMLP), 0.01),
        'w_s': nrm(ks[10], (DEPTH, N_GMLP_GROUPS, GMLP_CHUNK, GMLP_CHUNK), GMLP_CHUNK ** -0.5),
        'b_s': gain(ks[11], (DEPTH, N_GMLP_GROUPS, GMLP_CHUNK)),
        'w_out': nrm(ks[12], (DEPTH, D_MIX, D_MODEL), D_MIX ** -0.5),
        'g_xattn': gain(ks[13], (DEPTH, D_MODEL)),
        'g_mem': gain(ks[14], (DEPTH, D_MODEL)),
        'w_q_x': nrm(ks[15], (DEPTH, D_MODEL, N_XATTN_HEADS * XATTN_HEAD_DIM), D_MODEL ** -0.5),
        'w_kv_x': nrm(ks[16], (DEPTH, D_MODEL, 2 * N_XATTN_HEADS * XATTN_HEAD_DIM), D_MODEL ** -0.5),
        'w_o_x': nrm(ks[17], (DEPTH, N_XATTN_HEADS * XATTN_HEAD_DIM, D_MODEL), D_MODEL ** -0.5),
        'g_moe': gain(ks[18], (DEPTH, D_MODEL)),
        'w_rg': nrm(ks[19], (DEPTH, D_MODEL, N_EXPERT_GROUPS), D_MODEL ** -0.5),
        'b_rg': nrm(ks[20], (DEPTH, N_EXPERT_GROUPS), 0.01),
        'w_re': nrm(ks[21], (DEPTH, D_MODEL, N_EXPERTS), D_MODEL ** -0.5),
        'b_re': nrm(ks[22], (DEPTH, N_EXPERTS), 0.01),
        'w_gate': nrm(ks[23], (DEPTH, N_EXPERTS, D_MODEL, D_EXPERT), D_MODEL ** -0.5),
        'w_up': nrm(ks[24], (DEPTH, N_EXPERTS, D_MODEL, D_EXPERT), D_MODEL ** -0.5),
        'w_down': nrm(ks[25], (DEPTH, N_EXPERTS, D_EXPERT, D_MODEL), D_EXPERT ** -0.5),
        'g_final': gain(ks[26], (D_MODEL,)),
    }

def first_block(x, mem, g_mix, w_in, conv_w, conv_b, gate_b, g_head, ln_v_g, ln_v_b, w_s, b_s, w_out,
              g_xattn, g_mem, w_q_x, w_kv_x, w_o_x, g_moe, w_rg, b_rg, w_re, b_re,
              w_gate, w_up, w_down, g_final):
    Bq, S, D = x.shape
    for l in range(DEPTH):
        x = x + parallel_mixer(rms_norm(x, g_mix[l]), w_in[l], conv_w[l], conv_b[l], gate_b[l],
                               g_head[l], ln_v_g[l], ln_v_b[l], w_s[l], b_s[l], w_out[l])
        x = x + memory_cross_attention(rms_norm(x, g_xattn[l]), rms_norm(mem, g_mem[l]),
                                       w_q_x[l], w_kv_x[l], w_o_x[l])
        x = x + hier_moe(rms_norm(x, g_moe[l]).reshape(Bq * S, D), w_rg[l], b_rg[l], w_re[l], b_re[l],
                         w_gate[l], w_up[l], w_down[l]).reshape(Bq, S, D)
    return rms_norm(x, g_final)


DEPTH_2 = 2

GRID_W = 64
CTX_LEN = 256
D_MIX_2 = D_MODEL
W_F = D_MIX_2 // 4
W_ATT = D_MIX_2 // 4
W_CONV = D_MIX_2 // 4
W_POOL = D_MIX_2 // 4
HEAD_DIM = 64
N_HEADS = W_ATT // HEAD_DIM
N_KV_HEADS = N_HEADS // 2
GQA = N_HEADS // N_KV_HEADS
KV_DIM = N_KV_HEADS * HEAD_DIM
ATT_SCALE = HEAD_DIM ** -0.5
ROPE_FREQS = HEAD_DIM // 4
ROPE_THETA = 10000.0
Q_BLOCK = 128
F_HEADS = 4
F_DIM = W_F // F_HEADS
CONV_W = 3
POOL_WINDOWS = (2, 4, 8, 16)
POOL_DIM = W_POOL // len(POOL_WINDOWS)
EPS = 1e-6
SPLIT_WIDTHS = (W_ATT, KV_DIM, KV_DIM, W_ATT, W_F, W_F, W_CONV, W_CONV, W_CONV, W_CONV, W_POOL, W_POOL)
D_IN = sum(SPLIT_WIDTHS)


def _split_cols(p):
    return jnp.split(p, np.cumsum(SPLIT_WIDTHS)[:-1].tolist(), axis=-1)

def _rmsnorm(x, g):
    xf = x.astype(jnp.float32)
    y = xf * lax.rsqrt(jnp.mean(xf * xf, axis=-1, keepdims=True) + EPS)
    return (y * g.astype(jnp.float32)).astype(x.dtype)

def _axial_angles(n):
    n_rows = n // GRID_W
    row = jnp.repeat(jnp.arange(n_rows), GRID_W).astype(jnp.float32)
    col = jnp.tile(jnp.arange(GRID_W), n_rows).astype(jnp.float32)
    inv = ROPE_THETA ** (-jnp.arange(ROPE_FREQS, dtype=jnp.float32) / ROPE_FREQS)
    return row[:, None] * inv, col[:, None] * inv

def _rotate(x, ang):
    f = ang.shape[-1]
    cos = jnp.cos(ang)[None, :, None, :].astype(x.dtype)
    sin = jnp.sin(ang)[None, :, None, :].astype(x.dtype)
    x1, x2 = x[..., :f], x[..., f:]
    return jnp.concatenate([x1 * cos - x2 * sin, x2 * cos + x1 * sin], axis=-1)

def _axial_rope(x, ang_row, ang_col):
    half = HEAD_DIM // 2
    return jnp.concatenate([_rotate(x[..., :half], ang_row), _rotate(x[..., half:], ang_col)], axis=-1)

def _latent_attention(q, k, v, kc, vc):
    b, s = q.shape[0], q.shape[1]
    nblk = s // Q_BLOCK
    k_all = jnp.concatenate([kc, k], axis=1)
    v_all = jnp.concatenate([vc, v], axis=1)
    qb = q.reshape(b, nblk, Q_BLOCK, N_KV_HEADS, GQA, HEAD_DIM).transpose(1, 0, 2, 3, 4, 5)

    def one_block(qi):
        sc = jnp.einsum('bqkgd,bskd->bkgqs', qi, k_all, preferred_element_type=jnp.float32)
        p = jax.nn.softmax(sc, axis=-1).astype(v_all.dtype)
        return jnp.einsum('bkgqs,bskd->bqkgd', p, v_all)

    o = lax.map(one_block, qb)
    return o.transpose(1, 0, 2, 3, 4, 5).reshape(b, s, W_ATT)

def _context_attention(qc, kc, vc):
    b, n = qc.shape[0], qc.shape[1]
    qg = qc.reshape(b, n, N_KV_HEADS, GQA, HEAD_DIM)
    sc = jnp.einsum('bqkgd,bskd->bkgqs', qg, kc, preferred_element_type=jnp.float32)
    p = jax.nn.softmax(sc, axis=-1).astype(vc.dtype)
    return jnp.einsum('bkgqs,bskd->bqkgd', p, vc).reshape(b, n, W_ATT)

def _fourier_branch(u, z, w_fourier):
    b, n, _ = u.shape
    uf = u.astype(jnp.float32).reshape(b, n, F_HEADS, F_DIM)
    y = jnp.fft.fftn(uf, axes=(1, 3), norm='ortho').real.reshape(b, n, W_F).astype(u.dtype)
    return jax.nn.silu(z) * (y @ w_fourier)

def _conv_branch(bg, cg, hv, z, conv_w, conv_b):
    t = cg * hv
    tp = jnp.pad(t, ((0, 0), (1, 1), (0, 0)))
    y = tp[:, :-2] * conv_w[0] + tp[:, 1:-1] * conv_w[1] + tp[:, 2:] * conv_w[2] + conv_b
    return jax.nn.silu(z) * (bg * y)

def _pool_branch(u, z, pool_w, pool_scale):
    b, n, _ = u.shape
    cs = jnp.cumsum(u.astype(jnp.float32), axis=1)
    cs = jnp.concatenate([jnp.zeros((b, 1, W_POOL), jnp.float32), cs], axis=1)
    pos = jnp.arange(n)
    outs = []
    for i, w in enumerate(POOL_WINDOWS):
        left = w // 2
        right = w - 1 - left
        lo = jnp.clip(pos - left, 0, n)
        hi = jnp.clip(pos + right + 1, 0, n)
        sl = slice(i * POOL_DIM, (i + 1) * POOL_DIM)
        mean = (cs[:, hi, sl] - cs[:, lo, sl]) / (hi - lo).astype(jnp.float32)[None, :, None]
        d = (mean - u[..., sl].astype(jnp.float32)).astype(u.dtype)
        outs.append(d @ pool_w[i])
    y = jnp.concatenate(outs, axis=-1) * pool_scale
    return jax.nn.silu(z) * y

def _local_branches(parts, w_fourier, conv_w, conv_b, pool_w, pool_scale):
    _, _, _, _, u_f, z_f, b_c, c_c, h_c, z_c, u_p, z_p = parts
    o_f = _fourier_branch(u_f, z_f, w_fourier)
    o_c = _conv_branch(b_c, c_c, h_c, z_c, conv_w, conv_b)
    o_p = _pool_branch(u_p, z_p, pool_w, pool_scale)
    return o_f, o_c, o_p

def _layer(x, xc, c, c_ctx, ang_row, ang_col, w_mod, b_mod, norm_g, w_in, q_gain, k_gain,
           w_fourier, conv_w, conv_b, pool_w, pool_scale, w_out, ctx_out):
    b, s, _ = x.shape
    n_ctx = xc.shape[1]
    shift, scale, gate = jnp.split(jax.nn.silu(c) @ w_mod + b_mod, 3, axis=-1)
    shift_c, scale_c, gate_c = jnp.split(jax.nn.silu(c_ctx) @ w_mod + b_mod, 3, axis=-1)
    h = _rmsnorm(x, norm_g) * (1.0 + scale[:, None]) + shift[:, None]
    hc = _rmsnorm(xc, norm_g) * (1.0 + scale_c) + shift_c

    parts = _split_cols(h @ w_in)
    if ctx_out:
        parts_c = _split_cols(hc @ w_in)
        kc_raw, vc_raw = parts_c[1], parts_c[2]
    else:
        kc_raw, vc_raw = jnp.split(hc @ w_in[:, W_ATT:W_ATT + 2 * KV_DIM], 2, axis=-1)
    kc = _rmsnorm(kc_raw.reshape(b, n_ctx, N_KV_HEADS, HEAD_DIM), k_gain)
    vc = vc_raw.reshape(b, n_ctx, N_KV_HEADS, HEAD_DIM)

    q = _rmsnorm(parts[0].reshape(b, s, N_HEADS, HEAD_DIM), q_gain)
    k = _rmsnorm(parts[1].reshape(b, s, N_KV_HEADS, HEAD_DIM), k_gain)
    v = parts[2].reshape(b, s, N_KV_HEADS, HEAD_DIM)
    q = _axial_rope(q, ang_row, ang_col) * ATT_SCALE
    k = _axial_rope(k, ang_row, ang_col)
    o_att = jax.nn.silu(parts[3]) * _latent_attention(q, k, v, kc, vc)
    o_f, o_c, o_p = _local_branches(parts, w_fourier, conv_w, conv_b, pool_w, pool_scale)
    out = jnp.concatenate([o_f, o_att, o_c, o_p], axis=-1) @ w_out
    x_new = x + gate[:, None] * out

    if ctx_out:
        qc = _rmsnorm(parts_c[0].reshape(b, n_ctx, N_HEADS, HEAD_DIM), q_gain) * ATT_SCALE
        oc_att = jax.nn.silu(parts_c[3]) * _context_attention(qc, kc, vc)
        oc_f, oc_c, oc_p = _local_branches(parts_c, w_fourier, conv_w, conv_b, pool_w, pool_scale)
        out_c = jnp.concatenate([oc_f, oc_att, oc_c, oc_p], axis=-1) @ w_out
        xc = xc + gate_c * out_c
    return x_new, xc

def second_inputs(seed: int = 0) -> dict:
    key = jax.random.key(seed)
    ks = jax.random.split(key, 20)
    f32 = jnp.float32
    nrm = lambda k, shape: jax.random.normal(k, shape, f32)
    return {
        "x": nrm(ks[0], (BATCH, SEQ, D_MODEL)),
        "c": nrm(ks[1], (BATCH, D_MODEL)),
        "ctx": nrm(ks[2], (BATCH, CTX_LEN, D_MODEL)),
        "c_ctx": nrm(ks[3], (D_MODEL,)),
        "w_mod": nrm(ks[4], (DEPTH_2, D_MODEL, 3 * D_MODEL)) * (0.5 * D_MODEL ** -0.5),
        "b_mod": nrm(ks[5], (DEPTH_2, 3 * D_MODEL)) * 0.02,
        "norm_g": 1.0 + 0.05 * nrm(ks[6], (DEPTH_2, D_MODEL)),
        "w_in": nrm(ks[7], (DEPTH_2, D_MODEL, D_IN)) * D_MODEL ** -0.5,
        "q_gain": 1.0 + 0.05 * nrm(ks[8], (DEPTH_2, HEAD_DIM)),
        "k_gain": 1.0 + 0.05 * nrm(ks[9], (DEPTH_2, HEAD_DIM)),
        "w_fourier": nrm(ks[10], (DEPTH_2, W_F, W_F)) * W_F ** -0.5,
        "conv_w": nrm(ks[11], (DEPTH_2, CONV_W, W_CONV)) * CONV_W ** -0.5,
        "conv_b": nrm(ks[12], (DEPTH_2, W_CONV)) * 0.02,
        "pool_w": nrm(ks[13], (DEPTH_2, len(POOL_WINDOWS), POOL_DIM, POOL_DIM)) * POOL_DIM ** -0.5,
        "pool_scale": 1.0 + 0.1 * nrm(ks[14], (DEPTH_2, W_POOL)),
        "w_out": nrm(ks[15], (DEPTH_2, D_MIX_2, D_MODEL)) * D_MIX_2 ** -0.5,
    }

def second_block(x, c, ctx, c_ctx, w_mod, b_mod, norm_g, w_in, q_gain, k_gain,
              w_fourier, conv_w, conv_b, pool_w, pool_scale, w_out):
    ang_row, ang_col = _axial_angles(x.shape[1])
    xc = ctx
    for l in range(DEPTH_2):
        x, xc = _layer(x, xc, c, c_ctx, ang_row, ang_col, w_mod[l], b_mod[l], norm_g[l], w_in[l],
                       q_gain[l], k_gain[l], w_fourier[l], conv_w[l], conv_b[l], pool_w[l],
                       pool_scale[l], w_out[l], ctx_out=(l < DEPTH_2 - 1))
    return x


def setup_inputs(seed=0):
    out = dict(first_inputs(seed))
    for name, value in second_inputs(seed + 1).items():
        if name != "x":
            out[name + "_2"] = value
    return out


def reference(
    x, mem, g_mix, w_in, conv_w, conv_b, gate_b, g_head, ln_v_g, ln_v_b, w_s, b_s, w_out,
    g_xattn, g_mem, w_q_x, w_kv_x, w_o_x, g_moe, w_rg, b_rg, w_re, b_re, w_gate, w_up, w_down,
    g_final, c_2, ctx_2, c_ctx_2, w_mod_2, b_mod_2, norm_g_2, w_in_2, q_gain_2, k_gain_2,
    w_fourier_2, conv_w_2, conv_b_2, pool_w_2, pool_scale_2, w_out_2,
):
    x = first_block(
        x, mem, g_mix, w_in, conv_w, conv_b, gate_b, g_head, ln_v_g, ln_v_b, w_s, b_s, w_out,
        g_xattn, g_mem, w_q_x, w_kv_x, w_o_x, g_moe, w_rg, b_rg, w_re, b_re, w_gate, w_up,
        w_down, g_final,
    )
    return second_block(
        x, c_2, ctx_2, c_ctx_2, w_mod_2, b_mod_2, norm_g_2, w_in_2, q_gain_2, k_gain_2,
        w_fourier_2, conv_w_2, conv_b_2, pool_w_2, pool_scale_2, w_out_2,
    )


_drawn_inputs = setup_inputs


def setup_inputs(seed=0):
    import zlib

    import numpy as np

    out = dict(_drawn_inputs(seed))
    spreads = {}
    factors = {'conv_b': 8.0,
     'ln_v_b': 4.162,
     'b_rg': 8.0,
     'b_re': 4.991,
     'ctx_2': 7.166,
     'b_mod_2': 2.791,
     'q_gain_2': 8.0,
     'k_gain_2': 8.0,
     'conv_b_2': 8.0,
     'pool_scale_2': 4.25}
    for name, (base, spread) in spreads.items():
        noise = np.random.default_rng([zlib.crc32(name.encode()), seed]).standard_normal(out[name].shape)
        drawn = base * np.exp(spread * noise) if base else spread * noise
        out[name] = __import__('jax').numpy.asarray(drawn.astype(out[name].dtype))
    for name, factor in factors.items():
        out[name] = (out[name] * factor).astype(out[name].dtype)
    return out
```

```python
from contextlib import ExitStack

import concourse.bass as bass
from concourse import mybir

F32 = mybir.dt.float32
I32 = mybir.dt.int32
ALU = mybir.AluOpType
ACT = mybir.ActivationFunctionType
AX = mybir.AxisListType

P = 128
D = 1024
KT = D // P
S = 256
TT = S // P
NH = 4
DM = 512
NE = 32
NG = 4
EPG = NE // NG
FE = 512
C = 64
A = 2 * S
AP_ = A + C
RMS_EPS, LN_EPS = 1e-6, 1e-5
BIG = 1e30
SLOTS = 6
CW = 4096
HD2 = 64
W2 = 256
QK_SCALE = 128.0 ** -0.5
X_SCALE = 256.0 ** -0.5
A_SCALE = 64.0 ** -0.5

ID0, TRF0, TRB0, TRS0, ONE0, MKF0, MKB0, IO0 = (i * P for i in range(8))
CONST1 = IO0 + A
DFT0, CD0, POOL0, ROPE0 = 0, 1024, 1280, 1280 + 2048
CONST2 = ROPE0 + 128
WF0 = CONST2

V_GMIX, V_CB, V_CW, V_GX, V_GMEM, V_GMOE, V_GFIN, V_GHEAD, V_BS, NV1 = 0, 8, 16, 56, 64, 72, 80, 88, 92, 96
V_NG, V_BMOD, V_C, V_CW2, V_CB2, V_PS, NV2 = 0, 16, 64, 80, 92, 96, 100

ORDER = [("vec", "v")]
ORDER += [(f"x{g}", "a") for g in range(4)] + [("ss1", "a")]
ORDER += [(f"mem{g}", "a") for g in range(4)] + [("ws", "a")] + [(f"ctx{g}", "a") for g in range(4)]
ORDER += [(f"qk{g}", "a") for g in range(4)] + [("gate", "v")]
ORDER += [(f"v{t}", "a") for t in range(2)] + [(f"o{t}", "a") for t in range(2)]
ORDER += [(f"gv{t}", "a") for t in range(2)] + [(f"gu{t}", "a") for t in range(2)]
ORDER += [("ss2", "a")] + [(f"km{g}", "a") for g in range(4)]
ORDER += [("bcum", "v"), ("apT", "v")] + [(f"vm{g}", "a") for g in range(4)] + [("mxb", "v")]
ORDER += [(f"A{j}", "v") for j in range(4)] + [("mod0", "v")]
ORDER += [(f"KT{d}", "v") for d in range(2)] + [(f"QK{t}", "v") for t in range(2)]
ORDER += [(f"C{d}", "a") for d in range(2)] + [("nn", "v")] + [(f"SP{t}", "v") for t in range(2)]
ORDER += [(f"WT{j}", "a") for j in range(4)] + [("dI", "v")]
ORDER += [(f"NI{j}", "v") for j in range(4)] + [(f"CI{d}", "v") for d in range(2)]
ORDER += [(f"yT{g}", "v") for g in range(4)] + [(f"wo{g}", "v") for g in range(4)]
ORDER += [("ss3", "a")] + [(f"xq{g}", "a") for g in range(4)] + [(f"S{g}", "a") for g in range(4)]
ORDER += [(f"pT{h}", "a") for h in range(4)] + [(f"xo{h}", "a") for h in range(4)]
ORDER += [(f"xw{g}", "v") for g in range(4)]
ORDER += [("ss4", "a"), ("lg", "v")] + [(f"hk{g}", "a") for g in range(4)] + [("mod1", "a")]
ORDER += [("pos", "v"), ("start", "v")] + [(f"xs{k}", "a") for k in range(8)]
LOOP_AT = len(ORDER)
ORDER += [(f"pw{g}", "a") for g in range(2)] + [(f"yt{g}", "va"[g % 2]) for g in range(8)]
ORDER += [(f"co{g}", "v") for g in range(4)] + [("ss5", "a")]
CH_TILES = ["zf0", "zf1", "za0", "za1", "zc0", "zc1", "zp0", "zp1"]
for L in range(2):
    ntt = 4 if L == 0 else 2
    ORDER += [(f"{L}ss", "a")]
    ORDER += [(f"{L}qkv{t}", "a") for t in range(4)]
    ORDER += [(f"{L}za{i}", "a") for i in range(2)] + [(f"{L}uf{t}", "a") for t in range(ntt // 2)]
    ORDER += [(f"{L}zf{i}", "a") for i in range(2)] + [(f"{L}b{i}", "a") for i in range(2)]
    ORDER += [(f"{L}c{i}", "a") for i in range(2)] + [(f"{L}h{i}", "v") for i in range(2)]
    ORDER += [(f"{L}zc{i}", "a") for i in range(2)] + [(f"{L}up{t}", "a") for t in range(ntt // 2)]
    ORDER += [(f"{L}zp{i}", "a") for i in range(2)]
    ORDER += [(f"{L}B{s}{i}", "a") for s in range(ntt // 2) for i in range(2)]
    ORDER += [(f"{L}dT{i}", "a") for i in range(2)]
    ORDER += [(f"{L}yf{i}", "a") for i in range(2)] + [(f"{L}pl{i}", "v") for i in range(2)]
    ORDER += [(f"{L}wf{i}", "v") for i in range(2)]
    ORDER += [(f"{L}hT{h}", "a") for h in range(6)]
    if L == 0:
        ORDER += [(f"{L}cS{g}", "a") for g in range(4)] + [(f"{L}cP{h}", "a") for h in range(4)]
        ORDER += [(f"{L}co{i}", "v") for i in range(2)]
    ORDER += [(f"{L}xS{g}", "a") for g in range(8)] + [(f"{L}xP{g}", "a") for g in range(8)]
    ORDER += [(f"{L}xo{i}", "v") for i in range(2)]
    ORDER += [(f"{L}out{k}", "v") for k in range(8)]
ORDER += [(f"fin{g}", "a") for g in range(4)]
INDEX = {name: n for n, (name, _) in enumerate(ORDER)}


def drained_by(name):
    n = INDEX[name]
    who = ORDER[n][1]
    return who, sum(1 for _, w in ORDER[:n + 1] if w == who)


def first_and_second_block(nc, t):
    w_in, w_in2 = t["w_in"][0], t["w_in_2"]

    def rows(w, c0, n):
        return w[:, c0:c0 + n].rearrange("(k p) n -> p k n", p=P)

    before, after = [], []
    for i, (c0, last) in enumerate([(0, "qk1"), (512, "qk3"), (1024, "v1"), (1536, "o1"), (2576, "gv1"),
                                    (2064, "gu1")]):
        before.append((f"in{i}", [(0, rows(w_in, c0, 512))], last))
    for i, last in enumerate(["km1", "km3", "vm1", "vm3"]):
        before.append((f"kv{i}", [(0, rows(t["w_kv_x"][0], 512 * i, 512))], last))
    before += [(f"mod0{i}", [(0, rows(t["w_mod_2"][0], 512 * i, 512))], "mod0") for i in range(6)]
    before += [(f"wout{i}", [(0, rows(t["w_out"][0], 512 * i, 512))], f"wo{2 * i + 1}") for i in range(2)]
    before += [(f"wq{i}", [(0, rows(t["w_q_x"][0], 512 * i, 512))], f"xq{2 * i + 1}") for i in range(2)]
    before += [(f"wox{i}", [(0, rows(t["w_o_x"][0], 512 * i, 512))], f"xw{2 * i + 1}") for i in range(2)]
    before += [(f"mod1{i}", [(0, rows(t["w_mod_2"][1], 512 * i, 512))], "mod1") for i in range(6)]
    for L in range(2):
        lasts = [f"{L}qkv3", f"{L}uf{1 - L}", f"{L}b1", f"{L}h1", f"{L}up{1 - L}", f"{L}zp1"]
        for i, last in enumerate(lasts):
            after.append((f"{L}in{i}", [(0, rows(w_in2[L], 512 * i, min(512, 2816 - 512 * i)))], last))
        after.append((f"{L}const", [(0, t["const2"]), (WF0, rows(t["w_fourier_2"][L], 0, W2))], f"{L}xS7"))
        after += [(f"{L}wout{i}", [(0, rows(t["w_out_2"][L], 512 * i, 512))], f"{L}out{4 * i + 3}")
                  for i in range(2)]
    NB = len(before)
    experts = ["G0", "U0"] + [f"{m}{e - (m == 'D')}" for e in range(1, NE) for m in "GUD"] + [f"D{NE - 1}"]
    place = {name: (n % SLOTS) for n, name in
             enumerate([c[0] for c in before] + experts + [c[0] for c in after])}
    count = [0] * SLOTS
    landed = {}
    for name, pieces in [c[:2] for c in before] + [(e, [0]) for e in experts] + [c[:2] for c in after]:
        count[place[name]] += 16 * len(pieces)
        landed[name] = count[place[name]]

    with ExitStack() as ctx:
        def sb(name, shape, dt=F32):
            return ctx.enter_context(nc.sbuf_tensor(name, shape, dt))

        def sem(name):
            return ctx.enter_context(nc.semaphore(name))

        ring = sb("ring", [P, SLOTS, CW])
        c1 = sb("c1", [P, CONST1])
        X = sb("X", [P, 2, KT, S])
        H = sb("H", [P, 2, KT, S])
        AR = 14368
        ar = sb("ar", [P, AR])
        raw = sb("raw", [P, 2, P])
        vT = sb("vT", [P, NV1 + NV2])
        wg = sb("wg", [P, KT, 16])
        wr = sb("wr", [P, KT, NG + NE])
        gate_b = sb("gate_b", [P, 16])
        rb = sb("rb", [P, NG + NE])
        lng = sb("lng", [P, DM])
        lnb = sb("lnb", [P, DM])
        gains = sb("gains", [P, 2, 6, HD2])
        wsr = sb("wsr", [P, NH, P])
        wsT = sb("wsT", [P, NH, P])
        pwb = sb("pwb", [P, 2, 2, P])
        sd = sb("sd", [P, 2, S])
        rs = sb("rs", [P, 2, S])
        mod = sb("mod", [P, 2, 24, 2])
        gsc = sb("gsc", [P, 2, KT, 2])
        sc = sb("sc", [P, 2, KT])
        sm = sb("sm", [P, 1200])
        win = sb("win", [1, 4 * NE], I32)
        mxc = sb("mxc", [1, 1], I32)

        bank = [ctx.enter_context(nc.psum_tensor(f"bank{i}", [P, 512], F32)) for i in range(8)]

        def slot(name, k=KT, n=512, c0=0):
            return ring[:, place[name], c0:c0 + k * n].rearrange("p (k n) -> p k n", k=k)

        ident, trf, trb = c1[:, ID0:ID0 + P], c1[:, TRF0:TRF0 + P], c1[:, TRB0:TRB0 + P]
        trs, ones = c1[:, TRS0:TRS0 + P], c1[:, ONE0:ONE0 + P]
        mask = [c1[:, MKF0:MKF0 + P], c1[:, MKB0:MKB0 + P]]
        iota = c1[:, IO0:IO0 + A]

        def view(at, cols, **dims):
            v = ar[:, at:at + cols]
            names = " ".join(dims)
            last = dict(list(dims.items())[:-1])
            return v.rearrange(f"p ({names}) -> p {names}", **last) if len(dims) > 1 else v

        qkp = view(0, 2080, k=8, s=260)
        W = view(0, 2048, u=16, s=128)
        num = view(0, 2048, u=16, s=128)
        qkT = view(2080, 2048, k=8, s=256)
        yT = qkT
        vs = view(4128, 1024, t=2, n=512)
        tho = view(5152, 1024, t=2, n=512)
        gu = view(6176, 1024, t=2, n=512)
        gv = view(7200, 1024, t=2, n=512)
        kmT = view(8224, 2048, k=8, s=256)
        vm = view(10272, 2048, t=2, n=1024)
        E = view(12320, 2048, u=16, s=128)
        WT = E
        Ej = view(12320, 1024, t=2, n=512)
        msq = view(12320, 2048, k=8, s=256)
        xin = view(10272, 2048, t=2, n=1024)
        memin = view(12320, 2048, t=2, n=1024)
        ctxin = view(8224, 2048, t=2, n=1024)
        h0 = H[:, 0].rearrange("p k s -> p (k s)")
        bd = h0[0:16, :].rearrange("p (u s) -> p u s", u=16)
        kw = h0[:, 0:1024].rearrange("p (d h s) -> p d h s", d=2, h=4)
        Cs = h0[:, 1024:2048].rearrange("p (d h s) -> p d h s", d=2, h=4)
        xqT = view(0, 2048, k=8, s=256)
        pTx = view(2080, 2048, h=4, m=2, s=256)
        oTx = view(4128, 2048, k=8, s=256)
        px = view(12320, 2048, t=2, h=4, m=256)
        hk = view(0, 2048, t=2, n=1024)
        Pm = view(2048, 1024, t=2, a=512)
        Pw = view(3072, 1024, t=2, a=512)
        xs = view(4096, 8 * AP_, k=8, a=AP_)
        ys = view(8704, 8 * AP_, k=8, a=AP_)
        xe = view(0, 1024, b=2, k=8, c=64)
        th = view(1024, 1024, b=2, f=512)[0:C]
        ac = view(2048, 1024, b=2, f=512)[0:C]
        acT = view(13312, 512, b=2, k=4, c=64)
        yb = h0.rearrange("p (b n) -> p b n", b=2)[0:C]
        yk = view(4096, 4096, a=4, n=1024)
        PwT = view(0, 1024, a=4, s=256)
        oT = view(0, 4096, k=8, r=2, s=256)
        qkv = view(4096, 2048, t=4, n=512)
        uf = view(6144, 1024, t=4, n=256)
        up = view(7168, 1024, t=4, n=256)
        bs2 = view(8192, 1024, k=2, r=2, s=256)
        cs2 = view(9216, 1024, k=2, r=2, s=256)
        tp = view(10240, 1032, k=2, r=2, s=258)
        q2T = view(11264, 3072, h=6, s=512)[0:HD2]
        px2 = view(6144, 4096, t=2, h=4, m=512)
        pc2 = view(6144, 2048, t=2, h=4, m=256)
        hf = H[:, :].rearrange("p r k s -> p (r k s)")
        B2 = hf[:, 0:2048].rearrange("p (r k s) -> p r k s", r=2, k=2)
        yf2 = hf[:, 2048:3072].rearrange("p (k r s) -> p k r s", k=2, r=2)
        dT2 = hf[:, 3072:4096].rearrange("p (k r s) -> p k r s", k=2, r=2)
        pT2 = hf.rearrange("p (h m s) -> p h m s", h=4, m=4)
        pcT2 = hf[:, 0:2048].rearrange("p (h m s) -> p h m s", h=4, m=2)
        outb = view(0, 2048, t=2, n=1024)

        ld_x, ld_mem, ld_ctx, ld_const, ld_vec, ld_misc = (
            sem(n) for n in ("ld_x", "ld_mem", "ld_ctx", "ld_const", "ld_vec", "ld_misc"))
        w_loaded = [sem(f"w_loaded{i}") for i in range(SLOTS)]
        psum_full = sem("psum_full")
        a_drained = sem("a_drained")
        v_drained = sem("v_drained")
        a_chain, v_chain = sem("a_chain"), sem("v_chain")
        sq_ready = sem("sq_ready")
        h_ready = sem("h_ready")
        conv_ready = sem("conv_ready")
        qk_ready = sem("qk_ready")
        nf_ready, lse_ready, lf_ready = sem("nf_ready"), sem("lse_ready"), sem("lf_ready")
        ap_ready, dmx_ready = sem("ap_ready"), sem("dmx_ready")
        em_ready, e_ready = sem("em_ready"), sem("e_ready")
        ei_ready, ee_ready = sem("ei_ready"), sem("ee_ready")
        w_ready, gvc_ready, gvs_ready, gvn_ready = (sem(n) for n in ("w_ready", "gvc_ready", "gvs_ready",
                                                                     "gvn_ready"))
        hss_ready, hsd_ready, y_ready = sem("hss_ready"), sem("hsd_ready"), sem("y_ready")
        mx_ready, px_ready, pn_ready = sem("mx_ready"), sem("px_ready"), sem("pn_ready")
        sc_ready, mod_ready = sem("sc_ready"), sem("mod_ready")
        ge_ready, ge_exp, me_ready, me_exp = (sem(n) for n in ("ge_ready", "ge_exp", "me_ready", "me_exp"))
        A_ready, cnt_ready, P_ready, win_ready = (sem(n) for n in ("A_ready", "cnt_ready", "P_ready",
                                                                   "win_ready"))
        qs_ready, qd_ready, rope_ready = sem("qs_ready"), sem("qd_ready"), sem("rope_ready")
        conv2_ready = sem("conv2_ready")
        stored = sem("stored")
        XE, GF, UF, TH, AC, AF, AT, YF, YB, TF, YS = range(11)
        fast = [sem(f"fast_{n}") for n in ("window", "gate", "up", "tanh", "act", "act_turned", "actT",
                                           "down", "y", "y_turned", "yT")]
        slow = [sem(f"slow_{n}") for n in ("window", "gate", "up", "tanh", "act", "act_turned", "actT",
                                           "down", "y", "y_turned", "yT")]
        chain_e, chain_s = sem("chain_e"), sem("chain_s")
        s_loaded = sem("s_loaded")

        def v1(a, k=0):
            return vT[:, a + k:a + k + 1]

        def v2(a, k=0):
            return vT[:, NV1 + a + k:NV1 + a + k + 1]

        def full(eng, name):
            eng.wait_ge(psum_full, INDEX[name] + 1)
            return bank[INDEX[name] % 8]

        def emptied(eng, name):
            who, n = drained_by(name)
            eng.wait_ge(a_drained if who == "a" else v_drained, n)

        def weights(eng, name):
            eng.wait_ge(w_loaded[place[name]], landed[name])

        def tiles(a, pat):
            return a.rearrange(pat, p=P)

        vec_loads, r0 = [], 0
        for a in (tiles(t["g_mix"], "o (k p) -> (o k) p"), tiles(t["conv_b"], "o (k p) -> (o k) p"),
                  tiles(t["conv_w"], "a w o (k p) -> (a w o k) p"), tiles(t["g_xattn"], "o (k p) -> (o k) p"),
                  tiles(t["g_mem"], "o (k p) -> (o k) p"), tiles(t["g_moe"], "o (k p) -> (o k) p"),
                  tiles(t["g_final"], "(k p) -> k p"), tiles(t["g_head"], "o (k p) -> (o k) p"),
                  t["b_s"][0]):
            vec_loads.append((raw[r0:r0 + a.shape[0], 0, :], a))
            r0 += a.shape[0]
        assert r0 == NV1
        r0 = 0
        for a in (tiles(t["norm_g_2"], "l (k p) -> (l k) p"), tiles(t["b_mod_2"], "l (k p) -> (l k) p"),
                  tiles(t["c_2"], "o (k p) -> (o k) p"), tiles(t["c_ctx_2"], "(k p) -> k p"),
                  tiles(t["conv_w_2"], "l w (k p) -> (l w k) p"), tiles(t["conv_b_2"], "l (k p) -> (l k) p"),
                  tiles(t["pool_scale_2"], "l (k p) -> (l k) p")):
            vec_loads.append((raw[r0:r0 + a.shape[0], 1, :], a))
            r0 += a.shape[0]
        assert r0 == NV2

        def everywhere(a, shape):
            return a.unsqueeze(0).broadcast_to(shape)

        misc_loads = [(wg[:, :, :], rows(w_in, 2048, 16)), (wr[:, :, 0:NG], rows(t["w_rg"][0], 0, NG)),
                      (wr[:, :, NG:NG + NE], rows(t["w_re"][0], 0, NE)),
                      (gate_b[:, :], everywhere(t["gate_b"][0], [P, 16])),
                      (rb[:, 0:NG], everywhere(t["b_rg"][0], [P, NG])),
                      (rb[:, NG:NG + NE], everywhere(t["b_re"][0], [P, NE])),
                      (lng[:, :], everywhere(t["ln_v_g"][0], [P, DM])),
                      (lnb[:, :], everywhere(t["ln_v_b"][0], [P, DM])),
                      (wsr[:, :, :], t["w_s"][0].rearrange("g t s -> t g s"))]
        for L in range(2):
            for name, a, b in (("q_gain_2", 0, 4), ("k_gain_2", 4, 6)):
                misc_loads += [(gains[:, L, h_, :], everywhere(t[name][L], [P, HD2])) for h_ in range(a, b)]
            for i in range(2):
                for hf_ in range(2):
                    c = slice(64 * hf_, 64 * hf_ + 64)
                    misc_loads.append((pwb[c, L, i, c], t["pool_w_2"][L, 2 * i + hf_]))

        block = ctx.enter_context(nc.Block())

        @block.sync
        def _(sp):
            sp.dma_start(xin, t["x"][0].rearrange("(t p) n -> p t n", p=P)).then_inc(ld_x, 16)
            sent = []

            def load(name, pieces, release):
                n = len(sent)
                if n >= SLOTS:
                    old = sent[n - SLOTS]
                    if old[0][0] in "GUD":
                        sp.wait_ge(fast[{"G": GF, "U": UF, "D": YF}[old[0][0]]], int(old[0][1:]) + 1)
                    else:
                        sp.wait_ge(psum_full, INDEX[old[1]] + 1)
                for c0, src in pieces:
                    k, m = (src.shape[1], src.shape[2]) if len(src.shape) == 3 else (1, src.shape[1])
                    dst = ring[:, place[name], c0:c0 + k * m]
                    if len(src.shape) == 3:
                        dst = dst.rearrange("p (k n) -> p k n", k=k)
                    sp.dma_start(dst, src).then_inc(w_loaded[place[name]], 16)
                sent.append((name, release))

            wsrc = {"G": t["w_gate"][0], "U": t["w_up"][0], "D": t["w_down"][0]}

            def expert(m, e):
                return wsrc[m][bass.ds(e, 1)].rearrange("a (k p) n -> p (a k) n", p=P)

            load(*before[0])
            sp.dma_start(memin, t["mem"][0].rearrange("(t p) n -> p t n", p=P)).then_inc(ld_mem, 16)
            sp.dma_start(ctxin, t["ctx_2"][0].rearrange("(t p) n -> p t n", p=P)).then_inc(ld_ctx, 16)
            for name, pieces, release in before[1:]:
                load(name, pieces, release)
            lead = 11
            for name in experts[:lead]:
                load(name, [(0, expert(name[0], int(name[1:])))], None)
            with sp.Fori(0, (len(experts) - lead - 1) // 6) as i:
                for q, name in enumerate(experts[lead:lead + 6]):
                    m, e = name[0], int(name[1:])
                    sp.wait_ge(fast[{"G": GF, "U": UF, "D": YF}[m]], i * 2 + (e - 2 + 1))
                    k = 4 if m == "D" else 8
                    sp.dma_start(ring[:, place[name], :].rearrange("p (k n) -> p k n", k=k),
                                 expert(m, i * 2 + e)).then_inc(w_loaded[place[name]], 16)
            sent += [(name, None) for name in experts[lead:-1]]
            name = experts[-1]
            load(name, [(0, expert("D", NE - 1))], None)

            sp.wait_ge(win_ready, 2)
            rows_max = sp.value_load(mxc[0:1, 0:1], min_val=0, max_val=S)
            with sp.If(rows_max > C):
                sp.wait_ge(fast[YS], NE)
                with sp.Fori(0, NE) as e:
                    sp.wait_ge(slow[XE], e * 4 + 1)
                    for m, k in (("G", 8), ("U", 8), ("D", 4)):
                        sp.dma_start(ring[:, "GUD".index(m), :].rearrange("p (k n) -> p k n", k=k),
                                     expert(m, e)).then_inc(s_loaded, 16)
                sp.wait_ge(slow[YS], NE * 4)

            for name, pieces, release in after:
                load(name, pieces, release)

            emptied(sp, "fin3")
            sp.dma_start(t["out"][0].rearrange("(t p) n -> p t n", p=P), outb).then_inc(stored, 16)
            sp.wait_ge(stored, 16)

        @block.tensor
        def _(pe):
            at = [0]
            last = [None]

            def group(name):
                n = at[0]
                assert ORDER[n][0] == name, (ORDER[n][0], name)
                if n >= 8 and not LOOP_AT <= n < LOOP_AT + 8:
                    emptied(pe, ORDER[n - 8][0])
                at[0] += 1
                return bank[n % 8]

            def mm(o, lhsT, rhs, start=True, stop=True):
                last[0] = pe.matmul(o, lhsT, rhs, start=start, stop=stop)

            def turn(o, a):
                last[0] = pe.transpose(o, a, ident[0:a.shape[0], 0:a.shape[0]])

            def filled():
                last[0].then_inc(psum_full, 1)

            def turn_tokens(prefix, src):
                for g in range(4):
                    b = group(f"{prefix}{g}")
                    for k in range(2):
                        for tt in range(TT):
                            kk = 2 * g + k
                            turn(b[:, k * S + tt * P:k * S + tt * P + P], src[:, tt, kk * P:kk * P + P])
                    filled()

            def norm_sum(name, sq, n, streams=1):
                pe.wait_ge(sq_ready, n)
                b = group(name)
                for k in range(KT):
                    rhs = sq[:, k] if streams == 1 else sq[:, :, k]
                    o = b[:, 0:S] if streams == 1 else b[:, :].rearrange("p (r s) -> p r s", r=2)
                    mm(o, ones, rhs, k == 0, k == KT - 1)
                filled()

            def to_channels(names, w, h):
                for g, name in enumerate(names):
                    b = group(name)
                    for j in range(2):
                        m = 2 * g + j
                        for k in range(KT):
                            mm(b[:, j * S:j * S + S], w[:, k, m * P:m * P + P], h[:, k], k == 0, k == KT - 1)
                    filled()

            def to_tokens(names, w, h):
                for tt, name in enumerate(names):
                    b = group(name)
                    for k in range(KT):
                        mm(b[:, :], h[:, k, tt * P:tt * P + P], w[:, k], k == 0, k == KT - 1)
                    filled()

            pe.wait_ge(ld_const, 16)
            pe.wait_ge(ld_vec, 16 * len(vec_loads))
            b = group("vec")
            turn(b[:, 0:NV1], raw[0:NV1, 0, :])
            turn(b[:, NV1:NV1 + NV2], raw[0:NV2, 1, :])
            filled()
            pe.wait_ge(ld_x, 16)
            turn_tokens("x", xin)
            norm_sum("ss1", H[:, 0], 1)
            pe.wait_ge(ld_mem, 16)
            turn_tokens("mem", memin)
            pe.wait_ge(ld_misc, 16 * len(misc_loads))
            b = group("ws")
            for g in range(NH):
                turn(b[:, g * P:g * P + P], wsr[:, g, :])
            filled()
            pe.wait_ge(ld_ctx, 16)
            turn_tokens("ctx", ctxin)

            h = H[:, 0]
            pe.wait_ge(h_ready, 1)
            for c in range(2):
                weights(pe, f"in{c}")
                to_channels([f"qk{2 * c}", f"qk{2 * c + 1}"], slot(f"in{c}"), h)
            b = group("gate")
            for tt in range(TT):
                for k in range(KT):
                    mm(b[:, tt * 16:tt * 16 + 16], h[:, k, tt * P:tt * P + P], wg[:, k, :], k == 0, k == KT - 1)
            filled()
            for c, n in ((2, "v"), (3, "o"), (4, "gv"), (5, "gu")):
                weights(pe, f"in{c}")
                to_tokens([f"{n}0", f"{n}1"], slot(f"in{c}"), h)

            norm_sum("ss2", msq, 2)
            pe.wait_ge(h_ready, 2)
            for c in range(2):
                weights(pe, f"kv{c}")
                to_channels([f"km{2 * c}", f"km{2 * c + 1}"], slot(f"kv{c}"), H[:, 1])
            pe.wait_ge(lf_ready, 1)
            b = group("bcum")
            lf = sm[:, 64:80]
            mm(b[:, 0:8], trf, lf[:, 0:8])
            mm(b[:, 8:16], trb, lf[:, 8:16])
            mm(b[:, 16:32], ones, lf)
            filled()
            pe.wait_ge(ap_ready, 1)
            b = group("apT")
            turn(b[0:16, 0:P], sm[:, 112:128])
            filled()
            for c in range(2):
                weights(pe, f"kv{c + 2}")
                to_tokens([f"vm{2 * c}", f"vm{2 * c + 1}"], slot(f"kv{c + 2}"), H[:, 1])
            pe.wait_ge(dmx_ready, 1)
            b = group("mxb")
            mm(b[:, 0:16], ones[0:16, :], sm[0:16, 129:145])
            filled()
            for j in range(4):
                b = group(f"A{j}")
                mm(b[:, :], ones[0:16, :], bd[:, 4 * j:4 * j + 4, :])
                filled()

            def modulation(L):
                pe.wait_ge(sc_ready, 1)
                b = group(f"mod{L}")
                for c in range(6):
                    weights(pe, f"mod{L}{c}")
                    w = slot(f"mod{L}{c}")
                    for m in range(4):
                        o = b[:, (4 * c + m) * 2:(4 * c + m) * 2 + 2]
                        for k in range(KT):
                            mm(o, w[:, k, m * P:m * P + P], sc[:, :, k], k == 0, k == KT - 1)
                filled()

            modulation(0)

            pe.wait_ge(qk_ready, 1)
            for d in range(2):
                b = group(f"KT{d}")
                for hh in range(NH):
                    turn(b[:, hh * P:hh * P + P], qkT[:, 4 + hh, d * P:d * P + P])
                filled()
            for tt in range(TT):
                b = group(f"QK{tt}")
                for hh in range(NH):
                    mm(b[:, hh * P:hh * P + P], qkT[:, hh, tt * P:tt * P + P],
                       qkT[:, 4 + hh, tt * P:tt * P + P])
                filled()
            emptied(pe, "KT1")
            emptied(pe, "v1")
            for d in range(2):
                b = group(f"C{d}")
                for hh in range(NH):
                    mm(b[:, hh * P:hh * P + P], kw[:, d, hh, :], vs[:, d, hh * P:hh * P + P])
                filled()
            b = group("nn")
            for d in range(2):
                for hh in range(NH):
                    mm(b[:, d * 4 + hh:d * 4 + hh + 1], kw[:, d, hh, :], ones[:, 0:1])
            filled()
            pe.wait_ge(gvn_ready, 1)
            emptied(pe, "ws")
            for tt in range(TT):
                b = group(f"SP{tt}")
                for g in range(NH):
                    mm(b[:, g * P:g * P + P], wsT[:, g, :], gv[:, tt, g * P:g * P + P])
                filled()
            pe.wait_ge(w_ready, 1)
            for j in range(4):
                b = group(f"WT{j}")
                for hh in range(NH):
                    turn(b[:, hh * P:hh * P + P], W[:, 4 * j + hh, :])
                filled()
            emptied(pe, "nn")
            b = group("dI")
            for d in range(2):
                for hh in range(NH):
                    mm(b[:, d * 4 + hh:d * 4 + hh + 1], qkT[:, hh, (1 - d) * P:(2 - d) * P],
                       sm[:, 240 + d * 4 + hh:241 + d * 4 + hh])
            filled()
            for j in range(4):
                emptied(pe, f"WT{j}")
                b = group(f"NI{j}")
                for hh in range(NH):
                    mm(b[:, hh * P:hh * P + P], WT[:, 4 * j + hh, :], vs[:, j % 2, hh * P:hh * P + P])
                filled()
            emptied(pe, "C1")
            for d in range(2):
                b = group(f"CI{d}")
                for hh in range(NH):
                    mm(b[:, hh * P:hh * P + P], qkT[:, hh, (1 - d) * P:(2 - d) * P], Cs[:, d, hh, :])
                filled()
            pe.wait_ge(y_ready, 1)
            emptied(pe, "SP1")
            for g in range(4):
                b = group(f"yT{g}")
                for j in range(2):
                    for tt in range(TT):
                        src = (tho if g < 2 else gu)[:, tt, ((2 * g + j) % 4) * P:((2 * g + j) % 4) * P + P]
                        turn(b[:, j * S + tt * P:j * S + tt * P + P], src)
                filled()
            emptied(pe, "yT3")
            for c in range(2):
                weights(pe, f"wout{c}")
                to_channels([f"wo{2 * c}", f"wo{2 * c + 1}"], slot(f"wout{c}"), yT)

            norm_sum("ss3", H[:, 0], 3)
            pe.wait_ge(h_ready, 3)
            for c in range(2):
                weights(pe, f"wq{c}")
                to_channels([f"xq{2 * c}", f"xq{2 * c + 1}"], slot(f"wq{c}"), H[:, 0])
            emptied(pe, "xq3")
            emptied(pe, "vm3")
            for g in range(4):
                tt, hp = divmod(g, 2)
                b = group(f"S{g}")
                for j in range(2):
                    for k in range(2):
                        kk = 2 * (2 * hp + j) + k
                        mm(b[:, j * S:j * S + S], xqT[:, kk, tt * P:tt * P + P], kmT[:, kk, :], k == 0, k == 1)
                filled()
            pe.wait_ge(pn_ready, 1)
            for hh in range(NH):
                b = group(f"pT{hh}")
                for m in range(2):
                    for tt in range(TT):
                        turn(b[:, m * S + tt * P:m * S + tt * P + P], px[:, tt, hh, m * P:m * P + P])
                filled()
            for hh in range(NH):
                emptied(pe, f"pT{hh}")
                b = group(f"xo{hh}")
                for j in range(2):
                    for m in range(2):
                        c0 = hh * 256 + j * P
                        mm(b[:, j * S:j * S + S], vm[:, m, c0:c0 + P], pTx[:, hh, m, :], m == 0, m == 1)
                filled()
            emptied(pe, "xo3")
            for c in range(2):
                weights(pe, f"wox{c}")
                to_channels([f"xw{2 * c}", f"xw{2 * c + 1}"], slot(f"wox{c}"), oTx)

            norm_sum("ss4", H[:, 0], 4)
            pe.wait_ge(h_ready, 4)
            b = group("lg")
            for tt in range(TT):
                for k in range(KT):
                    mm(b[:, tt * 36:tt * 36 + 36], H[:, 0, k, tt * P:tt * P + P], wr[:, k, :],
                       k == 0, k == KT - 1)
            filled()
            for g in range(4):
                tt, half = divmod(g, 2)
                b = group(f"hk{g}")
                for j in range(4):
                    turn(b[:, j * P:j * P + P], H[:, 0, 4 * half + j, tt * P:tt * P + P])
                filled()
            modulation(1)
            pe.wait_ge(A_ready, 1)
            b = group("pos")
            As = sm[:, 320:384].rearrange("p (t e) -> p t e", t=2)
            mm(b[:, 0:32], trs, As[:, 0, :])
            mm(b[:, 32:64], ones, As[:, 0, :], True, False)
            mm(b[:, 32:64], trs, As[:, 1, :], False, True)
            mm(b[:, 64:96], ones, As[:, 0, :], True, False)
            mm(b[:, 64:96], ones, As[:, 1, :], False, True)
            mm(b[0:32, 96:97], As[:, 0, :], ones[:, 0:1], True, False)
            mm(b[0:32, 96:97], As[:, 1, :], ones[:, 0:1], False, True)
            filled()
            pe.wait_ge(cnt_ready, 1)
            b = group("start")
            mm(b[:, 0:32], sm[0:32, 1000:1128], trs[0:32, 0:32])
            filled()
            pe.wait_ge(P_ready, 1)
            emptied(pe, "hk3")
            for k in range(KT):
                b = group(f"xs{k}")
                for tt in range(TT):
                    mm(b[:, :], hk[:, tt, k * P:k * P + P], Pm[:, tt, :], tt == 0, tt == 1)
                filled()
            emptied(pe, "xs7")
            emptied(pe, "start")

            def project(bk, w, x, done, before_last=None):
                for k in range(KT):
                    if before_last and k == KT - 1:
                        before_last()
                    m = pe.matmul(bk[0:C, :], x[:, k, :], w[:, k], start=(k == 0), stop=(k == KT - 1))
                m.then_inc(done, 1)

            def hold():
                pe.matmul(bank[4][:, 0:1], ident, ones[:, 0:1], start=True, stop=True)

            def turn_act(s, j):
                for k in range(4):
                    m = pe.transpose(bank[4][:, k * C:k * C + C], ac[:, j, k * P:k * P + P], ident[0:C, 0:C])
                m.then_inc(s[AF], 1)

            def down(s, w, j):
                for half in range(2):
                    for k in range(4):
                        m = pe.matmul(bank[5 + half][0:C, :], acT[:, j, k, :], w[:, k, half * 512:half * 512 + 512],
                                      start=(k == 0), stop=(k == 3))
                m.then_inc(s[YF], 1)

            def turn_down(s, j):
                for k in range(KT):
                    m = pe.transpose(bank[7][:, k * C:k * C + C], yb[:, j, k * P:k * P + P], ident[0:C, 0:C])
                m.then_inc(s[TF], 1)

            def expert_step(e, parity, gname, uname, dname, more, has):
                gate, act1, out2, up, down1 = has

                def turns_ready():
                    if down1:
                        pe.wait_ge(fast[AC], e)
                        if act1 == "wait":
                            pe.wait_ge(fast[AT], e - 1)
                    if out2:
                        pe.wait_ge(fast[YB], e - 1)
                        if out2 == "wait":
                            pe.wait_ge(fast[YS], e - 2)

                if gate:
                    pe.wait_ge(fast[XE], e + 1)
                    if act1 == "wait":
                        pe.wait_ge(fast[AC], e - 1)
                    pe.wait_ge(w_loaded[place[gname]], landed[gname] + more)
                    project(bank[parity], slot(gname), xe[:, parity], fast[GF], turns_ready)
                else:
                    turns_ready()
                if down1:
                    turn_act(fast, 1 - parity)
                if out2:
                    turn_down(fast, parity)
                if up:
                    pe.wait_ge(w_loaded[place[uname]], landed[uname] + more)
                    project(bank[2 + parity], slot(uname), xe[:, parity], fast[UF])
                if down1:
                    pe.wait_ge(fast[AT], e)
                    if act1 == "wait":
                        pe.wait_ge(fast[YB], e - 1)
                    pe.wait_ge(w_loaded[place[dname]], landed[dname] + more)
                    down(fast, slot(dname, 4, 1024), 1 - parity)

            expert_step(0, 0, "G0", "U0", None, 0, (True, "none", False, True, False))
            expert_step(1, 1, "G1", "U1", "D0", 0, (True, "none", False, True, True))
            expert_step(2, 0, "G2", "U2", "D1", 0, (True, "wait", True, True, True))
            expert_step(3, 1, "G3", "U3", "D2", 0, (True, "wait", "wait", True, True))
            with pe.Fori(0, (NE - 4) // 2) as i:
                for j in range(2):
                    expert_step(i * 2 + (4 + j), j, f"G{4 + j}", f"U{4 + j}", f"D{3 + j}", i * 16,
                                (True, "wait", "wait", True, True))
            expert_step(NE, 0, None, None, f"D{NE - 1}", 0, (False, "wait", "wait", False, True))
            expert_step(NE + 1, 1, None, None, None, 0, (False, "wait", "wait", False, False))

            pe.wait_ge(win_ready, 2)
            rows_max = pe.value_load(mxc[0:1, 0:1], min_val=0, max_val=S)
            with pe.If(rows_max > C):
                with pe.Fori(0, NE) as e:
                    for q in range(4):
                        pe.wait_ge(slow[XE], e * 4 + (q + 1))
                        if q == 0:
                            pe.wait_ge(s_loaded, e * 48 + 48)
                        project(bank[0], ring[:, 0, :].rearrange("p (k n) -> p k n", k=8), xe[:, 0], slow[GF])
                        project(bank[2], ring[:, 1, :].rearrange("p (k n) -> p k n", k=8), xe[:, 0], slow[UF])
                        pe.wait_ge(slow[AC], e * 4 + (q + 1))
                        hold()
                        turn_act(slow, 0)
                        pe.wait_ge(slow[AT], e * 4 + (q + 1))
                        down(slow, ring[:, 2, :].rearrange("p (k n) -> p k n", k=4), 0)
                        pe.wait_ge(slow[YB], e * 4 + (q + 1))
                        hold()
                        turn_down(slow, 0)
                pe.wait_ge(slow[YS], NE * 4)

            pe.wait_ge(fast[YS], NE)
            for g in range(2):
                b = group(f"pw{g}")
                for j in range(2):
                    for tt in range(TT):
                        turn(b[:, j * S + tt * P:j * S + tt * P + P], Pw[:, tt, (2 * g + j) * P:(2 * g + j) * P + P])
                filled()
            for g in range(8):
                st, half = divmod(g, 2)
                b = group(f"yt{g}")
                for j in range(4):
                    turn(b[:, j * P:j * P + P], ys[:, 4 * half + j, st * P:st * P + P])
                filled()
            emptied(pe, "pw1")
            emptied(pe, "yt6")
            emptied(pe, "yt7")
            for g in range(4):
                b = group(f"co{g}")
                for j in range(2):
                    for a in range(4):
                        kk = 2 * g + j
                        mm(b[:, j * S:j * S + S], yk[:, a, kk * P:kk * P + P], PwT[:, a, :], a == 0, a == 3)
                filled()
            norm_sum("ss5", H[:, 0], 5)

            for L in range(2):
                R = 2 - L
                norm_sum(f"{L}ss", H, 6 + L, 2)
                pe.wait_ge(h_ready, 6 + L)

                def wide(name, w, m):
                    b = group(f"{L}{name}")
                    for k in range(KT):
                        if R == 2:
                            mm(b[:, :].rearrange("p (r s) -> p r s", r=2), w[:, k, m * P:m * P + P],
                               H[:, :, k], k == 0, k == KT - 1)
                        else:
                            mm(b[:, 0:S], w[:, k, m * P:m * P + P], H[:, 0, k], k == 0, k == KT - 1)
                    filled()

                def tokens2(name, w):
                    for r in range(R):
                        b = group(f"{L}{name}{r}")
                        for tt in range(TT):
                            for k in range(KT):
                                mm(b[:, tt * W2:tt * W2 + W2], H[:, r, k, tt * P:tt * P + P], w[:, k, :],
                                   k == 0, k == KT - 1)
                        filled()

                weights(pe, f"{L}in0")
                w = slot(f"{L}in0")
                for r in range(2):
                    c0 = 256 if L == 1 and r == 1 else 0
                    for tt in range(TT):
                        b = group(f"{L}qkv{2 * r + tt}")
                        for k in range(KT):
                            mm(b[:, c0:512], H[:, r, k, tt * P:tt * P + P], w[:, k, c0:512], k == 0, k == KT - 1)
                        filled()
                weights(pe, f"{L}in1")
                w = slot(f"{L}in1")
                wide("za0", w, 0)
                wide("za1", w, 1)
                tokens2("uf", w[:, :, 256:512])
                weights(pe, f"{L}in2")
                w = slot(f"{L}in2")
                for i, n in enumerate(("zf0", "zf1", "b0", "b1")):
                    wide(n, w, i)
                weights(pe, f"{L}in3")
                w = slot(f"{L}in3")
                for i, n in enumerate(("c0", "c1", "h0", "h1")):
                    wide(n, w, i)
                weights(pe, f"{L}in4")
                w = slot(f"{L}in4")
                wide("zc0", w, 0)
                wide("zc1", w, 1)
                tokens2("up", w[:, :, 256:512])
                weights(pe, f"{L}in5")
                w = slot(f"{L}in5", KT, 256)
                wide("zp0", w, 0)
                wide("zp1", w, 1)

                weights(pe, f"{L}const")
                cc = ring[:, place[f"{L}const"], :]
                dft = cc[:, DFT0:DFT0 + 1024].rearrange("p (t n) -> p t n", t=2)
                pool = cc[:, POOL0:POOL0 + 2048].rearrange("p (t i s) -> p t i s", t=2, i=4)
                wf = cc[:, WF0:WF0 + 512].rearrange("p (k n) -> p k n", k=2)
                for r in range(R):
                    emptied(pe, f"{L}uf{r}")
                    for i in range(2):
                        b = group(f"{L}B{r}{i}")
                        for tt in range(TT):
                            mm(b[:, :], uf[:, 2 * r + tt, i * P:i * P + P], dft[:, tt, :], tt == 0, tt == 1)
                        filled()
                emptied(pe, f"{L}up{R - 1}")
                for i in range(2):
                    b = group(f"{L}dT{i}")
                    for half in range(2):
                        g = 2 * i + half
                        for r in range(R):
                            for tt in range(TT):
                                mm(b[half * 64:half * 64 + 64, r * S:r * S + S],
                                   up[:, 2 * r + tt, g * 64:g * 64 + 64], pool[:, tt, g, :], tt == 0, tt == 1)
                    filled()
                emptied(pe, f"{L}B{R - 1}1")
                for i in range(2):
                    b = group(f"{L}yf{i}")
                    for r in range(R):
                        mm(b[:, r * S:r * S + S], cc[:, CD0:CD0 + P], B2[:, r, i, 0:S], True, False)
                        mm(b[:, r * S:r * S + S], cc[:, CD0 + P:CD0 + 2 * P], B2[:, r, i, S:2 * S], False, True)
                    filled()

                def both(b):
                    return b[:, 0:R * S]

                for i in range(2):
                    emptied(pe, f"{L}dT{i}")
                    b = group(f"{L}pl{i}")
                    mm(both(b), pwb[:, L, i, :], dT2[:, i, 0:R].rearrange("p r s -> p (r s)"))
                    filled()
                emptied(pe, f"{L}yf1")
                for i in range(2):
                    b = group(f"{L}wf{i}")
                    for k in range(2):
                        mm(both(b), wf[:, k, i * P:i * P + P], yf2[:, k, 0:R].rearrange("p r s -> p (r s)"),
                           k == 0, k == 1)
                    filled()
                pe.wait_ge(rope_ready, L + 1)
                for hh in range(6):
                    b = group(f"{L}hT{hh}")
                    for tt in range(4):
                        if hh < 4 and tt >= 2 * R:
                            continue
                        turn(b[0:HD2, tt * P:tt * P + P], qkv[:, tt, hh * HD2:hh * HD2 + HD2])
                    filled()
                emptied(pe, f"{L}hT5")
                if L == 0:
                    for g in range(4):
                        tt, hp = divmod(g, 2)
                        b = group(f"{L}cS{g}")
                        for j in range(2):
                            mm(b[:, j * S:j * S + S], q2T[:, 2 * hp + j, S + tt * P:S + tt * P + P],
                               q2T[:, 4 + hp, S:2 * S])
                        filled()
                    pe.wait_ge(pn_ready, 2)
                    for hh in range(NH):
                        b = group(f"{L}cP{hh}")
                        for m in range(2):
                            for tt in range(TT):
                                turn(b[:, m * S + tt * P:m * S + tt * P + P], pc2[:, tt, hh, m * P:m * P + P])
                        filled()
                    emptied(pe, f"{L}cP3")
                    for i in range(2):
                        b = group(f"{L}co{i}")
                        for j in range(2):
                            for m in range(2):
                                mm(b[j * 64:j * 64 + 64, 0:S], qkv[:, 2 + m, 384 + i * 64:384 + i * 64 + 64],
                                   pcT2[:, 2 * i + j, m, :], m == 0, m == 1)
                        filled()
                for g in range(8):
                    tt, hh = divmod(g, 4)
                    b = group(f"{L}xS{g}")
                    mm(b[:, :], q2T[:, hh, tt * P:tt * P + P], q2T[:, 4 + hh // 2, :])
                    filled()
                pe.wait_ge(pn_ready, 3 + L)
                for g in range(8):
                    hh, mp = divmod(g, 2)
                    b = group(f"{L}xP{g}")
                    for m in range(2):
                        for tt in range(TT):
                            mk = 2 * mp + m
                            turn(b[:, m * S + tt * P:m * S + tt * P + P], px2[:, tt, hh, mk * P:mk * P + P])
                    filled()
                emptied(pe, f"{L}xP7")
                for i in range(2):
                    b = group(f"{L}xo{i}")
                    for j in range(2):
                        for m in range(4):
                            mm(b[j * 64:j * 64 + 64, 0:S], qkv[:, m, 384 + i * 64:384 + i * 64 + 64],
                               pT2[:, 2 * i + j, m, :], m == 0, m == 3)
                    filled()
                pe.wait_ge(conv2_ready, L + 1)
                emptied(pe, f"{L}xo1")
                for c in range(2):
                    weights(pe, f"{L}wout{c}")
                    w = slot(f"{L}wout{c}")
                    for m in range(4):
                        b = group(f"{L}out{4 * c + m}")
                        for k in range(KT):
                            mm(both(b), w[:, k, m * P:m * P + P], oT[:, k, 0:R].rearrange("p r s -> p (r s)"),
                               k == 0, k == KT - 1)
                        filled()
            emptied(pe, "1out7")
            for g in range(4):
                tt, half = divmod(g, 2)
                b = group(f"fin{g}")
                for j in range(4):
                    turn(b[:, j * P:j * P + P], X[:, 0, 4 * half + j, tt * P:tt * P + P])
                filled()
            assert at[0] == len(ORDER)

        @block.scalar
        def _(act):
            n = [0]

            def link(ins):
                n[0] += 1
                ins.then_inc(a_chain, 1)
                act.wait_ge(a_chain, n[0])

            for dst, src in vec_loads:
                act.dma_start(dst, src).then_inc(ld_vec, 16)
            act.dma_start(c1[:, :], t["const1"]).then_inc(ld_const, 16)
            act.wait_ge(v_chain, 6)
            for dst, src in misc_loads:
                act.dma_start(dst, src).then_inc(ld_misc, 16)

            def take(name, dst, src=None, func=ACT.Copy, **kw):
                b = full(act, name)
                src = b[:, :] if src is None else src(b)
                act.activation(dst, src, func, **kw).then_inc(a_drained, 1)

            def flat(v):
                return v.rearrange("p a b -> p (a b)")

            def root(k, name, n=S):
                if k > 1:
                    act.wait_ge(h_ready, k - 1)
                take(name, flat(sd)[:, 0:n], lambda b: b[:, 0:n], ACT.Sqrt, scale=1.0 / D, bias=eps[:, 0:1])

            eps, eps_ln = sm[:, 1190:1191], sm[:, 1191:1192]
            for g in range(4):
                take(f"x{g}", flat(X[:, 0, 2 * g:2 * g + 2]))
            root(1, "ss1")
            for g in range(4):
                take(f"mem{g}", flat(H[:, 1, 2 * g:2 * g + 2]))
            take("ws", flat(wsT))
            for g in range(4):
                take(f"ctx{g}", flat(X[:, 1, 2 * g:2 * g + 2]))
            emptied(act, "vec")
            act.activation(flat(sc), vT[:, NV1 + V_C:NV1 + V_C + 16], ACT.Silu).then_inc(sc_ready, 1)
            for g in range(4):
                take(f"qk{g}", qkp[:, 2 * g:2 * g + 2, 2:2 + S],
                     lambda b: b[:, :].rearrange("p (k s) -> p k s", k=2))
            for tt in range(TT):
                take(f"v{tt}", vs[:, tt, :])
            for tt in range(TT):
                take(f"o{tt}", tho[:, tt, :], None, ACT.Tanh, scale=0.5)
            for tt in range(TT):
                take(f"gv{tt}", gv[:, tt, :], None, ACT.Gelu_apprx_tanh)
            for tt in range(TT):
                take(f"gu{tt}", gu[:, tt, :], None, ACT.Gelu_apprx_tanh)
            root(2, "ss2")
            act.wait_ge(nf_ready, 1)
            link(act.activation(sm[:, 80:96], sm[:, 32:48], ACT.Exp, scale=-1.0))
            act.activation(sm[:, 96:112], sm[:, 80:96], ACT.Ln, bias=1.0).then_inc(lse_ready, 1)
            act.wait_ge(gvc_ready, 1)
            for tt in range(TT):
                ins = act.activation(Ej[:, tt], gv[:, tt, :], ACT.Square, accum_out=sm[:, 264 + tt:265 + tt])
            ins.then_inc(gvs_ready, 1)
            act.wait_ge(gvs_ready, 1)
            act.activation(sm[:, 266:268], sm[:, 264:266], ACT.Sqrt, scale=1.0 / DM, bias=eps_ln)\
                .then_inc(gvs_ready, 1)
            for g in range(4):
                take(f"km{g}", flat(kmT[:, 2 * g:2 * g + 2]))
            for g in range(4):
                c, tt = divmod(g, 2)
                take(f"vm{g}", vm[:, tt, c * 512:c * 512 + 512])
            act.wait_ge(conv_ready, 40)
            act.activation(qkT[:, :, :], qkT[:, :, :], ACT.Silu).then_inc(qk_ready, 1)
            act.wait_ge(ei_ready, 1)
            act.activation(sm[:, 184:224], sm[:, 144:184], ACT.Exp).then_inc(ee_ready, 1)
            act.wait_ge(em_ready, 1)
            act.activation(E[:, :, :], E[:, :, :], ACT.Exp).then_inc(e_ready, 1)
            for d in range(2):
                take(f"C{d}", Cs[:, d].rearrange("p h s -> p (h s)"))
            for j in range(4):
                take(f"WT{j}", flat(WT[:, 4 * j:4 * j + 4, :]))
            act.wait_ge(hss_ready, 1)
            act.activation(sm[:, 280:288], sm[:, 272:280], ACT.Sqrt, scale=1.0 / 128, bias=eps)\
                .then_inc(hsd_ready, 1)
            root(3, "ss3")
            for g in range(4):
                take(f"xq{g}", flat(xqT[:, 2 * g:2 * g + 2]))

            def softmax_exp(names, heads, p, width, base, col):
                for g, name in enumerate(names):
                    b = full(act, name)
                    act.wait_ge(mx_ready, base + g + 1)
                    for j in range(heads):
                        tt, hh = divmod(heads * g + j, NH)
                        ins = act.activation(p[:, tt, hh, :], b[:, j * width:j * width + width], ACT.Exp,
                                             scale=col[2], bias=sm[:, col[0] + 4 * tt + hh:col[0] + 4 * tt + hh + 1],
                                             accum_out=sm[:, col[1] + 4 * tt + hh:col[1] + 4 * tt + hh + 1])
                        if j == heads - 1:
                            ins.then_inc(a_drained, 1)

            softmax_exp([f"S{g}" for g in range(4)], 2, px, 256, 0, (288, 296, X_SCALE))
            for hh in range(NH):
                take(f"pT{hh}", pTx[:, hh].rearrange("p m s -> p (m s)"))
            for hh in range(NH):
                take(f"xo{hh}", flat(oTx[:, 2 * hh:2 * hh + 2]))
            root(4, "ss4")
            for g in range(4):
                tt, half = divmod(g, 2)
                take(f"hk{g}", hk[:, tt, half * 512:half * 512 + 512])
            act.wait_ge(ge_ready, 1)
            act.activation(sm[:, 472:480], sm[:, 464:472], ACT.Exp).then_inc(ge_exp, 1)
            act.wait_ge(me_ready, 1)
            act.activation(sm[:, 484:486], sm[:, 482:484], ACT.Exp).then_inc(me_exp, 1)
            take("mod1", sm[:, 1130:1178], lambda b: b[:, 0:48])
            for k in range(KT):
                take(f"xs{k}", xs[:, k, 0:A])

            def window(s, x, w0, done):
                act.activation(x, xs[:, :, bass.ds(w0, C)], ACT.Copy).then_inc(s[XE], 1)

            act.wait_ge(win_ready, 2)

            def starts_at(e, q):
                return act.value_load(win[0:1, bass.ds(e + q * NE, 1)], min_val=0, max_val=A)

            def scalar_step(e, parity, has):
                rows1, gate, act1, out2 = has
                if rows1:
                    w0 = starts_at(e + 1, 0)
                    if rows1 == "wait":
                        act.wait_ge(fast[UF], e)
                    window(fast, xe[:, 1 - parity], w0, None)
                if gate:
                    act.wait_ge(fast[GF], e + 1)
                    if gate == "wait":
                        act.wait_ge(fast[AC], e - 1)
                    act.activation(th[:, parity], bank[parity][0:C, :], ACT.Tanh, scale=0.5).then_inc(fast[TH], 1)
                if act1:
                    act.wait_ge(fast[AF], e)
                    if act1 == "wait":
                        act.wait_ge(fast[YF], e - 2)
                    act.activation(acT[:, 1 - parity].rearrange("p k c -> p (k c)"), bank[4][:, 0:4 * C],
                                   ACT.Copy).then_inc(fast[AT], 1)
                if out2:
                    w0 = starts_at(e - 2, 0)
                    act.wait_ge(fast[TF], e - 1)
                    if out2 == "wait":
                        act.wait_ge(fast[YS], e - 2)
                    act.activation(ys[:, :, bass.ds(w0, C)], bank[7][:, :].rearrange("p (k c) -> p k c", k=KT),
                                   ACT.Copy).then_inc(fast[YS], 1)

            w0 = starts_at(0, 0)
            for k in range(KT):
                if k == KT - 1:
                    emptied(act, "xs7")
            window(fast, xe[:, 0], w0, None)
            scalar_step(0, 0, (True, True, False, False))
            scalar_step(1, 1, ("wait", True, True, False))
            scalar_step(2, 0, ("wait", "wait", True, True))
            scalar_step(3, 1, ("wait", "wait", "wait", "wait"))
            with act.Fori(0, (NE - 4) // 2 - 1) as i:
                for j in range(2):
                    scalar_step(i * 2 + (4 + j), j, ("wait", "wait", "wait", "wait"))
            scalar_step(NE - 2, 0, ("wait", "wait", "wait", "wait"))
            scalar_step(NE - 1, 1, (False, "wait", "wait", "wait"))
            scalar_step(NE, 0, (False, False, "wait", "wait"))
            scalar_step(NE + 1, 1, (False, False, False, "wait"))

            rows_max = act.value_load(mxc[0:1, 0:1], min_val=0, max_val=S)
            with act.If(rows_max > C):
                act.wait_ge(fast[YS], NE)
                with act.Fori(0, NE) as e:
                    for q in range(4):
                        w0 = starts_at(e, q)
                        window(slow, xe[:, 0], w0, None)
                        act.wait_ge(slow[GF], e * 4 + (q + 1))
                        act.activation(th[:, 0], bank[0][0:C, :], ACT.Tanh, scale=0.5).then_inc(slow[TH], 1)
                        act.wait_ge(slow[AF], e * 4 + (q + 1))
                        act.activation(acT[:, 0].rearrange("p k c -> p (k c)"), bank[4][:, 0:4 * C],
                                       ACT.Copy).then_inc(slow[AT], 1)
                        act.wait_ge(slow[TF], e * 4 + (q + 1))
                        act.activation(ys[:, :, bass.ds(w0, C)], bank[7][:, :].rearrange("p (k c) -> p k c", k=KT),
                                       ACT.Copy).then_inc(slow[YS], 1)
                        act.wait_ge(slow[YS], e * 4 + (q + 1))

            for g in range(2):
                take(f"pw{g}", flat(PwT[:, 2 * g:2 * g + 2]))
            for g in range(1, 8, 2):
                st, half = divmod(g, 2)
                if g == 1:
                    act.wait_ge(fast[YS], NE)
                take(f"yt{g}", yk[:, st, half * 512:half * 512 + 512])
            root(5, "ss5")

            for L in range(2):
                R = 2 - L

                def half(b):
                    return b[:, 0:R * S]

                def two(v):
                    return v.rearrange("p r s -> p (r s)")

                root(6 + L, f"{L}ss", 2 * S)
                for tt in range(4):
                    c0 = 256 if L == 1 and tt >= 2 else 0
                    take(f"{L}qkv{tt}", qkv[:, tt, c0:512], lambda b: b[:, c0:512])
                for i in range(2):
                    take(f"{L}za{i}", two(oT[:, 2 + i, 0:R]), half, ACT.Silu)
                for r in range(R):
                    take(f"{L}uf{r}", flat(uf[:, 2 * r:2 * r + 2]))
                for i in range(2):
                    take(f"{L}zf{i}", two(oT[:, i, 0:R]), half, ACT.Silu)
                for n_, dst in (("b", bs2), ("c", cs2)):
                    for i in range(2):
                        take(f"{L}{n_}{i}", two(dst[:, i, 0:R]), half)
                for i in range(2):
                    take(f"{L}zc{i}", two(oT[:, 4 + i, 0:R]), half, ACT.Silu)
                for r in range(R):
                    take(f"{L}up{r}", flat(up[:, 2 * r:2 * r + 2]))
                for i in range(2):
                    take(f"{L}zp{i}", two(oT[:, 6 + i, 0:R]), half, ACT.Silu)
                act.wait_ge(qs_ready, L + 1)
                act.activation(sm[:, 624:648], sm[:, 600:624], ACT.Sqrt, scale=1.0 / HD2, bias=eps)\
                    .then_inc(qd_ready, 1)
                for r in range(R):
                    for i in range(2):
                        take(f"{L}B{r}{i}", B2[:, r, i, :])
                for i in range(2):
                    take(f"{L}dT{i}", two(dT2[:, i, 0:R]), half)
                for i in range(2):
                    take(f"{L}yf{i}", two(yf2[:, i, 0:R]), half)
                for hh in range(6):
                    n_ = R * S if hh < 4 else 2 * S
                    take(f"{L}hT{hh}", q2T[:, hh, 0:n_], lambda b: b[0:HD2, 0:n_])
                if L == 0:
                    softmax_exp([f"0cS{g}" for g in range(4)], 2, pc2, 256, 4, (680, 688, A_SCALE))
                    for hh in range(NH):
                        take(f"0cP{hh}", pcT2[:, hh].rearrange("p m s -> p (m s)"))
                softmax_exp([f"{L}xS{g}" for g in range(8)], 1, px2, 512, 8 + 8 * L, (700, 708, A_SCALE))
                for g in range(8):
                    hh, mp = divmod(g, 2)
                    take(f"{L}xP{g}", pT2[:, hh, 2 * mp:2 * mp + 2].rearrange("p m s -> p (m s)"))
            for g in range(4):
                tt, half_ = divmod(g, 2)
                take(f"fin{g}", outb[:, tt, half_ * 512:half_ * 512 + 512])

        @block.vector
        def _(dve):
            n = [0]

            def link(ins):
                n[0] += 1
                ins.then_inc(v_chain, 1)
                dve.wait_ge(v_chain, n[0])

            def tail(ins, s):
                tails[id(s)] = tails.get(id(s), 0) + 1
                ins.then_inc(s, 1)
                dve.wait_ge(s, tails[id(s)])

            tails = {}

            def taken(ins):
                taken_n[0] += 1
                ins.then_inc(v_drained, 1)
                dve.wait_ge(v_drained, taken_n[0])

            taken_n = [0]

            def over(v, shape, axis):
                return v.unsqueeze(axis).broadcast_to(shape)

            def tt_(o, a, b, op):
                return dve.tensor_tensor(o, a, b, op)

            def ts_(o, a, s1, s2=None, op0=ALU.mult, op1=None):
                if s2 is None:
                    return dve.tensor_scalar(o, a, s1, None, op0)
                return dve.tensor_scalar(o, a, s1, s2, op0, op1)

            def stt(o, a, s, b, op0, op1):
                return dve.scalar_tensor_tensor(out=o, in0=a, scalar=s, in1=b, op0=op0, op1=op1)

            link(dve.memset(pwb[:, :, :, :], 0.0))
            link(dve.memset(sm[:, :], 0.0))
            link(dve.memset(sm[:, 1190:1191], RMS_EPS))
            link(dve.memset(sm[:, 1191:1192], LN_EPS))
            link(dve.memset(qkp[:, :, 0:2], 0.0))
            link(dve.memset(qkp[:, :, 2 + S:4 + S], 0.0))
            b = full(dve, "vec")
            taken(dve.tensor_copy(vT[:, :], b[:, 0:NV1 + NV2]))

            def squares(src, dst, last):
                ins = tt_(dst, src, src, ALU.mult)
                tail(ins, sq_ready) if last else link(ins)

            def inverse_root(name, n=S):
                emptied(dve, name)
                link(dve.reciprocal(rs[:, :, :].rearrange("p r s -> p (r s)")[:, 0:n],
                                    sd[:, :, :].rearrange("p r s -> p (r s)")[:, 0:n]))

            def norm(name, src, dst, gain):
                inverse_root(name)
                for k in range(KT):
                    ins = stt(dst[:, k], src[:, k], gain(k), rs[:, 0, :], ALU.mult, ALU.mult)
                tail(ins, h_ready)

            def modulation(src, L):
                o = V_BMOD + NV1 + 24 * L
                ins = tt_(mod[:, L], src.rearrange("p (m r) -> p m r", r=2), over(vT[:, o:o + 24], [P, 24, 2], 2),
                          ALU.add)
                taken(ins) if L == 0 else link(ins)
                o = V_NG + NV1 + 8 * L
                link(stt(gsc[:, L], mod[:, L, 8:16], 1.0, over(vT[:, o:o + 8], [P, 8, 2], 2), ALU.add, ALU.mult))

            emptied(dve, "x3")
            squares(X[:, 0], H[:, 0], True)
            norm("ss1", X[:, 0], H[:, 0], lambda k: v1(V_GMIX, k))
            emptied(dve, "mem3")
            squares(H[:, 1], msq, True)
            dve.wait_ge(ld_misc, 16 * len(misc_loads))
            gsb = sm[:, 0:32].rearrange("p (t c) -> p t c", t=2)
            b = full(dve, "gate")
            taken(tt_(gsb, b[:, 0:32].rearrange("p (t c) -> p t c", t=2), over(gate_b[:, :], [P, 2, 16], 1),
                      ALU.add))
            g5 = sm[:, 0:32].rearrange("p (t d w h) -> p d t w h", t=2, d=2, w=2)

            def u16(a):
                return sm[:, a:a + 16].rearrange("p (d t h) -> p d t h", d=2, t=2)

            link(dve.tensor_copy(u16(48), g5[:, :, :, 1, :]))
            link(ts_(sm[:, 32:48], sm[:, 48:64], -1.0))
            tail(tt_(sm[:, 32:48], sm[:, 32:48], sm[:, 48:64], ALU.max), nf_ready)
            emptied(dve, "qk3")
            for w in range(5):
                for k in range(KT):
                    src = qkp[:, k, w:w + S]
                    cw = v1(V_CW, 8 * w + k)
                    if w:
                        dve.wait_ge(conv_ready, 8 * (w - 1) + k + 1)
                        stt(qkT[:, k], src, cw, qkT[:, k], ALU.mult, ALU.add).then_inc(conv_ready, 1)
                    else:
                        ts_(qkT[:, k], src, cw, v1(V_CB, k), ALU.mult, ALU.add).then_inc(conv_ready, 1)
            dve.wait_ge(lse_ready, 1)
            tail(stt(sm[:, 64:80], sm[:, 48:64], 0.0, sm[:, 96:112], ALU.min, ALU.subtract), lf_ready)
            norm("ss2", H[:, 1], H[:, 1], lambda k: v1(V_GMEM, k))
            emptied(dve, "gv1")
            link(dve.tensor_reduce(sm[:, 260:262], gv[:, :, :], AX.X, ALU.add))
            link(ts_(sm[:, 262:264], sm[:, 260:262], 1.0 / DM))
            link(ts_(gv[:, 0], gv[:, 0], sm[:, 262:263], None, ALU.subtract))
            tail(ts_(gv[:, 1], gv[:, 1], sm[:, 263:264], None, ALU.subtract), gvc_ready)
            b = full(dve, "bcum")
            taken(dve.tensor_copy(sm[:, 900:932], b[:, 0:32]))
            bb, FF = sm[:, 900:916], sm[:, 916:932]
            apc = sm[:, 112:128]
            tail(tt_(u16(112), g5[:, :, :, 0, :], u16(900), ALU.subtract), ap_ready)
            b = full(dve, "apT")
            taken(dve.tensor_copy(sm[0:16, 500:628], b[0:16, 0:P]))
            link(dve.tensor_reduce(sm[0:16, 128:129], sm[0:16, 500:628], AX.X, ALU.max))
            full(dve, "gu1")
            link(tt_(bd, over(sm[0:16, 500:628], [16, 16, P], 1), over(ident[0:16, 0:16], [16, 16, P], 2),
                     ALU.mult))
            tail(ts_(sm[0:16, 129:145], ident[0:16, 0:16], sm[0:16, 128:129]), dmx_ready)
            dve.wait_ge(gvs_ready, 2)
            link(dve.reciprocal(sm[:, 268:270], sm[:, 266:268]))
            for tt in range(TT):
                link(stt(gv[:, tt], gv[:, tt], sm[:, 268 + tt:269 + tt], lng[:, :], ALU.mult, ALU.mult))
            tail(tt_(gv[:, :, :], gv[:, :, :], over(lnb[:, :], [P, 2, DM], 1), ALU.add), gvn_ready)

            b = full(dve, "mxb")
            mxb, ml, M = sm[:, 932:948], sm[:, 948:964], sm[:, 964:980]
            taken(dve.tensor_copy(mxb, b[:, 0:16]))
            link(tt_(ml, FF, mxb, ALU.add))
            for j in range(4):
                b = full(dve, f"A{j}")
                taken(tt_(E[:, 4 * j:4 * j + 4, :], b[:, :].rearrange("p (h s) -> p h s", h=4),
                          over(mask[j // 2], [P, 4, P], 1), ALU.add))
            link(dve.tensor_reduce(M, E[:, :, :], AX.X, ALU.max))
            M2 = M[:, 4:12].rearrange("p (d h) -> p d h", d=2)
            mlp = sm[:, 948:964].rearrange("p (u h) -> p u h", u=4)[:, 0:4:3, :]
            link(tt_(M2, M2, mlp, ALU.max))
            exi, exo = sm[:, 144:184], sm[:, 184:224]
            link(stt(exi[:, 0:16], bb, -1.0, M, ALU.mult, ALU.subtract))
            link(tt_(exi[:, 16:24].rearrange("p (d h) -> p d h", d=2), mlp, M2, ALU.subtract))
            tail(tt_(exi[:, 24:40], apc, mxb, ALU.subtract), ei_ready)
            tail(tt_(E[:, :, :], E[:, :, :], over(M, [P, 16, P], 2), ALU.subtract), em_ready)
            b = full(dve, "mod0")
            modulation(b[:, 0:48], 0)
            dve.wait_ge(ee_ready, 1)
            link(ts_(sm[:, 224:240], exo[:, 24:40], QK_SCALE))
            for d in range(2):
                b = full(dve, f"KT{d}")
                taken(tt_(kw[:, d], b[:, :].rearrange("p (h s) -> p h s", h=4),
                          over(sm[:, 224 + 12 * d:228 + 12 * d], [P, 4, P], 2), ALU.mult))
            dve.wait_ge(e_ready, 1)
            for tt in range(TT):
                b = full(dve, f"QK{tt}")
                for d in range(2):
                    u = 4 * (2 * d + tt)
                    ins = stt(W[:, u:u + 4, :], E[:, u:u + 4, :], QK_SCALE,
                              b[:, :].rearrange("p (h s) -> p h s", h=4), ALU.mult, ALU.mult)
                    if d:
                        taken(ins)
            dve.wait_ge(v_chain, n[0])
            tail(dve.tensor_reduce(sm[:, 980:996], W[:, :, :], AX.X, ALU.add), w_ready)
            b = full(dve, "nn")
            taken(dve.tensor_copy(sm[:, 240:248], b[:, 0:8]))
            emptied(dve, "gu1")
            for tt in range(TT):
                b = full(dve, f"SP{tt}")
                for g in range(NH):
                    c = slice(g * P, g * P + P)
                    ins = stt(gu[:, tt, c], b[:, c], v1(V_BS, g), gu[:, tt, c], ALU.add, ALU.mult)
                taken(ins)
            b = full(dve, "dI")
            den, r = sm[:, 980:996], sm[:, 248:264]
            taken(tt_(sm[:, 300:308], b[:, 0:8], exo[:, 16:24], ALU.mult))
            link(tt_(den[:, 4:12], den[:, 4:12], sm[:, 300:308], ALU.add))
            link(stt(r, den, -1.0, den, ALU.mult, ALU.max))
            link(tt_(r, r, exo[:, 0:16], ALU.max))
            link(dve.reciprocal(r, r))
            link(tt_(sm[:, 300:308], exo[:, 16:24], r[:, 4:12], ALU.mult))
            for j in range(4):
                b = full(dve, f"NI{j}")
                taken(tt_(num[:, 4 * j:4 * j + 4, :], b[:, :].rearrange("p (h s) -> p h s", h=4),
                          over(r[:, 4 * j:4 * j + 4], [P, 4, P], 2), ALU.mult))
            for d in range(2):
                b = full(dve, f"CI{d}")
                for hh in range(NH):
                    u = 4 + 4 * d + hh
                    ins = stt(num[:, u], b[:, hh * P:hh * P + P], sm[:, 300 + 4 * d + hh:301 + 4 * d + hh],
                              num[:, u], ALU.mult, ALU.add)
                taken(ins)
            hs, hq = num[:, 0:8], num[:, 8:16]
            link(tt_(hs, hs, hq, ALU.add))
            link(tt_(hq, hs, hs, ALU.mult))
            tail(dve.tensor_reduce(sm[:, 272:280], hq, AX.X, ALU.add), hss_ready)
            dve.wait_ge(hsd_ready, 1)
            link(dve.reciprocal(sm[:, 280:288], sm[:, 280:288]))
            link(tt_(hs, hs, over(sm[:, 280:288], [P, 8, P], 2), ALU.mult))
            tho2 = tho[:, :, :].rearrange("p t n -> p (t n)")
            tail(stt(tho2, tho2, 1.0, hs.rearrange("p u s -> p (u s)"), ALU.add, ALU.mult), y_ready)
            for g in range(4):
                b = full(dve, f"yT{g}")
                if g < 2:
                    for j in range(2):
                        k = 2 * g + j
                        ins = ts_(yT[:, k], b[:, j * S:j * S + S], v1(V_GHEAD, k), 0.5, ALU.mult, ALU.mult)
                    taken(ins)
                else:
                    taken(dve.tensor_copy(yT[:, 2 * g:2 * g + 2].rearrange("p k s -> p (k s)"), b[:, :]))

            def residual(prefix):
                for g in range(4):
                    b = full(dve, f"{prefix}{g}")
                    v = X[:, 0, 2 * g:2 * g + 2].rearrange("p k s -> p (k s)")
                    taken(tt_(v, v, b[:, :], ALU.add))

            residual("wo")
            squares(X[:, 0], H[:, 0], True)
            norm("ss3", X[:, 0], H[:, 0], lambda k: v1(V_GX, k))

            def maxima(names, heads, width, col, scale):
                for g, name in enumerate(names):
                    b = full(dve, name)
                    c = col + heads * g
                    link(dve.tensor_reduce(sm[:, c:c + heads], b[:, :].rearrange("p (h m) -> p h m", h=heads),
                                           AX.X, ALU.max))
                    tail(ts_(sm[:, c:c + heads], sm[:, c:c + heads], -scale), mx_ready)

            def normalise(p, width, col, last):
                emptied(dve, last)
                link(dve.reciprocal(sm[:, col:col + 8], sm[:, col:col + 8]))
                v = p.rearrange("p t h m -> p (t h) m")
                tail(tt_(v, v, over(sm[:, col:col + 8], [P, 8, width], 2), ALU.mult), pn_ready)

            maxima([f"S{g}" for g in range(4)], 2, 256, 288, X_SCALE)
            normalise(px, 256, 296, "S3")
            residual("xw")
            squares(X[:, 0], H[:, 0], True)
            norm("ss4", X[:, 0], H[:, 0], lambda k: v1(V_GMOE, k))

            b = full(dve, "lg")
            lg = sm[:, 392:464].rearrange("p (t e) -> p t e", t=2)
            taken(tt_(lg, b[:, 0:72].rearrange("p (t e) -> p t e", t=2), over(rb[:, :], [P, 2, 36], 1), ALU.add))
            scr = sm[:, 500:564].rearrange("p (t e) -> p t e", t=2)

            def first_max(vals, w, mx, one):
                s = scr[:, :, 0:w]
                link(dve.tensor_reduce(mx, vals, AX.X, ALU.max))
                link(tt_(s, vals, over(mx, [P, 2, w], 2), ALU.is_equal))
                link(ts_(s, s, -64.0, 64.0, ALU.mult, ALU.add))
                link(tt_(s, s, over(iota[:, 0:w], [P, 2, w], 1), ALU.add))
                link(dve.tensor_reduce(sm[:, 570:572], s, AX.X, ALU.min))
                link(tt_(one, over(iota[:, 0:w], [P, 2, w], 1), over(sm[:, 570:572], [P, 2, w], 2), ALU.is_equal))

            gl, el = lg[:, :, 0:NG], lg[:, :, NG:NG + NE]
            gmax, m1, m2 = sm[:, 572:574], sm[:, 574:576], sm[:, 576:578]
            og = sm[:, 580:588].rearrange("p (t g) -> p t g", t=2)
            first_max(gl, NG, gmax, og)
            tail(tt_(sm[:, 464:472].rearrange("p (t g) -> p t g", t=2), gl, over(gmax, [P, 2, NG], 2),
                     ALU.subtract), ge_ready)
            em = sm[:, 588:652]
            em4 = em.rearrange("p (q e) -> p q e", q=8)
            em3 = em.rearrange("p (t e) -> p t e", t=2)
            link(dve.tensor_copy(em3, el))
            link(tt_(em4, em4, over(sm[:, 580:588], [P, 8, EPG], 2), ALU.mult))
            link(ts_(sm[:, 652:660], sm[:, 580:588], BIG, -BIG, ALU.mult, ALU.add))
            link(tt_(em4, em4, over(sm[:, 652:660], [P, 8, EPG], 2), ALU.add))
            o1 = sm[:, 664:728].rearrange("p (t e) -> p t e", t=2)
            o2 = sm[:, 728:792].rearrange("p (t e) -> p t e", t=2)
            first_max(em3, NE, m1, o1)
            link(stt(em, sm[:, 664:728], -2.0 * BIG, em, ALU.mult, ALU.add))
            first_max(em3, NE, m2, o2)
            tail(tt_(sm[:, 482:484], m2, m1, ALU.subtract), me_ready)
            tail(tt_(sm[:, 320:384], sm[:, 664:728], sm[:, 728:792], ALU.add), A_ready)
            dve.wait_ge(ge_exp, 1)
            link(dve.tensor_reduce(sm[:, 486:488], sm[:, 472:480].rearrange("p (t g) -> p t g", t=2), AX.X, ALU.add))
            dve.wait_ge(me_exp, 1)
            w1_, w2_ = sm[:, 488:490], sm[:, 490:492]
            link(stt(sm[:, 486:488], sm[:, 484:486], 1.0, sm[:, 486:488], ALU.add, ALU.mult))
            link(dve.reciprocal(w1_, sm[:, 486:488]))
            link(tt_(w2_, w1_, sm[:, 484:486], ALU.mult))
            b = full(dve, "pos")
            posn = sm[:, 792:888]
            link(dve.tensor_copy(sm[0:32, 888:889], b[0:32, 96:97]))
            taken(dve.tensor_copy(posn, b[:, 0:96]))
            tail(ts_(sm[0:32, 1000:1128], ones[0:32, :], sm[0:32, 888:889]), cnt_ready)
            b = full(dve, "start")
            taken(dve.tensor_copy(sm[:, 1034 - 134:1034 - 134 + 32], b[:, 0:32]))
            strt = sm[:, 900:932]
            slt = sm[:, 792:856].rearrange("p (t e) -> p t e", t=2)
            for q in range(4):
                ins = ts_(win[0:1, q * NE:q * NE + NE], strt[0:1, :], float(C * q), float(A), ALU.add, ALU.min)
                link(ins) if q < 3 else tail(ins, win_ready)
            link(dve.tensor_reduce(sm[0:1, 889:890], sm[0:1, 856:888], AX.X, ALU.max))
            tail(dve.tensor_copy(mxc[:, :], sm[0:1, 889:890]), win_ready)
            link(tt_(slt, slt, over(strt, [P, 2, NE], 1), ALU.add))
            for o, c in ((664, 478), (728, 480)):
                link(tt_(sm[:, 500:564], sm[:, o:o + 64], sm[:, 792:856], ALU.mult))
                link(dve.tensor_reduce(sm[:, c:c + 2], scr, AX.X, ALU.add))
            for tt in range(TT):
                s1, s2 = sm[:, 478 + tt:479 + tt], sm[:, 480 + tt:481 + tt]
                link(ts_(Pw[:, tt], iota, s1, None, ALU.is_equal))
                ins = stt(Pm[:, tt], iota, s2, Pw[:, tt], ALU.is_equal, ALU.add)
                link(ins)
            tail(dve.memset(xs[:, :, A:AP_], 0.0), P_ready)
            for tt in range(TT):
                s1, s2 = sm[:, 478 + tt:479 + tt], sm[:, 480 + tt:481 + tt]
                link(ts_(Pw[:, tt], iota, s1, w1_[:, tt:tt + 1], ALU.is_equal, ALU.mult))
                link(ts_(ys[:, 0, 0:A], iota, s2, w2_[:, tt:tt + 1], ALU.is_equal, ALU.mult))
                link(tt_(Pw[:, tt], Pw[:, tt], ys[:, 0, 0:A], ALU.add))
            emptied(dve, "mod1")
            modulation(sm[:, 1130:1178], 1)

            full(dve, "xs7")

            def vector_step(e, parity, has):
                gate, out1 = has
                if gate:
                    dve.wait_ge(fast[TH], e + 1)
                    dve.wait_ge(fast[UF], e + 1)
                    if gate == "wait":
                        dve.wait_ge(fast[AF], e - 1)
                    stt(th[:, parity], th[:, parity], 1.0, bank[parity][0:C, :], ALU.add, ALU.mult)\
                        .then_inc(chain_e, 1)
                    dve.wait_ge(chain_e, e + 1)
                    stt(ac[:, parity], th[:, parity], 0.5, bank[2 + parity][0:C, :], ALU.mult, ALU.mult)\
                        .then_inc(fast[AC], 1)
                if out1:
                    dve.wait_ge(fast[YF], e)
                    if out1 == "wait":
                        dve.wait_ge(fast[TF], e - 2)
                    dve.tensor_copy(yb[:, 1 - parity, 0:512], bank[5][0:C, :])
                    dve.tensor_copy(yb[:, 1 - parity, 512:1024], bank[6][0:C, :]).then_inc(fast[YB], 1)

            vector_step(0, 0, (True, False))
            vector_step(1, 1, (True, True))
            vector_step(2, 0, ("wait", True))
            vector_step(3, 1, ("wait", "wait"))
            with dve.Fori(0, (NE - 4) // 2) as i:
                for j in range(2):
                    vector_step(i * 2 + (4 + j), j, ("wait", "wait"))
            vector_step(NE, 0, (False, "wait"))

            rows_max = dve.value_load(mxc[0:1, 0:1], min_val=0, max_val=S)
            with dve.If(rows_max > C):
                with dve.Fori(0, NE) as e:
                    for q in range(4):
                        dve.wait_ge(slow[TH], e * 4 + (q + 1))
                        dve.wait_ge(slow[UF], e * 4 + (q + 1))
                        stt(th[:, 0], th[:, 0], 1.0, bank[0][0:C, :], ALU.add, ALU.mult).then_inc(chain_s, 1)
                        dve.wait_ge(chain_s, e * 4 + (q + 1))
                        stt(ac[:, 0], th[:, 0], 0.5, bank[2][0:C, :], ALU.mult, ALU.mult).then_inc(slow[AC], 1)
                        dve.wait_ge(slow[YF], e * 4 + (q + 1))
                        dve.tensor_copy(yb[:, 0, 0:512], bank[5][0:C, :])
                        dve.tensor_copy(yb[:, 0, 512:1024], bank[6][0:C, :]).then_inc(slow[YB], 1)

            for g in range(0, 8, 2):
                st, half = divmod(g, 2)
                b = full(dve, f"yt{g}")
                taken(dve.tensor_copy(yk[:, st, half * 512:half * 512 + 512], b[:, :]))
            residual("co")
            squares(X[:, 0], H[:, 0], True)
            norm("ss5", X[:, 0], X[:, 0], lambda k: v1(V_GFIN, k))

            for L in range(2):
                R = 2 - L

                def two(v):
                    return v.rearrange("p r s -> p (r s)")

                squares(X[:, :, :, :], H[:, :, :, :], True)
                inverse_root(f"{L}ss", 2 * S)
                for r in range(2):
                    link(tt_(H[:, r], X[:, r], over(rs[:, r], [P, KT, S], 1), ALU.mult))
                for r in range(2):
                    for k in range(KT):
                        ins = ts_(H[:, r, k], H[:, r, k], gsc[:, L, k, r:r + 1], mod[:, L, k, r:r + 1],
                                  ALU.mult, ALU.add)
                tail(ins, h_ready)
                link(dve.memset(tp[:, :, :, 0:1], 0.0))
                link(dve.memset(tp[:, :, :, 1 + S:2 + S], 0.0))
                for i in range(2):
                    emptied(dve, f"{L}c{i}")
                    b = full(dve, f"{L}h{i}")
                    taken(tt_(tp[:, i, 0:R, 1:1 + S], b[:, 0:R * S].rearrange("p (r s) -> p r s", r=R),
                              cs2[:, i, 0:R], ALU.mult))
                for i in range(2):
                    o = cs2[:, i, 0:R]

                    def cw2(w):
                        return v2(V_CW2, (L * 3 + w) * 2 + i)

                    link(ts_(o, tp[:, i, 0:R, 0:S], cw2(0), v2(V_CB2, 2 * L + i), ALU.mult, ALU.add))
                    for w in (1, 2):
                        link(stt(o, tp[:, i, 0:R, w:w + S], cw2(w), o, ALU.mult, ALU.add))
                    link(tt_(o, o, bs2[:, i, 0:R], ALU.mult))
                emptied(dve, f"{L}zc1")
                link(tt_(oT[:, 4, 0:R], oT[:, 4, 0:R], cs2[:, 0, 0:R], ALU.mult))
                tail(tt_(oT[:, 5, 0:R], oT[:, 5, 0:R], cs2[:, 1, 0:R], ALU.mult), conv2_ready)
                emptied(dve, f"{L}qkv3")
                qsq = view(8192, 1536, t=4, n=384)

                def heads(v, t0, t1, h0_, h1_):
                    return v[:, t0:t1, h0_ * HD2:h1_ * HD2].rearrange("p t (h e) -> p t h e", e=HD2)

                parts = [(0, 4, 0, 6)] if L == 0 else [(0, 2, 0, 6), (2, 4, 4, 6)]
                for a0, a1, b0, b1 in parts:
                    link(tt_(heads(qsq, a0, a1, b0, b1), heads(qkv, a0, a1, b0, b1),
                             heads(qkv, a0, a1, b0, b1), ALU.mult))
                ssq = sm[:, 600:624].rearrange("p (t h) -> p t h", t=4)
                link(dve.memset(sm[:, 600:624], 1.0))
                for n_, (a0, a1, b0, b1) in enumerate(parts):
                    ins = dve.tensor_reduce(ssq[:, a0:a1, b0:b1], heads(qsq, a0, a1, b0, b1), AX.X, ALU.add)
                    tail(ins, qs_ready) if n_ == len(parts) - 1 else link(ins)
                dve.wait_ge(qd_ready, L + 1)
                link(dve.reciprocal(sm[:, 648:672], sm[:, 624:648]))
                rq = sm[:, 648:672].rearrange("p (t h) -> p t h", t=4)
                for a0, a1, b0, b1 in parts:
                    for ta in range(a0, a1):
                        v = heads(qkv, ta, ta + 1, b0, b1)[:, 0]
                        link(tt_(v, v, over(rq[:, ta, b0:b1], [P, b1 - b0, HD2], 2), ALU.mult))
                        ins = tt_(v, v, gains[:, L, b0:b1, :], ALU.mult)
                        link(ins)
                weights(dve, f"{L}const")
                rope = ring[:, place[f"{L}const"], ROPE0:ROPE0 + 128].rearrange("p (t c a f) -> p t c a f", t=2, c=2, a=2)
                for tt in range(TT):
                    v = qkv[:, tt, 0:384].rearrange("p (h a w f) -> p h a w f", h=6, a=2, w=2)
                    for a in range(2):
                        x1, x2 = v[:, :, a, 0, :], v[:, :, a, 1, :]
                        cos = over(rope[:, tt, 0, a, :], [P, 6, 16], 1)
                        sin = over(rope[:, tt, 1, a, :], [P, 6, 16], 1)
                        T = [sm[:, 500 + 96 * 0:596], sm[:, 1000:1096], sm[:, 792:888], sm[:, 392:488]]
                        T = [x.rearrange("p (h f) -> p h f", h=6) for x in T]
                        for o, p1, p2 in ((T[0], x1, cos), (T[1], x2, sin), (T[2], x2, cos), (T[3], x1, sin)):
                            ins = tt_(o, p1, p2, ALU.mult)
                        link(ins)
                        tt_(x1, T[0], T[1], ALU.subtract)
                        ins = tt_(x2, T[2], T[3], ALU.add)
                        tail(ins, rope_ready) if tt == 1 and a == 1 else link(ins)
                for i in range(2):
                    b = full(dve, f"{L}pl{i}")
                    emptied(dve, f"{L}zp{i}")
                    o = two(oT[:, 6 + i, 0:R])
                    taken(stt(o, b[:, 0:R * S], v2(V_PS, 2 * L + i), o, ALU.mult, ALU.mult))
                for i in range(2):
                    b = full(dve, f"{L}wf{i}")
                    emptied(dve, f"{L}zf{i}")
                    o = two(oT[:, i, 0:R])
                    taken(tt_(o, o, b[:, 0:R * S], ALU.mult))
                if L == 0:
                    maxima([f"0cS{g}" for g in range(4)], 2, 256, 680, A_SCALE)
                    normalise(pc2, 256, 688, "0cS3")
                    for i in range(2):
                        b = full(dve, f"0co{i}")
                        o = oT[:, 2 + i, 1]
                        taken(tt_(o, o, b[:, 0:S], ALU.mult))
                maxima([f"{L}xS{g}" for g in range(8)], 1, 512, 700, A_SCALE)
                normalise(px2, 512, 708, f"{L}xS7")
                for i in range(2):
                    b = full(dve, f"{L}xo{i}")
                    o = oT[:, 2 + i, 0]
                    taken(tt_(o, o, b[:, 0:S], ALU.mult))
                for k in range(KT):
                    b = full(dve, f"{L}out{k}")
                    for r in range(R):
                        ins = stt(X[:, r, k], b[:, r * S:r * S + S], mod[:, L, 16 + k, r:r + 1], X[:, r, k],
                                  ALU.mult, ALU.add)
                    taken(ins)


def constants():
    import numpy as np

    i, j = np.arange(P)[:, None], np.arange(P)[None, :]
    one = np.zeros((P, CONST1), np.float32)
    for at, m in ((ID0, i == j), (TRF0, i <= j), (TRB0, i >= j), (TRS0, i < j), (ONE0, i == i + 0 * j),
                  (MKF0, np.where(j <= i, 0.0, -BIG)), (MKB0, np.where(j >= i, 0.0, -BIG))):
        one[:, at:at + P] = m
    one[:, IO0:] = np.arange(A)[None, :]

    def by_tile(m):
        return m.reshape(TT, P, -1).transpose(1, 0, 2).reshape(P, -1)

    two = np.zeros((P, CONST2), np.float32)
    a = 2 * np.pi * (np.outer(np.arange(S), np.arange(S)) % S) / S
    two[:, DFT0:CD0] = by_tile(np.concatenate([np.cos(a), np.sin(a)], 1) / np.sqrt(S))
    a = 2 * np.pi * (np.outer(np.arange(64), np.arange(64)) % 64) / 64
    for h in range(2):
        c = slice(64 * h, 64 * h + 64)
        two[c, CD0 + 64 * h:CD0 + 64 * h + 64] = np.cos(a) / 8
        two[c, CD0 + P + 64 * h:CD0 + P + 64 * h + 64] = -np.sin(a) / 8
    pool = np.zeros((S, 4, S))
    tok = np.arange(S)
    for n, w in enumerate((2, 4, 8, 16)):
        lo, hi = np.clip(tok - w // 2, 0, S), np.clip(tok + w - w // 2, 0, S)
        inside = (tok[:, None] >= lo[None, :]) & (tok[:, None] < hi[None, :])
        pool[:, n, :] = inside / (hi - lo)[None, :] - np.eye(S)
    two[:, POOL0:ROPE0] = by_tile(pool)
    inv = 10000.0 ** (-np.arange(16) / 16)
    ang = np.stack([(tok // 64)[:, None] * inv, (tok % 64)[:, None] * inv], 1)
    two[:, ROPE0:] = by_tile(np.stack([np.cos(ang), np.sin(ang)], 1))
    return one, two


_INS = ['x', 'mem', 'g_mix', 'w_in', 'conv_w', 'conv_b', 'gate_b', 'g_head', 'ln_v_g', 'ln_v_b', 'w_s', 'b_s',
        'w_out', 'g_xattn', 'g_mem', 'w_q_x', 'w_kv_x', 'w_o_x', 'g_moe', 'w_rg', 'b_rg', 'w_re', 'b_re',
        'w_gate', 'w_up', 'w_down', 'g_final', 'c_2', 'ctx_2', 'c_ctx_2', 'w_mod_2', 'b_mod_2', 'norm_g_2',
        'w_in_2', 'q_gain_2', 'k_gain_2', 'w_fourier_2', 'conv_w_2', 'conv_b_2', 'pool_w_2', 'pool_scale_2',
        'w_out_2']


def kernel(**inputs):
    import numpy as _np
    import concourse.bacc as _bacc
    from concourse import mybir as _mybir
    from concourse.bass_utils import run_bass_kernel_spmd as _run

    nc = _bacc.Bacc("TRN2", target_bir_lowering=False, num_devices=1, dynamic_dma_scratch_size=1024)
    arrays, tensors = {}, {}
    one, two = constants()
    for name, a in [(n, inputs[n]) for n in _INS] + [("const1", one), ("const2", two)]:
        a = _np.ascontiguousarray(a)
        arrays[f"in_{name}_dram"] = a
        tensors[name] = nc.dram_tensor(f"in_{name}_dram", a.shape, _mybir.dt.from_np(a.dtype),
                                       kind="ExternalInput").ap()
    tensors["out"] = nc.dram_tensor("out_0_dram", (1, S, D), F32, kind="ExternalOutput").ap()
    first_and_second_block(nc, tensors)
    r = _run(nc, [arrays], core_ids=[0])
    return r.results[0]["out_0_dram"]
```

```python
from contextlib import ExitStack

import concourse.bass as bass
from concourse import mybir

F32 = mybir.dt.float32
I32 = mybir.dt.int32
ALU = mybir.AluOpType
ACT = mybir.ActivationFunctionType
AX = mybir.AxisListType

P = 128
D = 1024
KT = D // P
S = 256
TT = S // P
NH = 4
DM = 512
NE = 32
NG = 4
EPG = NE // NG
FE = 512
C = 64
A = 2 * S
AP_ = A + C
RMS_EPS, LN_EPS = 1e-6, 1e-5
BIG = 1e30
SLOTS = 6
CW = 4096
HD2 = 64
W2 = 256
QK_SCALE = 128.0 ** -0.5
X_SCALE = 256.0 ** -0.5
A_SCALE = 64.0 ** -0.5

ID0, TRF0, TRB0, TRS0, ONE0, MKF0, MKB0, IO0 = (i * P for i in range(8))
CONST1 = IO0 + A
DFT0, CD0, POOL0, ROPE0 = 0, 1024, 1280, 1280 + 2048
CONST2 = ROPE0 + 128
WF0 = CONST2

V_GMIX, V_CB, V_CW, V_GX, V_GMEM, V_GMOE, V_GFIN, V_GHEAD, V_BS, NV1 = 0, 8, 16, 56, 64, 72, 80, 88, 92, 96
V_NG, V_BMOD, V_C, V_CW2, V_CB2, V_PS, NV2 = 0, 16, 64, 80, 92, 96, 100

NORMS = ["ss1", "ss2", "ss3", "ss4", "ss5", "0ss", "1ss"]
SQ_BASE = {name: 4 * n for n, name in enumerate(NORMS)}
H_BASE = {name: 8 * n for n, name in enumerate(NORMS)}

MOD0_SPLIT, MOD1_SPLIT = 4, (1, 4)

ORDER = [(f"x{g}", "a") for g in range(4)] + [("vec1", "v"), ("ss1", "a"), ("qk0", "a"), ("qk1", "a")]
ORDER += [(f"mem{g}", "a") for g in range(4)] + [("ss2", "a")] + [(f"ctx{g}", "a") for g in range(4)]
ORDER += [("vec2", "v"), ("qk2", "a"), ("qk3", "a"), ("gate", "v"), ("ws", "a")]
ORDER += [(f"v{t}", "a") for t in range(2)] + [(f"o{t}", "a") for t in range(2)]
ORDER += [(f"gv{t}", "a") for t in range(2)] + [(f"gu{t}", "a") for t in range(2)]
ORDER += [(f"km{g}", "a") for g in range(4)]
ORDER += [("bcum", "v"), ("apT", "v")] + [(f"vm{g}", "a") for g in range(4)] + [("mxb", "v")]
ORDER += [(f"A{j}", "v") for j in range(4)]


def modulation_groups(L, c0, c1):
    names = []
    for c in range(c0, c1):
        names += [f"mr{L}{c}"] + ([f"mt{L}{c - 1}"] if c else [])
    return names + ([f"mt{L}5"] if c1 == 6 else [])


ORDER += [(n, "a") for n in modulation_groups(0, 0, MOD0_SPLIT)]
ORDER += [(f"KT{d}", "v") for d in range(2)] + [(f"QK{t}", "v") for t in range(2)]
ORDER += [(f"C{d}", "a") for d in range(2)] + [("nn", "v")] + [(f"SP{t}", "v") for t in range(2)]
ORDER += [(f"WT{j}", "a") for j in range(4)] + [("dI", "v")]
ORDER += [(f"NI{j}", "v") for j in range(4)] + [(f"CI{d}", "v") for d in range(2)]
ORDER += [(n, "a") for n in modulation_groups(0, MOD0_SPLIT, 6)]
ORDER += [(f"yT{g}", "v") for g in range(4)] + [(f"wo{g}", "v") for g in range(4)]
ORDER += [("ss3", "a")] + [(f"xq{g}", "a") for g in range(4)] + [(f"S{g}", "a") for g in range(4)]
ORDER += [(n, "a") for n in modulation_groups(1, 0, MOD1_SPLIT[0])]
ORDER += [(f"pT{h}", "a") for h in range(4)] + [(f"xo{h}", "a") for h in range(4)]
ORDER += [(f"xw{g}", "v") for g in range(4)]
ORDER += [("ss4", "a"), ("lg", "v")] + [(f"hk{g}", "a") for g in range(4)]
ORDER += [(n, "a") for n in modulation_groups(1, MOD1_SPLIT[0], MOD1_SPLIT[1])]
ORDER += [("pos", "v"), ("start", "v"), ("css", "a")]
ORDER += [(n, "a") for n in modulation_groups(1, MOD1_SPLIT[1], 6)]
ORDER += [(f"xs{k}", "a") for k in range(8)]
LOOP_AT = len(ORDER)
ORDER += [(f"pw{g}", "a") for g in range(2)] + [(f"yt{g}", "va"[g % 2]) for g in range(8)]
ORDER += [(f"co{g}", "v") for g in range(4)] + [("ss5", "a")]
for L in range(2):
    R = 2 - L
    if L == 0:
        ORDER += [("0qkv2", "a"), ("0ss", "a"), ("0qkv3", "a"), ("0qkv0", "a"), ("0qkv1", "a")]
    else:
        ORDER += [("1ss", "a")] + [(f"1qkv{t}", "a") for t in range(4)]
    ORDER += [(f"{L}za{i}", "a") for i in range(2)] + [(f"{L}uf{t}", "a") for t in range(R)]
    ORDER += [(f"{L}zf{i}", "a") for i in range(2)] + [(f"{L}b{i}", "a") for i in range(2)]
    ORDER += [(f"{L}c{i}", "a") for i in range(2)] + [(f"{L}h{i}", "v") for i in range(2)]
    ORDER += [(f"{L}zc{i}", "a") for i in range(2)] + [(f"{L}up{t}", "a") for t in range(R)]
    ORDER += [(f"{L}zp{i}", "a") for i in range(2)]
    ORDER += [(f"{L}hT{h}", "a") for h in range(6)]
    if L == 0:
        ORDER += [(f"{L}cS{g}", "a") for g in range(4)]
    ORDER += [(f"{L}xS{g}", "a") for g in range(8)]
    ORDER += [(f"{L}B{s}{i}", "a") for s in range(R) for i in range(2)]
    ORDER += [(f"{L}dT{i}", "a") for i in range(2)]
    ORDER += [(f"{L}yf{i}", "a") for i in range(2)] + [(f"{L}pl{i}", "v") for i in range(2)]
    ORDER += [(f"{L}wf{i}", "v") for i in range(2)]
    if L == 0:
        ORDER += [(f"{L}cP{h}", "a") for h in range(4)] + [(f"{L}co{i}", "v") for i in range(2)]
    ORDER += [(f"{L}xP{g}", "a") for g in range(8)] + [(f"{L}xo{i}", "v") for i in range(2)]
    ORDER += [(f"{L}out{k}", "v") for k in range(8)]
ORDER += [(f"fin{g}", "a") for g in range(4)]
INDEX = {name: n for n, (name, _) in enumerate(ORDER)}


def drained_by(name):
    n = INDEX[name]
    who = ORDER[n][1]
    return who, sum(1 for _, w in ORDER[:n + 1] if w == who)


def first_and_second_block(nc, t):
    w_in, w_in2 = t["w_in"][0], t["w_in_2"]

    def rows(w, c0, n):
        return w[:, c0:c0 + n].rearrange("(k p) n -> p k n", p=P)

    before, after = [], []
    for i, (c0, last) in enumerate([(0, "qk1"), (512, "qk3"), (1024, "v1"), (1536, "o1"), (2576, "gv1"),
                                    (2064, "gu1")]):
        before.append((f"in{i}", [(0, rows(w_in, c0, 512))], last))
    for i, last in enumerate(["km1", "km3", "vm1", "vm3"]):
        before.append((f"kv{i}", [(0, rows(t["w_kv_x"][0], 512 * i, 512))], last))

    def mod_chunks(L, c0, c1):
        return [(f"mod{L}{i}", [(0, rows(t["w_mod_2"][L], 512 * i, 512))], f"mr{L}{i}") for i in range(c0, c1)]

    before += mod_chunks(0, 0, 6)
    before += [(f"wout{i}", [(0, rows(t["w_out"][0], 512 * i, 512))], f"wo{2 * i + 1}") for i in range(2)]
    before += [(f"wq{i}", [(0, rows(t["w_q_x"][0], 512 * i, 512))], f"xq{2 * i + 1}") for i in range(2)]
    before += mod_chunks(1, 0, MOD1_SPLIT[0])
    before += [(f"wox{i}", [(0, rows(t["w_o_x"][0], 512 * i, 512))], f"xw{2 * i + 1}") for i in range(2)]
    before += mod_chunks(1, MOD1_SPLIT[0], 6)
    for L in range(2):
        lasts = [f"{L}qkv{2 * L + 1}", f"{L}uf{1 - L}", f"{L}b1", f"{L}h1", f"{L}up{1 - L}", f"{L}zp1"]
        for i, last in enumerate(lasts):
            after.append((f"{L}in{i}", [(0, rows(w_in2[L], 512 * i, min(512, 2816 - 512 * i)))], last))
        after.append((f"{L}const", [(0, t["const2"]), (WF0, rows(t["w_fourier_2"][L], 0, W2))], f"{L}wf1"))
        if L == 0:
            after.append(("0pc", [], "0co1"))
        after += [(f"{L}px", [], f"{L}xP7"), (f"{L}pT", [], f"{L}xo1")]
        after += [(f"{L}wout{i}", [(0, rows(t["w_out_2"][L], 512 * i, 512))], f"{L}out{4 * i + 3}")
                  for i in range(2)]
    NB = len(before)
    experts = ["G0", "U0"] + [f"{m}{e - (m == 'D')}" for e in range(1, NE) for m in "GUD"] + [f"D{NE - 1}"]
    place = {name: (n % SLOTS) for n, name in
             enumerate([c[0] for c in before] + experts + [c[0] for c in after])}
    count = [0] * SLOTS
    landed = {}
    for name, pieces in [c[:2] for c in before] + [(e, [0]) for e in experts] + [c[:2] for c in after]:
        count[place[name]] += 16 * len(pieces)
        landed[name] = count[place[name]]

    with ExitStack() as ctx:
        def sb(name, shape, dt=F32):
            return ctx.enter_context(nc.sbuf_tensor(name, shape, dt))

        def sem(name):
            return ctx.enter_context(nc.semaphore(name))

        ring = sb("ring", [P, SLOTS, CW])
        c1 = sb("c1", [P, CONST1])
        X = sb("X", [P, 2, KT, S])
        H = sb("H", [P, 2, KT, S])
        AR = 14368
        ar = sb("ar", [P, AR])
        raw = sb("raw", [P, 2, P])
        vT = sb("vT", [P, NV1 + NV2])
        wg = sb("wg", [P, KT, 16])
        wr = sb("wr", [P, KT, NG + NE])
        gate_b = sb("gate_b", [P, 16])
        rb = sb("rb", [P, NG + NE])
        lng = sb("lng", [P, DM])
        lnb = sb("lnb", [P, DM])
        gains = sb("gains", [P, 2, 6, HD2])
        wsr = sb("wsr", [P, NH, P])
        wsT = sb("wsT", [P, NH, P])
        pwb = sb("pwb", [P, 2, 2, P])
        sd = sb("sd", [P, 2, S])
        rs = sb("rs", [P, 2, S])
        mrow = sb("mrow", [2, 2, 512])
        modr = sb("modr", [P, 2, 48])
        mod = sb("mod", [P, 2, 24, 2])
        gsc = sb("gsc", [P, 2, KT, 2])
        sc = sb("sc", [P, 2, KT])
        sm = sb("sm", [P, 1200])
        win = sb("win", [1, 4 * NE], I32)
        mxc = sb("mxc", [1, 1], I32)

        bank = [ctx.enter_context(nc.psum_tensor(f"bank{i}", [P, 512], F32)) for i in range(8)]

        def slot(name, k=KT, n=512, c0=0):
            return ring[:, place[name], c0:c0 + k * n].rearrange("p (k n) -> p k n", k=k)

        ident, trf, trb = c1[:, ID0:ID0 + P], c1[:, TRF0:TRF0 + P], c1[:, TRB0:TRB0 + P]
        trs, ones = c1[:, TRS0:TRS0 + P], c1[:, ONE0:ONE0 + P]
        mask = [c1[:, MKF0:MKF0 + P], c1[:, MKB0:MKB0 + P]]
        iota = c1[:, IO0:IO0 + A]

        def view(at, cols, **dims):
            v = ar[:, at:at + cols]
            names = " ".join(dims)
            last = dict(list(dims.items())[:-1])
            return v.rearrange(f"p ({names}) -> p {names}", **last) if len(dims) > 1 else v

        qkp = view(0, 2080, k=8, s=260)
        W = view(0, 2048, u=16, s=128)
        num = view(0, 2048, u=16, s=128)
        qkT = view(2080, 2048, k=8, s=256)
        yT = qkT
        vs = view(4128, 1024, t=2, n=512)
        tho = view(5152, 1024, t=2, n=512)
        gu = view(6176, 1024, t=2, n=512)
        gv = view(7200, 1024, t=2, n=512)
        kmT = view(8224, 2048, k=8, s=256)
        vm = view(10272, 2048, t=2, n=1024)
        E = view(12320, 2048, u=16, s=128)
        WT = E
        Ej = view(12320, 1024, t=2, n=512)
        msq = view(4128, 2048, k=8, s=256)
        xin = view(10272, 2048, t=2, n=1024)
        memin = view(12320, 2048, t=2, n=1024)
        ctxin = view(8224, 2048, t=2, n=1024)
        h0 = H[:, 0].rearrange("p k s -> p (k s)")
        bd = h0[0:16, :].rearrange("p (u s) -> p u s", u=16)
        kw = h0[:, 0:1024].rearrange("p (d h s) -> p d h s", d=2, h=4)
        Cs = h0[:, 1024:2048].rearrange("p (d h s) -> p d h s", d=2, h=4)
        xqT = view(0, 2048, k=8, s=256)
        pTx = view(2080, 2048, h=4, m=2, s=256)
        oTx = view(4128, 2048, k=8, s=256)
        px = view(12320, 2048, t=2, h=4, m=256)
        hk = view(0, 2048, t=2, n=1024)
        Pm = view(2048, 1024, t=2, a=512)
        Pw = view(3072, 1024, t=2, a=512)
        xs = view(4096, 8 * AP_, k=8, a=AP_)
        ys = view(8704, 8 * AP_, k=8, a=AP_)
        xe = view(0, 1024, b=2, k=8, c=64)
        th = view(1024, 1024, b=2, f=512)[0:C]
        ac = view(2048, 1024, b=2, f=512)[0:C]
        acT = view(13312, 512, b=2, k=4, c=64)
        yb = h0.rearrange("p (b n) -> p b n", b=2)[0:C]
        yk = view(4096, 4096, a=4, n=1024)
        PwT = view(0, 1024, a=4, s=256)
        oT = view(0, 4096, k=8, r=2, s=256)
        qkv = view(4096, 2048, t=4, n=512)
        uf = view(6144, 1024, t=4, n=256)
        up = view(7168, 1024, t=4, n=256)
        bs2 = view(8192, 1024, k=2, r=2, s=256)
        cs2 = view(9216, 1024, k=2, r=2, s=256)
        tp = view(10240, 1032, k=2, r=2, s=258)
        q2T = view(11296, 3072, h=6, s=512)[0:HD2]
        hf = H[:, :].rearrange("p r k s -> p (r k s)")
        B2 = hf[:, 0:2048].rearrange("p (r k s) -> p r k s", r=2, k=2)
        yf2 = hf[:, 2048:3072].rearrange("p (k r s) -> p k r s", k=2, r=2)
        dT2 = hf[:, 3072:4096].rearrange("p (k r s) -> p k r s", k=2, r=2)
        outb = view(0, 2048, t=2, n=1024)

        ld_x, ld_mem, ld_ctx, ld_const, ld_vec1, ld_vec2, ld_gates, ld_misc = (
            sem(n) for n in ("ld_x", "ld_mem", "ld_ctx", "ld_const", "ld_vec1", "ld_vec2", "ld_gates", "ld_misc"))
        w_loaded = [sem(f"w_loaded{i}") for i in range(SLOTS)]
        psum_full = sem("psum_full")
        a_drained = sem("a_drained")
        v_drained = sem("v_drained")
        a_chain, v_chain = sem("a_chain"), sem("v_chain")
        sq_ready = sem("sq_ready")
        h_ready = sem("h_ready")
        csq_ready = sem("csq_ready")
        ctx_ready = sem("ctx_ready")
        conv_ready = sem("conv_ready")
        qk_ready = sem("qk_ready")
        nf_ready, lse_ready, lf_ready = sem("nf_ready"), sem("lse_ready"), sem("lf_ready")
        ap_ready, dmx_ready = sem("ap_ready"), sem("dmx_ready")
        em_ready, e_ready = sem("em_ready"), sem("e_ready")
        ei_ready, ee_ready = sem("ei_ready"), sem("ee_ready")
        w_ready, gvc_ready, gvs_ready, gvn_ready = (sem(n) for n in ("w_ready", "gvc_ready", "gvs_ready",
                                                                     "gvn_ready"))
        hss_ready, hsd_ready, y_ready = sem("hss_ready"), sem("hsd_ready"), sem("y_ready")
        mx_ready, px_ready, pn_ready = sem("mx_ready"), sem("px_ready"), sem("pn_ready")
        sc_ready = sem("sc_ready")
        ge_ready, ge_exp, me_ready, me_exp = (sem(n) for n in ("ge_ready", "ge_exp", "me_ready", "me_exp"))
        A_ready, cnt_ready, P_ready, win_ready = (sem(n) for n in ("A_ready", "cnt_ready", "P_ready",
                                                                   "win_ready"))
        qs_ready, qd_ready, rope_ready = sem("qs_ready"), sem("qd_ready"), sem("rope_ready")
        conv2_ready = sem("conv2_ready")
        stored = sem("stored")
        XE, GF, UF, TH, AC, AF, AT, YF, YB, TF, YS = range(11)
        fast = [sem(f"fast_{n}") for n in ("window", "gate", "up", "tanh", "act", "act_turned", "actT",
                                           "down", "y", "y_turned", "yT")]
        slow = [sem(f"slow_{n}") for n in ("window", "gate", "up", "tanh", "act", "act_turned", "actT",
                                           "down", "y", "y_turned", "yT")]
        chain_e, chain_s = sem("chain_e"), sem("chain_s")
        s_loaded = sem("s_loaded")

        def v1(a, k=0):
            return vT[:, a + k:a + k + 1]

        def v2(a, k=0):
            return vT[:, NV1 + a + k:NV1 + a + k + 1]

        def attention_room(L):
            pc = ring[:, place["0pc"], :]
            return (pc[:, 0:2048].rearrange("p (t h m) -> p t h m", t=2, h=4),
                    pc[:, 2048:4096].rearrange("p (h m s) -> p h m s", h=4, m=2),
                    ring[:, place[f"{L}px"], :].rearrange("p (t h m) -> p t h m", t=2, h=4),
                    ring[:, place[f"{L}pT"], :].rearrange("p (h m s) -> p h m s", h=4, m=4))

        def full(eng, name):
            eng.wait_ge(psum_full, INDEX[name] + 1)
            return bank[INDEX[name] % 8]

        def emptied(eng, name):
            who, n = drained_by(name)
            eng.wait_ge(a_drained if who == "a" else v_drained, n)

        def weights(eng, name):
            eng.wait_ge(w_loaded[place[name]], landed[name])

        def tiles(a, pat):
            return a.rearrange(pat, p=P)

        vec1_loads, vec2_loads, r0 = [], [], 0
        for a in (tiles(t["g_mix"], "o (k p) -> (o k) p"), tiles(t["conv_b"], "o (k p) -> (o k) p"),
                  tiles(t["conv_w"], "a w o (k p) -> (a w o k) p"), tiles(t["g_xattn"], "o (k p) -> (o k) p"),
                  tiles(t["g_mem"], "o (k p) -> (o k) p"), tiles(t["g_moe"], "o (k p) -> (o k) p"),
                  tiles(t["g_final"], "(k p) -> k p"), tiles(t["g_head"], "o (k p) -> (o k) p"),
                  t["b_s"][0]):
            vec1_loads.append((raw[r0:r0 + a.shape[0], 0, :], a))
            r0 += a.shape[0]
        assert r0 == NV1
        r0 = 0
        for a in (tiles(t["norm_g_2"], "l (k p) -> (l k) p"), tiles(t["b_mod_2"], "l (k p) -> (l k) p"),
                  tiles(t["c_2"], "o (k p) -> (o k) p"), tiles(t["c_ctx_2"], "(k p) -> k p"),
                  tiles(t["conv_w_2"], "l w (k p) -> (l w k) p"), tiles(t["conv_b_2"], "l (k p) -> (l k) p"),
                  tiles(t["pool_scale_2"], "l (k p) -> (l k) p")):
            vec2_loads.append((raw[r0:r0 + a.shape[0], 1, :], a))
            r0 += a.shape[0]
        assert r0 == NV2

        def everywhere(a, shape):
            return a.unsqueeze(0).broadcast_to(shape)

        gate_loads = [(wg[:, :, :], rows(w_in, 2048, 16)), (wr[:, :, 0:NG], rows(t["w_rg"][0], 0, NG)),
                        (wr[:, :, NG:NG + NE], rows(t["w_re"][0], 0, NE))]
        misc_loads = [(gate_b[:, :], everywhere(t["gate_b"][0], [P, 16])),
                      (rb[:, 0:NG], everywhere(t["b_rg"][0], [P, NG])),
                      (rb[:, NG:NG + NE], everywhere(t["b_re"][0], [P, NE])),
                      (lng[:, :], everywhere(t["ln_v_g"][0], [P, DM])),
                      (lnb[:, :], everywhere(t["ln_v_b"][0], [P, DM])),
                      (wsr[:, :, :], t["w_s"][0].rearrange("g t s -> t g s"))]
        for L in range(2):
            for name, a, b in (("q_gain_2", 0, 4), ("k_gain_2", 4, 6)):
                misc_loads += [(gains[:, L, h_, :], everywhere(t[name][L], [P, HD2])) for h_ in range(a, b)]
        for L in range(2):
            for i in range(2):
                for hf_ in range(2):
                    c = slice(64 * hf_, 64 * hf_ + 64)
                    misc_loads.append((pwb[c, L, i, c], t["pool_w_2"][L, 2 * i + hf_]))

        block = ctx.enter_context(nc.Block())

        @block.sync
        def _(sp):
            sp.dma_start(xin, t["x"][0].rearrange("(t p) n -> p t n", p=P)).then_inc(ld_x, 16)
            sent = []

            def load(name, pieces, release):
                n = len(sent)
                if n >= SLOTS and pieces:
                    old = sent[n - SLOTS]
                    if old[0][0] in "GUD":
                        sp.wait_ge(fast[{"G": GF, "U": UF, "D": YF}[old[0][0]]], int(old[0][1:]) + 1)
                    else:
                        sp.wait_ge(psum_full, INDEX[old[1]] + 1)
                for c0, src in pieces:
                    k, m = (src.shape[1], src.shape[2]) if len(src.shape) == 3 else (1, src.shape[1])
                    dst = ring[:, place[name], c0:c0 + k * m]
                    if len(src.shape) == 3:
                        dst = dst.rearrange("p (k n) -> p k n", k=k)
                    sp.dma_start(dst, src).then_inc(w_loaded[place[name]], 16)
                sent.append((name, release))

            wsrc = {"G": t["w_gate"][0], "U": t["w_up"][0], "D": t["w_down"][0]}

            def expert(m, e):
                return wsrc[m][bass.ds(e, 1)].rearrange("a (k p) n -> p (a k) n", p=P)

            load(*before[0])
            sp.dma_start(memin, t["mem"][0].rearrange("(t p) n -> p t n", p=P)).then_inc(ld_mem, 16)
            load(*before[1])
            sp.dma_start(ctxin, t["ctx_2"][0].rearrange("(t p) n -> p t n", p=P)).then_inc(ld_ctx, 16)
            for name, pieces, release in before[2:]:
                load(name, pieces, release)
            lead = 11
            for name in experts[:lead]:
                load(name, [(0, expert(name[0], int(name[1:])))], None)
            with sp.Fori(0, (len(experts) - lead - 1) // 6) as i:
                for q, name in enumerate(experts[lead:lead + 6]):
                    m, e = name[0], int(name[1:])
                    sp.wait_ge(fast[{"G": GF, "U": UF, "D": YF}[m]], i * 2 + (e - 2 + 1))
                    k = 4 if m == "D" else 8
                    sp.dma_start(ring[:, place[name], :].rearrange("p (k n) -> p k n", k=k),
                                 expert(m, i * 2 + e)).then_inc(w_loaded[place[name]], 16)
            sent += [(name, None) for name in experts[lead:-1]]
            name = experts[-1]
            load(name, [(0, expert("D", NE - 1))], None)

            sp.wait_ge(win_ready, 2)
            rows_max = sp.value_load(mxc[0:1, 0:1], min_val=0, max_val=S)
            with sp.If(rows_max > C):
                sp.wait_ge(fast[YS], NE)
                with sp.Fori(0, NE) as e:
                    sp.wait_ge(slow[XE], e * 4 + 1)
                    for m, k in (("G", 8), ("U", 8), ("D", 4)):
                        sp.dma_start(ring[:, "GUD".index(m), :].rearrange("p (k n) -> p k n", k=k),
                                     expert(m, e)).then_inc(s_loaded, 16)
                sp.wait_ge(slow[YS], NE * 4)

            for name, pieces, release in after:
                load(name, pieces, release)

            emptied(sp, "fin3")
            sp.dma_start(t["out"][0].rearrange("(t p) n -> p t n", p=P), outb).then_inc(stored, 16)
            sp.wait_ge(stored, 16)

        @block.gpsimd
        def _(gp):
            for dst, src in vec2_loads:
                gp.dma_start(dst, src).then_inc(ld_vec2, 16)
            gp.wait_ge(v_chain, 1)
            for dst, src in misc_loads:
                gp.dma_start(dst, src).then_inc(ld_misc, 16)

        @block.tensor
        def _(pe):
            at = [0]
            last = [None]

            def group(name):
                n = at[0]
                assert ORDER[n][0] == name, (ORDER[n][0], name)
                if n >= 8 and not LOOP_AT <= n < LOOP_AT + 8:
                    emptied(pe, ORDER[n - 8][0])
                at[0] += 1
                return bank[n % 8]

            def mm(o, lhsT, rhs, start=True, stop=True):
                last[0] = pe.matmul(o, lhsT, rhs, start=start, stop=stop)

            def turn(o, a):
                last[0] = pe.transpose(o, a, ident[0:a.shape[0], 0:a.shape[0]])

            def filled():
                last[0].then_inc(psum_full, 1)

            def turn_tokens(prefix, src):
                for g in range(4):
                    b = group(f"{prefix}{g}")
                    for k in range(2):
                        for tt in range(TT):
                            kk = 2 * g + k
                            turn(b[:, k * S + tt * P:k * S + tt * P + P], src[:, tt, kk * P:kk * P + P])
                    filled()

            def norm_sum(name, sq, streams=1):
                b = group(name)
                for k in range(KT):
                    if k % 2 == 0:
                        pe.wait_ge(sq_ready, SQ_BASE[name] + k // 2 + 1)
                    rhs = sq[:, k] if streams == 1 else sq[:, :, k]
                    o = b[:, 0:S] if streams == 1 else b[:, :].rearrange("p (r s) -> p r s", r=2)
                    mm(o, ones, rhs, k == 0, k == KT - 1)
                filled()

            def tile_ready(norm, k):
                pe.wait_ge(h_ready, H_BASE[norm] + k + 1)

            def to_channels(names, w, h, norm=None):
                for g, name in enumerate(names):
                    b = group(name)
                    for j in range(2):
                        m = 2 * g + j
                        for k in range(KT):
                            if norm and m == 0:
                                tile_ready(norm, k)
                            mm(b[:, j * S:j * S + S], w[:, k, m * P:m * P + P], h[:, k], k == 0, k == KT - 1)
                    filled()

            def to_tokens(names, w, h):
                for tt, name in enumerate(names):
                    b = group(name)
                    for k in range(KT):
                        mm(b[:, :], h[:, k, tt * P:tt * P + P], w[:, k], k == 0, k == KT - 1)
                    filled()

            h = H[:, 0]
            pe.wait_ge(ld_const, 16)
            pe.wait_ge(ld_x, 16)
            turn_tokens("x", xin)
            pe.wait_ge(ld_vec1, 16 * len(vec1_loads))
            b = group("vec1")
            turn(b[:, 0:NV1], raw[0:NV1, 0, :])
            filled()
            norm_sum("ss1", h)
            weights(pe, "in0")
            to_channels(["qk0", "qk1"], slot("in0"), h, "ss1")
            pe.wait_ge(ld_mem, 16)
            turn_tokens("mem", memin)
            norm_sum("ss2", msq)
            pe.wait_ge(ld_ctx, 16)
            turn_tokens("ctx", ctxin)
            pe.wait_ge(ld_vec2, 16 * len(vec2_loads))
            b = group("vec2")
            turn(b[:, 0:NV2], raw[0:NV2, 1, :])
            filled()
            weights(pe, "in1")
            to_channels(["qk2", "qk3"], slot("in1"), h)
            pe.wait_ge(ld_gates, 16 * len(gate_loads))
            pe.wait_ge(ld_misc, 16 * len(misc_loads))
            b = group("gate")
            for tt in range(TT):
                for k in range(KT):
                    mm(b[:, tt * 16:tt * 16 + 16], h[:, k, tt * P:tt * P + P], wg[:, k, :], k == 0, k == KT - 1)
            filled()
            b = group("ws")
            for g in range(NH):
                turn(b[:, g * P:g * P + P], wsr[:, g, :])
            filled()
            for c, n in ((2, "v"), (3, "o"), (4, "gv"), (5, "gu")):
                weights(pe, f"in{c}")
                to_tokens([f"{n}0", f"{n}1"], slot(f"in{c}"), h)

            for c in range(2):
                weights(pe, f"kv{c}")
                to_channels([f"km{2 * c}", f"km{2 * c + 1}"], slot(f"kv{c}"), H[:, 1], "ss2" if c == 0 else None)
            pe.wait_ge(lf_ready, 1)
            b = group("bcum")
            lf = sm[:, 64:80]
            mm(b[:, 0:8], trf, lf[:, 0:8])
            mm(b[:, 8:16], trb, lf[:, 8:16])
            mm(b[:, 16:32], ones, lf)
            filled()
            pe.wait_ge(ap_ready, 1)
            b = group("apT")
            turn(b[0:16, 0:P], sm[:, 112:128])
            filled()
            for c in range(2):
                weights(pe, f"kv{c + 2}")
                to_tokens([f"vm{2 * c}", f"vm{2 * c + 1}"], slot(f"kv{c + 2}"), H[:, 1])
            pe.wait_ge(dmx_ready, 1)
            b = group("mxb")
            mm(b[:, 0:16], ones[0:16, :], sm[0:16, 129:145])
            filled()
            for j in range(4):
                b = group(f"A{j}")
                mm(b[:, :], ones[0:16, :], bd[:, 4 * j:4 * j + 4, :])
                filled()

            def modulation(L, c0, c1):
                def turned(c):
                    emptied(pe, f"mr{L}{c}")
                    b = group(f"mt{L}{c}")
                    for m in range(4):
                        turn(b[:, 2 * m:2 * m + 2], mrow[:, c % 2, m * P:m * P + P])
                    filled()

                pe.wait_ge(sc_ready, 1)
                for c in range(c0, c1):
                    weights(pe, f"mod{L}{c}")
                    w = slot(f"mod{L}{c}")
                    b = group(f"mr{L}{c}")
                    for k in range(KT):
                        mm(b[0:2, :], sc[:, :, k], w[:, k], k == 0, k == KT - 1)
                    filled()
                    if c:
                        turned(c - 1)
                if c1 == 6:
                    turned(5)

            modulation(0, 0, MOD0_SPLIT)

            pe.wait_ge(qk_ready, 1)
            for d in range(2):
                b = group(f"KT{d}")
                for hh in range(NH):
                    turn(b[:, hh * P:hh * P + P], qkT[:, 4 + hh, d * P:d * P + P])
                filled()
            for tt in range(TT):
                b = group(f"QK{tt}")
                for hh in range(NH):
                    mm(b[:, hh * P:hh * P + P], qkT[:, hh, tt * P:tt * P + P],
                       qkT[:, 4 + hh, tt * P:tt * P + P])
                filled()
            emptied(pe, "KT1")
            emptied(pe, "v1")
            for d in range(2):
                b = group(f"C{d}")
                for hh in range(NH):
                    mm(b[:, hh * P:hh * P + P], kw[:, d, hh, :], vs[:, d, hh * P:hh * P + P])
                filled()
            b = group("nn")
            for d in range(2):
                for hh in range(NH):
                    mm(b[:, d * 4 + hh:d * 4 + hh + 1], kw[:, d, hh, :], ones[:, 0:1])
            filled()
            pe.wait_ge(gvn_ready, 1)
            emptied(pe, "ws")
            for tt in range(TT):
                b = group(f"SP{tt}")
                for g in range(NH):
                    mm(b[:, g * P:g * P + P], wsT[:, g, :], gv[:, tt, g * P:g * P + P])
                filled()
            pe.wait_ge(w_ready, 1)
            for j in range(4):
                b = group(f"WT{j}")
                for hh in range(NH):
                    turn(b[:, hh * P:hh * P + P], W[:, 4 * j + hh, :])
                filled()
            emptied(pe, "nn")
            b = group("dI")
            for d in range(2):
                for hh in range(NH):
                    mm(b[:, d * 4 + hh:d * 4 + hh + 1], qkT[:, hh, (1 - d) * P:(2 - d) * P],
                       sm[:, 240 + d * 4 + hh:241 + d * 4 + hh])
            filled()
            for j in range(4):
                emptied(pe, f"WT{j}")
                b = group(f"NI{j}")
                for hh in range(NH):
                    mm(b[:, hh * P:hh * P + P], WT[:, 4 * j + hh, :], vs[:, j % 2, hh * P:hh * P + P])
                filled()
            emptied(pe, "C1")
            for d in range(2):
                b = group(f"CI{d}")
                for hh in range(NH):
                    mm(b[:, hh * P:hh * P + P], qkT[:, hh, (1 - d) * P:(2 - d) * P], Cs[:, d, hh, :])
                filled()
            modulation(0, MOD0_SPLIT, 6)
            pe.wait_ge(y_ready, 1)
            emptied(pe, "SP1")
            for g in range(4):
                b = group(f"yT{g}")
                for j in range(2):
                    for tt in range(TT):
                        src = (tho if g < 2 else gu)[:, tt, ((2 * g + j) % 4) * P:((2 * g + j) % 4) * P + P]
                        turn(b[:, j * S + tt * P:j * S + tt * P + P], src)
                filled()
            emptied(pe, "yT3")
            for c in range(2):
                weights(pe, f"wout{c}")
                to_channels([f"wo{2 * c}", f"wo{2 * c + 1}"], slot(f"wout{c}"), yT)

            norm_sum("ss3", H[:, 0])
            for c in range(2):
                weights(pe, f"wq{c}")
                to_channels([f"xq{2 * c}", f"xq{2 * c + 1}"], slot(f"wq{c}"), H[:, 0],
                            "ss3" if c == 0 else None)
            emptied(pe, "xq3")
            emptied(pe, "vm3")
            for g in range(4):
                hp, tt = divmod(g, 2)
                b = group(f"S{g}")
                for j in range(2):
                    for k in range(2):
                        kk = 2 * (2 * hp + j) + k
                        mm(b[:, j * S:j * S + S], xqT[:, kk, tt * P:tt * P + P], kmT[:, kk, :], k == 0, k == 1)
                filled()
            modulation(1, 0, MOD1_SPLIT[0])
            for hh in range(NH):
                pe.wait_ge(pn_ready, 2 * (hh // 2 + 1))
                b = group(f"pT{hh}")
                for m in range(2):
                    for tt in range(TT):
                        turn(b[:, m * S + tt * P:m * S + tt * P + P], px[:, tt, hh, m * P:m * P + P])
                filled()
            for hh in range(NH):
                emptied(pe, f"pT{hh}")
                b = group(f"xo{hh}")
                for j in range(2):
                    for m in range(2):
                        c0 = hh * 256 + j * P
                        mm(b[:, j * S:j * S + S], vm[:, m, c0:c0 + P], pTx[:, hh, m, :], m == 0, m == 1)
                filled()
            emptied(pe, "xo3")
            for c in range(2):
                weights(pe, f"wox{c}")
                to_channels([f"xw{2 * c}", f"xw{2 * c + 1}"], slot(f"wox{c}"), oTx)

            norm_sum("ss4", H[:, 0])
            b = group("lg")
            for tt in range(TT):
                for k in range(KT):
                    if tt == 0:
                        tile_ready("ss4", k)
                    mm(b[:, tt * 36:tt * 36 + 36], H[:, 0, k, tt * P:tt * P + P], wr[:, k, :],
                       k == 0, k == KT - 1)
            filled()
            for g in range(4):
                tt, half = divmod(g, 2)
                b = group(f"hk{g}")
                for j in range(4):
                    turn(b[:, j * P:j * P + P], H[:, 0, 4 * half + j, tt * P:tt * P + P])
                filled()
            modulation(1, *MOD1_SPLIT)
            pe.wait_ge(A_ready, 1)
            b = group("pos")
            As = sm[:, 320:384].rearrange("p (t e) -> p t e", t=2)
            mm(b[:, 0:32], trs, As[:, 0, :])
            mm(b[:, 32:64], ones, As[:, 0, :], True, False)
            mm(b[:, 32:64], trs, As[:, 1, :], False, True)
            mm(b[:, 64:96], ones, As[:, 0, :], True, False)
            mm(b[:, 64:96], ones, As[:, 1, :], False, True)
            mm(b[0:32, 96:97], As[:, 0, :], ones[:, 0:1], True, False)
            mm(b[0:32, 96:97], As[:, 1, :], ones[:, 0:1], False, True)
            filled()
            pe.wait_ge(cnt_ready, 1)
            b = group("start")
            mm(b[:, 0:32], sm[0:32, 1000:1128], trs[0:32, 0:32])
            filled()
            pe.wait_ge(csq_ready, 1)
            b = group("css")
            for k in range(KT):
                mm(b[:, 0:S], ones, H[:, 1, k], k == 0, k == KT - 1)
            filled()
            modulation(1, MOD1_SPLIT[1], 6)
            pe.wait_ge(P_ready, 1)
            emptied(pe, "hk3")
            for k in range(KT):
                b = group(f"xs{k}")
                for tt in range(TT):
                    mm(b[:, :], hk[:, tt, k * P:k * P + P], Pm[:, tt, :], tt == 0, tt == 1)
                filled()
            emptied(pe, "xs7")
            emptied(pe, "start")

            def project(bk, w, x, done, before_last=None):
                for k in range(KT):
                    if before_last and k == KT - 1:
                        before_last()
                    m = pe.matmul(bk[0:C, :], x[:, k, :], w[:, k], start=(k == 0), stop=(k == KT - 1))
                m.then_inc(done, 1)

            def hold():
                pe.matmul(bank[4][:, 0:1], ident, ones[:, 0:1], start=True, stop=True)

            def turn_act(s, j):
                for k in range(4):
                    m = pe.transpose(bank[4][:, k * C:k * C + C], ac[:, j, k * P:k * P + P], ident[0:C, 0:C])
                m.then_inc(s[AF], 1)

            def down(s, w, j):
                for half in range(2):
                    for k in range(4):
                        m = pe.matmul(bank[5 + half][0:C, :], acT[:, j, k, :], w[:, k, half * 512:half * 512 + 512],
                                      start=(k == 0), stop=(k == 3))
                m.then_inc(s[YF], 1)

            def turn_down(s, j):
                for k in range(KT):
                    m = pe.transpose(bank[7][:, k * C:k * C + C], yb[:, j, k * P:k * P + P], ident[0:C, 0:C])
                m.then_inc(s[TF], 1)

            def expert_step(e, parity, gname, uname, dname, more, has):
                gate, act1, out2, up, down1 = has

                def turns_ready():
                    if down1:
                        pe.wait_ge(fast[AC], e)
                        if act1 == "wait":
                            pe.wait_ge(fast[AT], e - 1)
                    if out2:
                        pe.wait_ge(fast[YB], e - 1)
                        if out2 == "wait":
                            pe.wait_ge(fast[YS], e - 2)

                if gate:
                    pe.wait_ge(fast[XE], e + 1)
                    if act1 == "wait":
                        pe.wait_ge(fast[AC], e - 1)
                    pe.wait_ge(w_loaded[place[gname]], landed[gname] + more)
                    project(bank[parity], slot(gname), xe[:, parity], fast[GF], turns_ready)
                else:
                    turns_ready()
                if down1:
                    turn_act(fast, 1 - parity)
                if out2:
                    turn_down(fast, parity)
                if up:
                    pe.wait_ge(w_loaded[place[uname]], landed[uname] + more)
                    project(bank[2 + parity], slot(uname), xe[:, parity], fast[UF])
                if down1:
                    pe.wait_ge(fast[AT], e)
                    if act1 == "wait":
                        pe.wait_ge(fast[YB], e - 1)
                    pe.wait_ge(w_loaded[place[dname]], landed[dname] + more)
                    down(fast, slot(dname, 4, 1024), 1 - parity)

            expert_step(0, 0, "G0", "U0", None, 0, (True, "none", False, True, False))
            expert_step(1, 1, "G1", "U1", "D0", 0, (True, "none", False, True, True))
            expert_step(2, 0, "G2", "U2", "D1", 0, (True, "wait", True, True, True))
            expert_step(3, 1, "G3", "U3", "D2", 0, (True, "wait", "wait", True, True))
            with pe.Fori(0, (NE - 4) // 2) as i:
                for j in range(2):
                    expert_step(i * 2 + (4 + j), j, f"G{4 + j}", f"U{4 + j}", f"D{3 + j}", i * 16,
                                (True, "wait", "wait", True, True))
            expert_step(NE, 0, None, None, f"D{NE - 1}", 0, (False, "wait", "wait", False, True))
            expert_step(NE + 1, 1, None, None, None, 0, (False, "wait", "wait", False, False))

            pe.wait_ge(win_ready, 2)
            rows_max = pe.value_load(mxc[0:1, 0:1], min_val=0, max_val=S)
            with pe.If(rows_max > C):
                with pe.Fori(0, NE) as e:
                    for q in range(4):
                        pe.wait_ge(slow[XE], e * 4 + (q + 1))
                        if q == 0:
                            pe.wait_ge(s_loaded, e * 48 + 48)
                        project(bank[0], ring[:, 0, :].rearrange("p (k n) -> p k n", k=8), xe[:, 0], slow[GF])
                        project(bank[2], ring[:, 1, :].rearrange("p (k n) -> p k n", k=8), xe[:, 0], slow[UF])
                        pe.wait_ge(slow[AC], e * 4 + (q + 1))
                        hold()
                        turn_act(slow, 0)
                        pe.wait_ge(slow[AT], e * 4 + (q + 1))
                        down(slow, ring[:, 2, :].rearrange("p (k n) -> p k n", k=4), 0)
                        pe.wait_ge(slow[YB], e * 4 + (q + 1))
                        hold()
                        turn_down(slow, 0)
                pe.wait_ge(slow[YS], NE * 4)

            pe.wait_ge(fast[YS], NE)
            for g in range(2):
                b = group(f"pw{g}")
                for j in range(2):
                    for tt in range(TT):
                        turn(b[:, j * S + tt * P:j * S + tt * P + P], Pw[:, tt, (2 * g + j) * P:(2 * g + j) * P + P])
                filled()
            for g in range(8):
                st, half = divmod(g, 2)
                b = group(f"yt{g}")
                for j in range(4):
                    turn(b[:, j * P:j * P + P], ys[:, 4 * half + j, st * P:st * P + P])
                filled()
            emptied(pe, "pw1")
            emptied(pe, "yt6")
            emptied(pe, "yt7")
            for g in range(4):
                b = group(f"co{g}")
                for j in range(2):
                    for a in range(4):
                        kk = 2 * g + j
                        mm(b[:, j * S:j * S + S], yk[:, a, kk * P:kk * P + P], PwT[:, a, :], a == 0, a == 3)
                filled()
            norm_sum("ss5", H[:, 0])

            for L in range(2):
                R = 2 - L
                pc2, pcT2, px2, pT2 = attention_room(L)
                def wide(name, w, m):
                    b = group(f"{L}{name}")
                    for k in range(KT):
                        if R == 2:
                            mm(b[:, :].rearrange("p (r s) -> p r s", r=2), w[:, k, m * P:m * P + P],
                               H[:, :, k], k == 0, k == KT - 1)
                        else:
                            mm(b[:, 0:S], w[:, k, m * P:m * P + P], H[:, 0, k], k == 0, k == KT - 1)
                    filled()

                def tokens2(name, w):
                    for r in range(R):
                        b = group(f"{L}{name}{r}")
                        for tt in range(TT):
                            for k in range(KT):
                                mm(b[:, tt * W2:tt * W2 + W2], H[:, r, k, tt * P:tt * P + P], w[:, k, :],
                                   k == 0, k == KT - 1)
                        filled()

                weights(pe, f"{L}in0")
                w = slot(f"{L}in0")

                def qkv_columns(r, tt, waits):
                    c0 = 256 if L == 1 and r == 1 else 0
                    b = group(f"{L}qkv{2 * r + tt}")
                    for k in range(KT):
                        if waits:
                            pe.wait_ge(h_ready, H_BASE[f"{L}ss"] + 8 * r + k + 1)
                        mm(b[:, c0:512], H[:, r, k, tt * P:tt * P + P], w[:, k, c0:512], k == 0, k == KT - 1)
                    filled()

                if L == 0:
                    pe.wait_ge(ctx_ready, 1)
                    qkv_columns(1, 0, False)
                    norm_sum("0ss", H[:, 0])
                    qkv_columns(1, 1, False)
                    qkv_columns(0, 0, True)
                    qkv_columns(0, 1, False)
                else:
                    norm_sum("1ss", H, 2)
                    for r in range(2):
                        qkv_columns(r, 0, True)
                        qkv_columns(r, 1, False)
                weights(pe, f"{L}in1")
                w = slot(f"{L}in1")
                wide("za0", w, 0)
                wide("za1", w, 1)
                tokens2("uf", w[:, :, 256:512])
                weights(pe, f"{L}in2")
                w = slot(f"{L}in2")
                for i, n in enumerate(("zf0", "zf1", "b0", "b1")):
                    wide(n, w, i)
                weights(pe, f"{L}in3")
                w = slot(f"{L}in3")
                for i, n in enumerate(("c0", "c1", "h0", "h1")):
                    wide(n, w, i)
                weights(pe, f"{L}in4")
                w = slot(f"{L}in4")
                wide("zc0", w, 0)
                wide("zc1", w, 1)
                tokens2("up", w[:, :, 256:512])
                weights(pe, f"{L}in5")
                w = slot(f"{L}in5", KT, 256)
                wide("zp0", w, 0)
                wide("zp1", w, 1)

                pe.wait_ge(rope_ready, L + 1)
                for hh in range(6):
                    b = group(f"{L}hT{hh}")
                    for tt in range(4):
                        if hh < 4 and tt >= 2 * R:
                            continue
                        turn(b[0:HD2, tt * P:tt * P + P], qkv[:, tt, hh * HD2:hh * HD2 + HD2])
                    filled()
                emptied(pe, f"{L}hT5")
                if L == 0:
                    for g in range(4):
                        hp, tt = divmod(g, 2)
                        b = group(f"{L}cS{g}")
                        for j in range(2):
                            mm(b[:, j * S:j * S + S], q2T[:, 2 * hp + j, S + tt * P:S + tt * P + P],
                               q2T[:, 4 + hp, S:2 * S])
                        filled()
                for g in range(8):
                    hh, tt = divmod(g, 2)
                    b = group(f"{L}xS{g}")
                    mm(b[:, :], q2T[:, hh, tt * P:tt * P + P], q2T[:, 4 + hh // 2, :])
                    filled()
                weights(pe, f"{L}const")
                cc = ring[:, place[f"{L}const"], :]
                dft = cc[:, DFT0:DFT0 + 1024].rearrange("p (t n) -> p t n", t=2)
                pool = cc[:, POOL0:POOL0 + 2048].rearrange("p (t i s) -> p t i s", t=2, i=4)
                wf = cc[:, WF0:WF0 + 512].rearrange("p (k n) -> p k n", k=2)
                for r in range(R):
                    emptied(pe, f"{L}uf{r}")
                    for i in range(2):
                        b = group(f"{L}B{r}{i}")
                        for tt in range(TT):
                            mm(b[:, :], uf[:, 2 * r + tt, i * P:i * P + P], dft[:, tt, :], tt == 0, tt == 1)
                        filled()
                emptied(pe, f"{L}up{R - 1}")
                for i in range(2):
                    b = group(f"{L}dT{i}")
                    for half in range(2):
                        g = 2 * i + half
                        for r in range(R):
                            for tt in range(TT):
                                mm(b[half * 64:half * 64 + 64, r * S:r * S + S],
                                   up[:, 2 * r + tt, g * 64:g * 64 + 64], pool[:, tt, g, :], tt == 0, tt == 1)
                    filled()
                emptied(pe, f"{L}B{R - 1}1")
                for i in range(2):
                    b = group(f"{L}yf{i}")
                    for r in range(R):
                        mm(b[:, r * S:r * S + S], cc[:, CD0:CD0 + P], B2[:, r, i, 0:S], True, False)
                        mm(b[:, r * S:r * S + S], cc[:, CD0 + P:CD0 + 2 * P], B2[:, r, i, S:2 * S], False, True)
                    filled()

                def both(b):
                    return b[:, 0:R * S]

                for i in range(2):
                    emptied(pe, f"{L}dT{i}")
                    b = group(f"{L}pl{i}")
                    mm(both(b), pwb[:, L, i, :], dT2[:, i, 0:R].rearrange("p r s -> p (r s)"))
                    filled()
                emptied(pe, f"{L}yf1")
                for i in range(2):
                    b = group(f"{L}wf{i}")
                    for k in range(2):
                        mm(both(b), wf[:, k, i * P:i * P + P], yf2[:, k, 0:R].rearrange("p r s -> p (r s)"),
                           k == 0, k == 1)
                    filled()

                if L == 0:
                    for hh in range(NH):
                        pe.wait_ge(pn_ready, 4 + 2 * (hh // 2 + 1))
                        b = group(f"{L}cP{hh}")
                        for m in range(2):
                            for tt in range(TT):
                                turn(b[:, m * S + tt * P:m * S + tt * P + P], pc2[:, tt, hh, m * P:m * P + P])
                        filled()
                    emptied(pe, f"{L}cP3")
                    for i in range(2):
                        b = group(f"{L}co{i}")
                        for j in range(2):
                            for m in range(2):
                                mm(b[j * 64:j * 64 + 64, 0:S], qkv[:, 2 + m, 384 + i * 64:384 + i * 64 + 64],
                                   pcT2[:, 2 * i + j, m, :], m == 0, m == 1)
                        filled()
                for g in range(8):
                    hh, mp = divmod(g, 2)
                    pe.wait_ge(pn_ready, 8 + 8 * L + 2 * (hh + 1))
                    b = group(f"{L}xP{g}")
                    for m in range(2):
                        for tt in range(TT):
                            mk = 2 * mp + m
                            turn(b[:, m * S + tt * P:m * S + tt * P + P], px2[:, tt, hh, mk * P:mk * P + P])
                    filled()
                emptied(pe, f"{L}xP7")
                for i in range(2):
                    b = group(f"{L}xo{i}")
                    for j in range(2):
                        for m in range(4):
                            mm(b[j * 64:j * 64 + 64, 0:S], qkv[:, m, 384 + i * 64:384 + i * 64 + 64],
                               pT2[:, 2 * i + j, m, :], m == 0, m == 3)
                    filled()
                pe.wait_ge(conv2_ready, L + 1)
                emptied(pe, f"{L}xo1")
                for c in range(2):
                    weights(pe, f"{L}wout{c}")
                    w = slot(f"{L}wout{c}")
                    for m in range(4):
                        b = group(f"{L}out{4 * c + m}")
                        for k in range(KT):
                            mm(both(b), w[:, k, m * P:m * P + P], oT[:, k, 0:R].rearrange("p r s -> p (r s)"),
                               k == 0, k == KT - 1)
                        filled()
            emptied(pe, "1out7")
            for g in range(4):
                tt, half = divmod(g, 2)
                b = group(f"fin{g}")
                for j in range(4):
                    turn(b[:, j * P:j * P + P], X[:, 0, 4 * half + j, tt * P:tt * P + P])
                filled()
            assert at[0] == len(ORDER)

        @block.scalar
        def _(act):
            n = [0]

            def link(ins):
                n[0] += 1
                ins.then_inc(a_chain, 1)
                act.wait_ge(a_chain, n[0])

            act.dma_start(c1[:, :], t["const1"]).then_inc(ld_const, 16)
            for dst, src in vec1_loads:
                act.dma_start(dst, src).then_inc(ld_vec1, 16)
            for dst, src in gate_loads:
                act.dma_start(dst, src).then_inc(ld_gates, 16)

            def take(name, dst, src=None, func=ACT.Copy, **kw):
                b = full(act, name)
                src = b[:, :] if src is None else src(b)
                act.activation(dst, src, func, **kw).then_inc(a_drained, 1)

            def flat(v):
                return v.rearrange("p a b -> p (a b)")

            def root(name, n=S):
                if H_BASE[name]:
                    act.wait_ge(h_ready, H_BASE[name])
                take(name, flat(sd)[:, 0:n], lambda b: b[:, 0:n], ACT.Sqrt, scale=1.0 / D, bias=eps[:, 0:1])

            eps, eps_ln = sm[:, 1190:1191], sm[:, 1191:1192]
            def take_qk(g):
                take(f"qk{g}", qkp[:, 2 * g:2 * g + 2, 2:2 + S], lambda b: b[:, :].rearrange("p (k s) -> p k s", k=2))

            for g in range(4):
                take(f"x{g}", flat(X[:, 0, 2 * g:2 * g + 2]))
            act.wait_ge(v_chain, 4)
            root("ss1")
            take_qk(0)
            take_qk(1)
            for g in range(4):
                take(f"mem{g}", flat(H[:, 1, 2 * g:2 * g + 2]))
            root("ss2")
            for g in range(4):
                take(f"ctx{g}", flat(X[:, 1, 2 * g:2 * g + 2]))
            take_qk(2)
            take_qk(3)
            take("ws", flat(wsT))
            for tt in range(TT):
                take(f"v{tt}", vs[:, tt, :])
            for tt in range(TT):
                take(f"o{tt}", tho[:, tt, :], None, ACT.Tanh, scale=0.5)
            for tt in range(TT):
                take(f"gv{tt}", gv[:, tt, :], None, ACT.Gelu_apprx_tanh)
            for tt in range(TT):
                take(f"gu{tt}", gu[:, tt, :], None, ACT.Gelu_apprx_tanh)
            emptied(act, "vec2")
            act.activation(flat(sc), vT[:, NV1 + V_C:NV1 + V_C + 16], ACT.Silu).then_inc(sc_ready, 1)
            act.wait_ge(nf_ready, 1)
            link(act.activation(sm[:, 80:96], sm[:, 32:48], ACT.Exp, scale=-1.0))
            act.activation(sm[:, 96:112], sm[:, 80:96], ACT.Ln, bias=1.0).then_inc(lse_ready, 1)
            act.wait_ge(gvc_ready, 1)
            for tt in range(TT):
                ins = act.activation(Ej[:, tt], gv[:, tt, :], ACT.Square, accum_out=sm[:, 264 + tt:265 + tt])
            ins.then_inc(gvs_ready, 1)
            act.wait_ge(gvs_ready, 1)
            act.activation(sm[:, 266:268], sm[:, 264:266], ACT.Sqrt, scale=1.0 / DM, bias=eps_ln)\
                .then_inc(gvs_ready, 1)
            for g in range(4):
                take(f"km{g}", flat(kmT[:, 2 * g:2 * g + 2]))
            for g in range(4):
                c, tt = divmod(g, 2)
                take(f"vm{g}", vm[:, tt, c * 512:c * 512 + 512])
            def take_modulation(L, c0, c1):
                for name in modulation_groups(L, c0, c1):
                    c = int(name[3])
                    if name[1] == "r":
                        if c >= 2:
                            full(act, f"mt{L}{c - 2}")
                        take(name, mrow[:, c % 2, :], lambda b: b[0:2, :])
                    else:
                        take(name, modr[:, L, 8 * c:8 * c + 8], lambda b: b[:, 0:8])

            act.wait_ge(conv_ready, 40)
            act.activation(qkT[:, :, :], qkT[:, :, :], ACT.Silu).then_inc(qk_ready, 1)
            act.wait_ge(ei_ready, 1)
            act.activation(sm[:, 184:224], sm[:, 144:184], ACT.Exp).then_inc(ee_ready, 1)
            act.wait_ge(em_ready, 1)
            act.activation(E[:, :, :], E[:, :, :], ACT.Exp).then_inc(e_ready, 1)
            take_modulation(0, 0, MOD0_SPLIT)
            for d in range(2):
                take(f"C{d}", Cs[:, d].rearrange("p h s -> p (h s)"))
            for j in range(4):
                take(f"WT{j}", flat(WT[:, 4 * j:4 * j + 4, :]))
            act.wait_ge(hss_ready, 1)
            act.activation(sm[:, 280:288], sm[:, 272:280], ACT.Sqrt, scale=1.0 / 128, bias=eps)\
                .then_inc(hsd_ready, 1)
            take_modulation(0, MOD0_SPLIT, 6)
            root("ss3")
            for g in range(4):
                take(f"xq{g}", flat(xqT[:, 2 * g:2 * g + 2]))

            def softmax_exp(names, heads, p, width, base, col):
                for g, name in enumerate(names):
                    b = full(act, name)
                    act.wait_ge(mx_ready, base + g + 1)
                    for j in range(heads):
                        tt, hh = g % TT, heads * (g // TT) + j
                        ins = act.activation(p[:, tt, hh, :], b[:, j * width:j * width + width], ACT.Exp,
                                             scale=col[2], bias=sm[:, col[0] + 4 * tt + hh:col[0] + 4 * tt + hh + 1],
                                             accum_out=sm[:, col[1] + 4 * tt + hh:col[1] + 4 * tt + hh + 1])
                        if j == heads - 1:
                            ins.then_inc(a_drained, 1)

            softmax_exp([f"S{g}" for g in range(4)], 2, px, 256, 0, (288, 296, X_SCALE))
            take_modulation(1, 0, MOD1_SPLIT[0])
            for hh in range(NH):
                take(f"pT{hh}", pTx[:, hh].rearrange("p m s -> p (m s)"))
            for hh in range(NH):
                take(f"xo{hh}", flat(oTx[:, 2 * hh:2 * hh + 2]))
            root("ss4")
            for g in range(4):
                tt, half = divmod(g, 2)
                take(f"hk{g}", hk[:, tt, half * 512:half * 512 + 512])
            act.activation(H[:, 1], X[:, 1], ACT.Square).then_inc(csq_ready, 1)
            act.wait_ge(ge_ready, 1)
            act.activation(sm[:, 472:480], sm[:, 464:472], ACT.Exp).then_inc(ge_exp, 1)
            act.wait_ge(me_ready, 1)
            act.activation(sm[:, 484:486], sm[:, 482:484], ACT.Exp).then_inc(me_exp, 1)
            take_modulation(1, *MOD1_SPLIT)
            take("css", sd[:, 1], lambda b: b[:, 0:S], ACT.Sqrt, scale=1.0 / D, bias=eps[:, 0:1])
            take_modulation(1, MOD1_SPLIT[1], 6)
            for k in range(KT):
                take(f"xs{k}", xs[:, k, 0:A])

            def window(s, x, w0, done):
                act.activation(x, xs[:, :, bass.ds(w0, C)], ACT.Copy).then_inc(s[XE], 1)

            act.wait_ge(win_ready, 2)

            def starts_at(e, q):
                return act.value_load(win[0:1, bass.ds(e + q * NE, 1)], min_val=0, max_val=A)

            def scalar_step(e, parity, has):
                rows1, gate, act1, out2 = has
                if rows1:
                    w0 = starts_at(e + 1, 0)
                    if rows1 == "wait":
                        act.wait_ge(fast[UF], e)
                    window(fast, xe[:, 1 - parity], w0, None)
                if gate:
                    act.wait_ge(fast[GF], e + 1)
                    if gate == "wait":
                        act.wait_ge(fast[AC], e - 1)
                    act.activation(th[:, parity], bank[parity][0:C, :], ACT.Tanh, scale=0.5).then_inc(fast[TH], 1)
                if act1:
                    act.wait_ge(fast[AF], e)
                    if act1 == "wait":
                        act.wait_ge(fast[YF], e - 2)
                    act.activation(acT[:, 1 - parity].rearrange("p k c -> p (k c)"), bank[4][:, 0:4 * C],
                                   ACT.Copy).then_inc(fast[AT], 1)
                if out2:
                    w0 = starts_at(e - 2, 0)
                    act.wait_ge(fast[TF], e - 1)
                    if out2 == "wait":
                        act.wait_ge(fast[YS], e - 2)
                    act.activation(ys[:, :, bass.ds(w0, C)], bank[7][:, :].rearrange("p (k c) -> p k c", k=KT),
                                   ACT.Copy).then_inc(fast[YS], 1)

            w0 = starts_at(0, 0)
            for k in range(KT):
                if k == KT - 1:
                    emptied(act, "xs7")
            window(fast, xe[:, 0], w0, None)
            scalar_step(0, 0, (True, True, False, False))
            scalar_step(1, 1, ("wait", True, True, False))
            scalar_step(2, 0, ("wait", "wait", True, True))
            scalar_step(3, 1, ("wait", "wait", "wait", "wait"))
            with act.Fori(0, (NE - 4) // 2 - 1) as i:
                for j in range(2):
                    scalar_step(i * 2 + (4 + j), j, ("wait", "wait", "wait", "wait"))
            scalar_step(NE - 2, 0, ("wait", "wait", "wait", "wait"))
            scalar_step(NE - 1, 1, (False, "wait", "wait", "wait"))
            scalar_step(NE, 0, (False, False, "wait", "wait"))
            scalar_step(NE + 1, 1, (False, False, False, "wait"))

            rows_max = act.value_load(mxc[0:1, 0:1], min_val=0, max_val=S)
            with act.If(rows_max > C):
                act.wait_ge(fast[YS], NE)
                with act.Fori(0, NE) as e:
                    for q in range(4):
                        w0 = starts_at(e, q)
                        window(slow, xe[:, 0], w0, None)
                        act.wait_ge(slow[GF], e * 4 + (q + 1))
                        act.activation(th[:, 0], bank[0][0:C, :], ACT.Tanh, scale=0.5).then_inc(slow[TH], 1)
                        act.wait_ge(slow[AF], e * 4 + (q + 1))
                        act.activation(acT[:, 0].rearrange("p k c -> p (k c)"), bank[4][:, 0:4 * C],
                                       ACT.Copy).then_inc(slow[AT], 1)
                        act.wait_ge(slow[TF], e * 4 + (q + 1))
                        act.activation(ys[:, :, bass.ds(w0, C)], bank[7][:, :].rearrange("p (k c) -> p k c", k=KT),
                                       ACT.Copy).then_inc(slow[YS], 1)
                        act.wait_ge(slow[YS], e * 4 + (q + 1))

            for g in range(2):
                take(f"pw{g}", flat(PwT[:, 2 * g:2 * g + 2]))
            for g in range(1, 8, 2):
                st, half = divmod(g, 2)
                if g == 1:
                    act.wait_ge(fast[YS], NE)
                take(f"yt{g}", yk[:, st, half * 512:half * 512 + 512])
            root("ss5")

            for L in range(2):
                R = 2 - L

                def half(b):
                    return b[:, 0:R * S]

                def two(v):
                    return v.rearrange("p r s -> p (r s)")

                pc2, pcT2, px2, pT2 = attention_room(L)

                def take_qkv(tt):
                    c0 = 256 if L == 1 and tt >= 2 else 0
                    take(f"{L}qkv{tt}", qkv[:, tt, c0:512], lambda b: b[:, c0:512])

                if L == 0:
                    take_qkv(2)
                    root("0ss")
                    for tt in (3, 0, 1):
                        take_qkv(tt)
                else:
                    root("1ss", 2 * S)
                    for tt in range(4):
                        take_qkv(tt)
                for i in range(2):
                    take(f"{L}za{i}", two(oT[:, 2 + i, 0:R]), half, ACT.Silu)
                for r in range(R):
                    take(f"{L}uf{r}", flat(uf[:, 2 * r:2 * r + 2]))
                for i in range(2):
                    take(f"{L}zf{i}", two(oT[:, i, 0:R]), half, ACT.Silu)
                act.wait_ge(qs_ready, L + 1)
                act.activation(sm[:, 624:648], sm[:, 600:624], ACT.Sqrt, scale=1.0 / HD2, bias=eps)\
                    .then_inc(qd_ready, 1)
                for n_, dst in (("b", bs2), ("c", cs2)):
                    for i in range(2):
                        take(f"{L}{n_}{i}", two(dst[:, i, 0:R]), half)
                for i in range(2):
                    take(f"{L}zc{i}", two(oT[:, 4 + i, 0:R]), half, ACT.Silu)
                for r in range(R):
                    take(f"{L}up{r}", flat(up[:, 2 * r:2 * r + 2]))
                for i in range(2):
                    take(f"{L}zp{i}", two(oT[:, 6 + i, 0:R]), half, ACT.Silu)
                for hh in range(6):
                    n_ = R * S if hh < 4 else 2 * S
                    take(f"{L}hT{hh}", q2T[:, hh, 0:n_], lambda b: b[0:HD2, 0:n_])
                if L == 0:
                    softmax_exp([f"0cS{g}" for g in range(4)], 2, pc2, 256, 4, (680, 688, A_SCALE))
                softmax_exp([f"{L}xS{g}" for g in range(8)], 1, px2, 512, 8 + 8 * L, (700, 708, A_SCALE))
                for r in range(R):
                    for i in range(2):
                        take(f"{L}B{r}{i}", B2[:, r, i, :])
                for i in range(2):
                    take(f"{L}dT{i}", two(dT2[:, i, 0:R]), half)
                for i in range(2):
                    take(f"{L}yf{i}", two(yf2[:, i, 0:R]), half)
                if L == 0:
                    for hh in range(NH):
                        take(f"0cP{hh}", pcT2[:, hh].rearrange("p m s -> p (m s)"))
                for g in range(8):
                    hh, mp = divmod(g, 2)
                    take(f"{L}xP{g}", pT2[:, hh, 2 * mp:2 * mp + 2].rearrange("p m s -> p (m s)"))
            for g in range(4):
                tt, half_ = divmod(g, 2)
                take(f"fin{g}", outb[:, tt, half_ * 512:half_ * 512 + 512])

        @block.vector
        def _(dve):
            n = [0]

            def link(ins):
                n[0] += 1
                ins.then_inc(v_chain, 1)
                dve.wait_ge(v_chain, n[0])

            def tail(ins, s):
                tails[id(s)] = tails.get(id(s), 0) + 1
                ins.then_inc(s, 1)
                dve.wait_ge(s, tails[id(s)])

            tails = {}

            def taken(ins):
                taken_n[0] += 1
                ins.then_inc(v_drained, 1)
                dve.wait_ge(v_drained, taken_n[0])

            taken_n = [0]

            def over(v, shape, axis):
                return v.unsqueeze(axis).broadcast_to(shape)

            def tt_(o, a, b, op):
                return dve.tensor_tensor(o, a, b, op)

            def ts_(o, a, s1, s2=None, op0=ALU.mult, op1=None):
                if s2 is None:
                    return dve.tensor_scalar(o, a, s1, None, op0)
                return dve.tensor_scalar(o, a, s1, s2, op0, op1)

            def stt(o, a, s, b, op0, op1):
                return dve.scalar_tensor_tensor(out=o, in0=a, scalar=s, in1=b, op0=op0, op1=op1)

            link(dve.memset(pwb[:, :, :, :], 0.0))
            link(dve.memset(sm[:, :], 0.0))
            link(dve.memset(sm[:, 1190:1191], RMS_EPS))
            link(dve.memset(sm[:, 1191:1192], LN_EPS))
            link(dve.memset(qkp[:, :, 0:2], 0.0))
            link(dve.memset(qkp[:, :, 2 + S:4 + S], 0.0))

            def squares(src, dst):
                tt_(dst, src, src, ALU.mult).then_inc(sq_ready, 1)

            def inverse_root(name, n=S):
                emptied(dve, name)
                link(dve.reciprocal(rs[:, :, :].rearrange("p r s -> p (r s)")[:, 0:n],
                                    sd[:, :, :].rearrange("p r s -> p (r s)")[:, 0:n]))

            def norm(name, src, dst, gain):
                inverse_root(name)
                for k in range(KT):
                    stt(dst[:, k], src[:, k], gain(k), rs[:, 0, :], ALU.mult, ALU.mult).then_inc(h_ready, 1)
                dve.wait_ge(h_ready, H_BASE[name] + KT)

            def modulation(L):
                emptied(dve, f"mt{L}5")
                o = V_BMOD + NV1 + 24 * L
                link(tt_(mod[:, L], modr[:, L].rearrange("p (m r) -> p m r", r=2),
                         over(vT[:, o:o + 24], [P, 24, 2], 2), ALU.add))
                o = V_NG + NV1 + 8 * L
                link(stt(gsc[:, L], mod[:, L, 8:16], 1.0, over(vT[:, o:o + 8], [P, 8, 2], 2), ALU.add, ALU.mult))

            def modulated_norm(L, r, ready):
                first = n[0]
                for k in range(KT + 1):
                    if k < KT:
                        n[0] += 1
                        stt(H[:, r, k], X[:, r, k], gsc[:, L, k, r:r + 1], rs[:, r], ALU.mult, ALU.mult)\
                            .then_inc(v_chain, 1)
                    if k:
                        dve.wait_ge(v_chain, first + k)
                        ins = ts_(H[:, r, k - 1], H[:, r, k - 1], mod[:, L, k - 1, r:r + 1], None, ALU.add)
                        if ready is h_ready or k == KT:
                            ins.then_inc(ready, 1)

            for g in range(4):
                emptied(dve, f"x{g}")
                squares(X[:, 0, 2 * g:2 * g + 2], H[:, 0, 2 * g:2 * g + 2])
            b = full(dve, "vec1")
            taken(dve.tensor_copy(vT[:, 0:NV1], b[:, 0:NV1]))
            norm("ss1", X[:, 0], H[:, 0], lambda k: v1(V_GMIX, k))
            for g in range(4):
                emptied(dve, f"mem{g}")
                squares(H[:, 1, 2 * g:2 * g + 2], msq[:, 2 * g:2 * g + 2])
            norm("ss2", H[:, 1], H[:, 1], lambda k: v1(V_GMEM, k))
            b = full(dve, "vec2")
            taken(dve.tensor_copy(vT[:, NV1:NV1 + NV2], b[:, 0:NV2]))
            dve.wait_ge(ld_misc, 16 * len(misc_loads))
            gsb = sm[:, 0:32].rearrange("p (t c) -> p t c", t=2)
            b = full(dve, "gate")
            taken(tt_(gsb, b[:, 0:32].rearrange("p (t c) -> p t c", t=2), over(gate_b[:, :], [P, 2, 16], 1),
                      ALU.add))
            g5 = sm[:, 0:32].rearrange("p (t d w h) -> p d t w h", t=2, d=2, w=2)

            def u16(a):
                return sm[:, a:a + 16].rearrange("p (d t h) -> p d t h", d=2, t=2)

            link(dve.tensor_copy(u16(48), g5[:, :, :, 1, :]))
            link(ts_(sm[:, 32:48], sm[:, 48:64], -1.0))
            tail(tt_(sm[:, 32:48], sm[:, 32:48], sm[:, 48:64], ALU.max), nf_ready)
            emptied(dve, "qk3")
            for w in range(5):
                for k in range(KT):
                    src = qkp[:, k, w:w + S]
                    cw = v1(V_CW, 8 * w + k)
                    if w:
                        dve.wait_ge(conv_ready, 8 * (w - 1) + k + 1)
                        stt(qkT[:, k], src, cw, qkT[:, k], ALU.mult, ALU.add).then_inc(conv_ready, 1)
                    else:
                        ts_(qkT[:, k], src, cw, v1(V_CB, k), ALU.mult, ALU.add).then_inc(conv_ready, 1)
            dve.wait_ge(lse_ready, 1)
            tail(stt(sm[:, 64:80], sm[:, 48:64], 0.0, sm[:, 96:112], ALU.min, ALU.subtract), lf_ready)
            emptied(dve, "gv1")
            link(dve.tensor_reduce(sm[:, 260:262], gv[:, :, :], AX.X, ALU.add))
            link(ts_(sm[:, 262:264], sm[:, 260:262], 1.0 / DM))
            link(ts_(gv[:, 0], gv[:, 0], sm[:, 262:263], None, ALU.subtract))
            tail(ts_(gv[:, 1], gv[:, 1], sm[:, 263:264], None, ALU.subtract), gvc_ready)
            b = full(dve, "bcum")
            taken(dve.tensor_copy(sm[:, 900:932], b[:, 0:32]))
            bb, FF = sm[:, 900:916], sm[:, 916:932]
            apc = sm[:, 112:128]
            tail(tt_(u16(112), g5[:, :, :, 0, :], u16(900), ALU.subtract), ap_ready)
            b = full(dve, "apT")
            taken(dve.tensor_copy(sm[0:16, 500:628], b[0:16, 0:P]))
            link(dve.tensor_reduce(sm[0:16, 128:129], sm[0:16, 500:628], AX.X, ALU.max))
            full(dve, "gu1")
            link(tt_(bd, over(sm[0:16, 500:628], [16, 16, P], 1), over(ident[0:16, 0:16], [16, 16, P], 2),
                     ALU.mult))
            tail(ts_(sm[0:16, 129:145], ident[0:16, 0:16], sm[0:16, 128:129]), dmx_ready)
            dve.wait_ge(gvs_ready, 2)
            link(dve.reciprocal(sm[:, 268:270], sm[:, 266:268]))
            for tt in range(TT):
                link(stt(gv[:, tt], gv[:, tt], sm[:, 268 + tt:269 + tt], lng[:, :], ALU.mult, ALU.mult))
            tail(tt_(gv[:, :, :], gv[:, :, :], over(lnb[:, :], [P, 2, DM], 1), ALU.add), gvn_ready)

            b = full(dve, "mxb")
            mxb, ml, M = sm[:, 932:948], sm[:, 948:964], sm[:, 964:980]
            taken(dve.tensor_copy(mxb, b[:, 0:16]))
            link(tt_(ml, FF, mxb, ALU.add))
            for j in range(4):
                b = full(dve, f"A{j}")
                taken(tt_(E[:, 4 * j:4 * j + 4, :], b[:, :].rearrange("p (h s) -> p h s", h=4),
                          over(mask[j // 2], [P, 4, P], 1), ALU.add))
            link(dve.tensor_reduce(M, E[:, :, :], AX.X, ALU.max))
            M2 = M[:, 4:12].rearrange("p (d h) -> p d h", d=2)
            mlp = sm[:, 948:964].rearrange("p (u h) -> p u h", u=4)[:, 0:4:3, :]
            link(tt_(M2, M2, mlp, ALU.max))
            exi, exo = sm[:, 144:184], sm[:, 184:224]
            link(stt(exi[:, 0:16], bb, -1.0, M, ALU.mult, ALU.subtract))
            link(tt_(exi[:, 16:24].rearrange("p (d h) -> p d h", d=2), mlp, M2, ALU.subtract))
            tail(tt_(exi[:, 24:40], apc, mxb, ALU.subtract), ei_ready)
            tail(tt_(E[:, :, :], E[:, :, :], over(M, [P, 16, P], 2), ALU.subtract), em_ready)
            dve.wait_ge(ee_ready, 1)
            link(ts_(sm[:, 224:240], exo[:, 24:40], QK_SCALE))
            for d in range(2):
                b = full(dve, f"KT{d}")
                taken(tt_(kw[:, d], b[:, :].rearrange("p (h s) -> p h s", h=4),
                          over(sm[:, 224 + 12 * d:228 + 12 * d], [P, 4, P], 2), ALU.mult))
            dve.wait_ge(e_ready, 1)
            for tt in range(TT):
                b = full(dve, f"QK{tt}")
                for d in range(2):
                    u = 4 * (2 * d + tt)
                    ins = stt(W[:, u:u + 4, :], E[:, u:u + 4, :], QK_SCALE,
                              b[:, :].rearrange("p (h s) -> p h s", h=4), ALU.mult, ALU.mult)
                    if d:
                        taken(ins)
            dve.wait_ge(v_chain, n[0])
            tail(dve.tensor_reduce(sm[:, 980:996], W[:, :, :], AX.X, ALU.add), w_ready)
            b = full(dve, "nn")
            taken(dve.tensor_copy(sm[:, 240:248], b[:, 0:8]))
            emptied(dve, "gu1")
            for tt in range(TT):
                b = full(dve, f"SP{tt}")
                for g in range(NH):
                    c = slice(g * P, g * P + P)
                    ins = stt(gu[:, tt, c], b[:, c], v1(V_BS, g), gu[:, tt, c], ALU.add, ALU.mult)
                taken(ins)
            b = full(dve, "dI")
            den, r = sm[:, 980:996], sm[:, 248:264]
            taken(tt_(sm[:, 300:308], b[:, 0:8], exo[:, 16:24], ALU.mult))
            link(tt_(den[:, 4:12], den[:, 4:12], sm[:, 300:308], ALU.add))
            link(stt(r, den, -1.0, den, ALU.mult, ALU.max))
            link(tt_(r, r, exo[:, 0:16], ALU.max))
            link(dve.reciprocal(r, r))
            link(tt_(sm[:, 300:308], exo[:, 16:24], r[:, 4:12], ALU.mult))
            for j in range(4):
                b = full(dve, f"NI{j}")
                taken(tt_(num[:, 4 * j:4 * j + 4, :], b[:, :].rearrange("p (h s) -> p h s", h=4),
                          over(r[:, 4 * j:4 * j + 4], [P, 4, P], 2), ALU.mult))
            for d in range(2):
                b = full(dve, f"CI{d}")
                for hh in range(NH):
                    u = 4 + 4 * d + hh
                    ins = stt(num[:, u], b[:, hh * P:hh * P + P], sm[:, 300 + 4 * d + hh:301 + 4 * d + hh],
                              num[:, u], ALU.mult, ALU.add)
                taken(ins)
            hs, hq = num[:, 0:8], num[:, 8:16]
            link(tt_(hs, hs, hq, ALU.add))
            link(tt_(hq, hs, hs, ALU.mult))
            tail(dve.tensor_reduce(sm[:, 272:280], hq, AX.X, ALU.add), hss_ready)
            dve.wait_ge(hsd_ready, 1)
            link(dve.reciprocal(sm[:, 280:288], sm[:, 280:288]))
            link(tt_(hs, hs, over(sm[:, 280:288], [P, 8, P], 2), ALU.mult))
            tho2 = tho[:, :, :].rearrange("p t n -> p (t n)")
            tail(stt(tho2, tho2, 1.0, hs.rearrange("p u s -> p (u s)"), ALU.add, ALU.mult), y_ready)
            for g in range(4):
                b = full(dve, f"yT{g}")
                if g < 2:
                    for j in range(2):
                        k = 2 * g + j
                        ins = ts_(yT[:, k], b[:, j * S:j * S + S], v1(V_GHEAD, k), 0.5, ALU.mult, ALU.mult)
                    taken(ins)
                else:
                    taken(dve.tensor_copy(yT[:, 2 * g:2 * g + 2].rearrange("p k s -> p (k s)"), b[:, :]))

            def residual(prefix):
                for g in range(4):
                    b = full(dve, f"{prefix}{g}")
                    v = X[:, 0, 2 * g:2 * g + 2].rearrange("p k s -> p (k s)")
                    taken(tt_(v, v, b[:, :], ALU.add))
                    squares(X[:, 0, 2 * g:2 * g + 2], H[:, 0, 2 * g:2 * g + 2])

            residual("wo")
            norm("ss3", X[:, 0], H[:, 0], lambda k: v1(V_GX, k))

            def softmax(names, heads, p, width, base, col, scale):
                def columns(c, g):
                    c += 4 * (g % TT) + heads * (g // TT)
                    return sm[:, c:c + heads]

                for g in range(len(names) + 1):
                    if g < len(names):
                        b = full(dve, names[g])
                        m = columns(col[0], g)
                        link(dve.tensor_reduce(m, b[:, :].rearrange("p (h m) -> p h m", h=heads), AX.X, ALU.max))
                        ts_(m, m, -scale).then_inc(mx_ready, 1)
                    if g:
                        emptied(dve, names[g - 1])
                        d = columns(col[1], g - 1)
                        link(dve.reciprocal(d, d))
                        h0_ = heads * ((g - 1) // TT)
                        v = p[:, (g - 1) % TT, h0_:h0_ + heads, :]
                        tt_(v, v, over(d, [P, heads, width], 2), ALU.mult).then_inc(pn_ready, 1)

            softmax([f"S{g}" for g in range(4)], 2, px, 256, 0, (288, 296), X_SCALE)
            residual("xw")
            norm("ss4", X[:, 0], H[:, 0], lambda k: v1(V_GMOE, k))

            b = full(dve, "lg")
            lg = sm[:, 392:464].rearrange("p (t e) -> p t e", t=2)
            taken(tt_(lg, b[:, 0:72].rearrange("p (t e) -> p t e", t=2), over(rb[:, :], [P, 2, 36], 1), ALU.add))
            scr = sm[:, 500:564].rearrange("p (t e) -> p t e", t=2)

            def first_max(vals, w, mx, one):
                s = scr[:, :, 0:w]
                link(dve.tensor_reduce(mx, vals, AX.X, ALU.max))
                link(tt_(s, vals, over(mx, [P, 2, w], 2), ALU.is_equal))
                link(ts_(s, s, -64.0, 64.0, ALU.mult, ALU.add))
                link(tt_(s, s, over(iota[:, 0:w], [P, 2, w], 1), ALU.add))
                link(dve.tensor_reduce(sm[:, 570:572], s, AX.X, ALU.min))
                link(tt_(one, over(iota[:, 0:w], [P, 2, w], 1), over(sm[:, 570:572], [P, 2, w], 2), ALU.is_equal))

            gl, el = lg[:, :, 0:NG], lg[:, :, NG:NG + NE]
            gmax, m1, m2 = sm[:, 572:574], sm[:, 574:576], sm[:, 576:578]
            og = sm[:, 580:588].rearrange("p (t g) -> p t g", t=2)
            first_max(gl, NG, gmax, og)
            tail(tt_(sm[:, 464:472].rearrange("p (t g) -> p t g", t=2), gl, over(gmax, [P, 2, NG], 2),
                     ALU.subtract), ge_ready)
            em = sm[:, 588:652]
            em4 = em.rearrange("p (q e) -> p q e", q=8)
            em3 = em.rearrange("p (t e) -> p t e", t=2)
            link(dve.tensor_copy(em3, el))
            link(tt_(em4, em4, over(sm[:, 580:588], [P, 8, EPG], 2), ALU.mult))
            link(ts_(sm[:, 652:660], sm[:, 580:588], BIG, -BIG, ALU.mult, ALU.add))
            link(tt_(em4, em4, over(sm[:, 652:660], [P, 8, EPG], 2), ALU.add))
            o1 = sm[:, 664:728].rearrange("p (t e) -> p t e", t=2)
            o2 = sm[:, 728:792].rearrange("p (t e) -> p t e", t=2)
            first_max(em3, NE, m1, o1)
            link(stt(em, sm[:, 664:728], -2.0 * BIG, em, ALU.mult, ALU.add))
            first_max(em3, NE, m2, o2)
            tail(tt_(sm[:, 482:484], m2, m1, ALU.subtract), me_ready)
            tail(tt_(sm[:, 320:384], sm[:, 664:728], sm[:, 728:792], ALU.add), A_ready)
            dve.wait_ge(ge_exp, 1)
            link(dve.tensor_reduce(sm[:, 486:488], sm[:, 472:480].rearrange("p (t g) -> p t g", t=2), AX.X, ALU.add))
            dve.wait_ge(me_exp, 1)
            w1_, w2_ = sm[:, 488:490], sm[:, 490:492]
            link(stt(sm[:, 486:488], sm[:, 484:486], 1.0, sm[:, 486:488], ALU.add, ALU.mult))
            link(dve.reciprocal(w1_, sm[:, 486:488]))
            link(tt_(w2_, w1_, sm[:, 484:486], ALU.mult))
            b = full(dve, "pos")
            posn = sm[:, 792:888]
            link(dve.tensor_copy(sm[0:32, 888:889], b[0:32, 96:97]))
            taken(dve.tensor_copy(posn, b[:, 0:96]))
            tail(ts_(sm[0:32, 1000:1128], ones[0:32, :], sm[0:32, 888:889]), cnt_ready)
            b = full(dve, "start")
            taken(dve.tensor_copy(sm[:, 1034 - 134:1034 - 134 + 32], b[:, 0:32]))
            strt = sm[:, 900:932]
            slt = sm[:, 792:856].rearrange("p (t e) -> p t e", t=2)
            for q in range(4):
                ins = ts_(win[0:1, q * NE:q * NE + NE], strt[0:1, :], float(C * q), float(A), ALU.add, ALU.min)
                link(ins) if q < 3 else tail(ins, win_ready)
            link(dve.tensor_reduce(sm[0:1, 889:890], sm[0:1, 856:888], AX.X, ALU.max))
            tail(dve.tensor_copy(mxc[:, :], sm[0:1, 889:890]), win_ready)
            link(tt_(slt, slt, over(strt, [P, 2, NE], 1), ALU.add))
            for o, c in ((664, 478), (728, 480)):
                link(tt_(sm[:, 500:564], sm[:, o:o + 64], sm[:, 792:856], ALU.mult))
                link(dve.tensor_reduce(sm[:, c:c + 2], scr, AX.X, ALU.add))
            for tt in range(TT):
                s1, s2 = sm[:, 478 + tt:479 + tt], sm[:, 480 + tt:481 + tt]
                link(ts_(Pw[:, tt], iota, s1, None, ALU.is_equal))
                ins = stt(Pm[:, tt], iota, s2, Pw[:, tt], ALU.is_equal, ALU.add)
                link(ins)
            tail(dve.memset(xs[:, :, A:AP_], 0.0), P_ready)
            for tt in range(TT):
                s1, s2 = sm[:, 478 + tt:479 + tt], sm[:, 480 + tt:481 + tt]
                link(ts_(Pw[:, tt], iota, s1, w1_[:, tt:tt + 1], ALU.is_equal, ALU.mult))
                link(ts_(ys[:, 0, 0:A], iota, s2, w2_[:, tt:tt + 1], ALU.is_equal, ALU.mult))
                link(tt_(Pw[:, tt], Pw[:, tt], ys[:, 0, 0:A], ALU.add))
            modulation(0)
            modulation(1)
            emptied(dve, "css")
            link(dve.reciprocal(rs[:, 1], sd[:, 1]))
            modulated_norm(0, 1, ctx_ready)

            full(dve, "xs7")

            def vector_step(e, parity, has):
                gate, out1 = has
                if gate:
                    dve.wait_ge(fast[TH], e + 1)
                    dve.wait_ge(fast[UF], e + 1)
                    if gate == "wait":
                        dve.wait_ge(fast[AF], e - 1)
                    stt(th[:, parity], th[:, parity], 1.0, bank[parity][0:C, :], ALU.add, ALU.mult)\
                        .then_inc(chain_e, 1)
                    dve.wait_ge(chain_e, e + 1)
                    stt(ac[:, parity], th[:, parity], 0.5, bank[2 + parity][0:C, :], ALU.mult, ALU.mult)\
                        .then_inc(fast[AC], 1)
                if out1:
                    dve.wait_ge(fast[YF], e)
                    if out1 == "wait":
                        dve.wait_ge(fast[TF], e - 2)
                    dve.tensor_copy(yb[:, 1 - parity, 0:512], bank[5][0:C, :])
                    dve.tensor_copy(yb[:, 1 - parity, 512:1024], bank[6][0:C, :]).then_inc(fast[YB], 1)

            vector_step(0, 0, (True, False))
            vector_step(1, 1, (True, True))
            vector_step(2, 0, ("wait", True))
            vector_step(3, 1, ("wait", "wait"))
            with dve.Fori(0, (NE - 4) // 2) as i:
                for j in range(2):
                    vector_step(i * 2 + (4 + j), j, ("wait", "wait"))
            vector_step(NE, 0, (False, "wait"))

            rows_max = dve.value_load(mxc[0:1, 0:1], min_val=0, max_val=S)
            with dve.If(rows_max > C):
                with dve.Fori(0, NE) as e:
                    for q in range(4):
                        dve.wait_ge(slow[TH], e * 4 + (q + 1))
                        dve.wait_ge(slow[UF], e * 4 + (q + 1))
                        stt(th[:, 0], th[:, 0], 1.0, bank[0][0:C, :], ALU.add, ALU.mult).then_inc(chain_s, 1)
                        dve.wait_ge(chain_s, e * 4 + (q + 1))
                        stt(ac[:, 0], th[:, 0], 0.5, bank[2][0:C, :], ALU.mult, ALU.mult).then_inc(slow[AC], 1)
                        dve.wait_ge(slow[YF], e * 4 + (q + 1))
                        dve.tensor_copy(yb[:, 0, 0:512], bank[5][0:C, :])
                        dve.tensor_copy(yb[:, 0, 512:1024], bank[6][0:C, :]).then_inc(slow[YB], 1)

            for g in range(0, 8, 2):
                st, half = divmod(g, 2)
                b = full(dve, f"yt{g}")
                taken(dve.tensor_copy(yk[:, st, half * 512:half * 512 + 512], b[:, :]))
            residual("co")
            norm("ss5", X[:, 0], X[:, 0], lambda k: v1(V_GFIN, k))
            for g in range(4):
                squares(X[:, 0, 2 * g:2 * g + 2], H[:, 0, 2 * g:2 * g + 2])

            for L in range(2):
                R = 2 - L
                pc2, pcT2, px2, pT2 = attention_room(L)

                def two(v):
                    return v.rearrange("p r s -> p (r s)")

                inverse_root(f"{L}ss", (1 + L) * S)
                modulated_norm(L, 0, h_ready)
                if L == 1:
                    modulated_norm(L, 1, h_ready)
                emptied(dve, f"{L}qkv{2 * L + 1}")
                qsq = view(11296, 1536, t=4, n=384)

                def heads(v, t0, t1, h0_, h1_):
                    return v[:, t0:t1, h0_ * HD2:h1_ * HD2].rearrange("p t (h e) -> p t h e", e=HD2)

                parts = [(0, 4, 0, 6)] if L == 0 else [(0, 2, 0, 6), (2, 4, 4, 6)]
                for a0, a1, b0, b1 in parts:
                    link(tt_(heads(qsq, a0, a1, b0, b1), heads(qkv, a0, a1, b0, b1),
                             heads(qkv, a0, a1, b0, b1), ALU.mult))
                ssq = sm[:, 600:624].rearrange("p (t h) -> p t h", t=4)
                link(dve.memset(sm[:, 600:624], 1.0))
                for n_, (a0, a1, b0, b1) in enumerate(parts):
                    ins = dve.tensor_reduce(ssq[:, a0:a1, b0:b1], heads(qsq, a0, a1, b0, b1), AX.X, ALU.add)
                    tail(ins, qs_ready) if n_ == len(parts) - 1 else link(ins)
                dve.wait_ge(qd_ready, L + 1)
                link(dve.reciprocal(sm[:, 648:672], sm[:, 624:648]))
                rq = sm[:, 648:672].rearrange("p (t h) -> p t h", t=4)
                for a0, a1, b0, b1 in parts:
                    for ta in range(a0, a1):
                        v = heads(qkv, ta, ta + 1, b0, b1)[:, 0]
                        link(tt_(v, v, over(rq[:, ta, b0:b1], [P, b1 - b0, HD2], 2), ALU.mult))
                        ins = tt_(v, v, gains[:, L, b0:b1, :], ALU.mult)
                        link(ins)
                weights(dve, f"{L}const")
                rope = ring[:, place[f"{L}const"], ROPE0:ROPE0 + 128].rearrange("p (t c a f) -> p t c a f", t=2, c=2, a=2)
                for tt in range(TT):
                    v = qkv[:, tt, 0:384].rearrange("p (h a w f) -> p h a w f", h=6, a=2, w=2)
                    for a in range(2):
                        x1, x2 = v[:, :, a, 0, :], v[:, :, a, 1, :]
                        cos = over(rope[:, tt, 0, a, :], [P, 6, 16], 1)
                        sin = over(rope[:, tt, 1, a, :], [P, 6, 16], 1)
                        T = [sm[:, 500 + 96 * 0:596], sm[:, 1000:1096], sm[:, 792:888], sm[:, 392:488]]
                        T = [x.rearrange("p (h f) -> p h f", h=6) for x in T]
                        for o, p1, p2 in ((T[0], x1, cos), (T[1], x2, sin), (T[2], x2, cos), (T[3], x1, sin)):
                            ins = tt_(o, p1, p2, ALU.mult)
                        link(ins)
                        tt_(x1, T[0], T[1], ALU.subtract)
                        ins = tt_(x2, T[2], T[3], ALU.add)
                        tail(ins, rope_ready) if tt == 1 and a == 1 else link(ins)
                link(dve.memset(tp[:, :, :, 0:1], 0.0))
                link(dve.memset(tp[:, :, :, 1 + S:2 + S], 0.0))
                for i in range(2):
                    emptied(dve, f"{L}c{i}")
                    b = full(dve, f"{L}h{i}")
                    taken(tt_(tp[:, i, 0:R, 1:1 + S], b[:, 0:R * S].rearrange("p (r s) -> p r s", r=R),
                              cs2[:, i, 0:R], ALU.mult))
                for i in range(2):
                    o = cs2[:, i, 0:R]

                    def cw2(w):
                        return v2(V_CW2, (L * 3 + w) * 2 + i)

                    link(ts_(o, tp[:, i, 0:R, 0:S], cw2(0), v2(V_CB2, 2 * L + i), ALU.mult, ALU.add))
                    for w in (1, 2):
                        link(stt(o, tp[:, i, 0:R, w:w + S], cw2(w), o, ALU.mult, ALU.add))
                    link(tt_(o, o, bs2[:, i, 0:R], ALU.mult))
                emptied(dve, f"{L}zc1")
                link(tt_(oT[:, 4, 0:R], oT[:, 4, 0:R], cs2[:, 0, 0:R], ALU.mult))
                tail(tt_(oT[:, 5, 0:R], oT[:, 5, 0:R], cs2[:, 1, 0:R], ALU.mult), conv2_ready)
                if L == 0:
                    softmax([f"0cS{g}" for g in range(4)], 2, pc2, 256, 4, (680, 688), A_SCALE)
                softmax([f"{L}xS{g}" for g in range(8)], 1, px2, 512, 8 + 8 * L, (700, 708), A_SCALE)
                for i in range(2):
                    b = full(dve, f"{L}pl{i}")
                    emptied(dve, f"{L}zp{i}")
                    o = two(oT[:, 6 + i, 0:R])
                    taken(stt(o, b[:, 0:R * S], v2(V_PS, 2 * L + i), o, ALU.mult, ALU.mult))
                for i in range(2):
                    b = full(dve, f"{L}wf{i}")
                    emptied(dve, f"{L}zf{i}")
                    o = two(oT[:, i, 0:R])
                    taken(tt_(o, o, b[:, 0:R * S], ALU.mult))
                if L == 0:
                    for i in range(2):
                        b = full(dve, f"0co{i}")
                        o = oT[:, 2 + i, 1]
                        taken(tt_(o, o, b[:, 0:S], ALU.mult))
                for i in range(2):
                    b = full(dve, f"{L}xo{i}")
                    o = oT[:, 2 + i, 0]
                    taken(tt_(o, o, b[:, 0:S], ALU.mult))
                for k in range(KT):
                    b = full(dve, f"{L}out{k}")
                    for r in range(R):
                        ins = stt(X[:, r, k], b[:, r * S:r * S + S], mod[:, L, 16 + k, r:r + 1], X[:, r, k],
                                  ALU.mult, ALU.add)
                    taken(ins)
                    if L == 0:
                        for r in range(2):
                            ins = tt_(H[:, r, k], X[:, r, k], X[:, r, k], ALU.mult)
                        if k % 2:
                            ins.then_inc(sq_ready, 1)


def constants():
    import numpy as np

    i, j = np.arange(P)[:, None], np.arange(P)[None, :]
    one = np.zeros((P, CONST1), np.float32)
    for at, m in ((ID0, i == j), (TRF0, i <= j), (TRB0, i >= j), (TRS0, i < j), (ONE0, i == i + 0 * j),
                  (MKF0, np.where(j <= i, 0.0, -BIG)), (MKB0, np.where(j >= i, 0.0, -BIG))):
        one[:, at:at + P] = m
    one[:, IO0:] = np.arange(A)[None, :]

    def by_tile(m):
        return m.reshape(TT, P, -1).transpose(1, 0, 2).reshape(P, -1)

    two = np.zeros((P, CONST2), np.float32)
    a = 2 * np.pi * (np.outer(np.arange(S), np.arange(S)) % S) / S
    two[:, DFT0:CD0] = by_tile(np.concatenate([np.cos(a), np.sin(a)], 1) / np.sqrt(S))
    a = 2 * np.pi * (np.outer(np.arange(64), np.arange(64)) % 64) / 64
    for h in range(2):
        c = slice(64 * h, 64 * h + 64)
        two[c, CD0 + 64 * h:CD0 + 64 * h + 64] = np.cos(a) / 8
        two[c, CD0 + P + 64 * h:CD0 + P + 64 * h + 64] = -np.sin(a) / 8
    pool = np.zeros((S, 4, S))
    tok = np.arange(S)
    for n, w in enumerate((2, 4, 8, 16)):
        lo, hi = np.clip(tok - w // 2, 0, S), np.clip(tok + w - w // 2, 0, S)
        inside = (tok[:, None] >= lo[None, :]) & (tok[:, None] < hi[None, :])
        pool[:, n, :] = inside / (hi - lo)[None, :] - np.eye(S)
    two[:, POOL0:ROPE0] = by_tile(pool)
    inv = 10000.0 ** (-np.arange(16) / 16)
    ang = np.stack([(tok // 64)[:, None] * inv, (tok % 64)[:, None] * inv], 1)
    two[:, ROPE0:] = by_tile(np.stack([np.cos(ang), np.sin(ang)], 1))
    return one, two


_INS = ['x', 'mem', 'g_mix', 'w_in', 'conv_w', 'conv_b', 'gate_b', 'g_head', 'ln_v_g', 'ln_v_b', 'w_s', 'b_s',
        'w_out', 'g_xattn', 'g_mem', 'w_q_x', 'w_kv_x', 'w_o_x', 'g_moe', 'w_rg', 'b_rg', 'w_re', 'b_re',
        'w_gate', 'w_up', 'w_down', 'g_final', 'c_2', 'ctx_2', 'c_ctx_2', 'w_mod_2', 'b_mod_2', 'norm_g_2',
        'w_in_2', 'q_gain_2', 'k_gain_2', 'w_fourier_2', 'conv_w_2', 'conv_b_2', 'pool_w_2', 'pool_scale_2',
        'w_out_2']


def kernel(**inputs):
    import numpy as _np
    import concourse.bacc as _bacc
    from concourse import mybir as _mybir
    from concourse.bass_utils import run_bass_kernel_spmd as _run

    nc = _bacc.Bacc("TRN2", target_bir_lowering=False, num_devices=1, dynamic_dma_scratch_size=1024)
    arrays, tensors = {}, {}
    one, two = constants()
    for name, a in [(n, inputs[n]) for n in _INS] + [("const1", one), ("const2", two)]:
        a = _np.ascontiguousarray(a)
        arrays[f"in_{name}_dram"] = a
        tensors[name] = nc.dram_tensor(f"in_{name}_dram", a.shape, _mybir.dt.from_np(a.dtype),
                                       kind="ExternalInput").ap()
    tensors["out"] = nc.dram_tensor("out_0_dram", (1, S, D), F32, kind="ExternalOutput").ap()
    first_and_second_block(nc, tensors)
    r = _run(nc, [arrays], core_ids=[0])
    return r.results[0]["out_0_dram"]
```

```python
from contextlib import ExitStack

import concourse.bass as bass
from concourse import mybir

F32 = mybir.dt.float32
I32 = mybir.dt.int32
F32R = mybir.dt.float32r
ALU = mybir.AluOpType
ACT = mybir.ActivationFunctionType
AX = mybir.AxisListType

P = 128
D = 1024
KT = D // P
S = 256
TT = S // P
NH = 4
DM = 512
NE = 32
NG = 4
EPG = NE // NG
C = 64
A = 2 * S
AP_ = A + C
RMS_EPS, LN_EPS = 1e-6, 1e-5
BIG = 1e30
SLOTS = 4
CW = 4096
QW = CW // 4
HD2 = 64
W2 = 256
QK_SCALE = 128.0 ** -0.5
X_SCALE = 256.0 ** -0.5
A_SCALE = 64.0 ** -0.5

ID0, TRF0, TRB0, TRS0, ONE0, MKF0, MKB0, IO0 = (i * P for i in range(8))
CONST1 = IO0 + A
DFT0, CD0, POOL0, ROPE0 = 0, 1024, 1280, 1280 + 2048
CONST2 = ROPE0 + 128
WF0 = CONST2

V_GMIX, V_CB, V_CW, V_GX, V_GMEM, V_GMOE, V_GFIN, V_GHEAD, V_BS, NV1 = 0, 8, 16, 56, 64, 72, 80, 88, 92, 96
V_NG, V_BMOD, V_C, V_CW2, V_CB2, V_PS, NV2 = 0, 16, 64, 80, 92, 96, 100

NORMS = ["ss1", "ss2", "ss3", "ss4", "ss5", "0ss", "1ss"]
SQ_BASE = {name: 4 * n for n, name in enumerate(NORMS)}
H_BASE = {name: 8 * n for n, name in enumerate(NORMS)}

MOD0_SPLIT, MOD1_SPLIT = 4, (1, 4)

ORDER = [(f"x{g}", "a") for g in range(4)] + [("vec1", "v"), ("ss1", "a"), ("qk0", "a"), ("qk1", "a")]
ORDER += [(f"mem{g}", "a") for g in range(4)] + [("ss2", "a")] + [(f"ctx{g}", "a") for g in range(4)]
ORDER += [("vec2", "v"), ("qk2", "a"), ("qk3", "a"), ("gate", "v"), ("ws", "a")]
ORDER += [(f"v{t}", "a") for t in range(2)] + [(f"o{t}", "a") for t in range(2)]
ORDER += [(f"gv{t}", "a") for t in range(2)] + [(f"gu{t}", "a") for t in range(2)]
ORDER += [(f"km{g}", "a") for g in range(4)]
ORDER += [("bcum", "v"), ("apT", "v")] + [(f"vm{g}", "a") for g in range(4)] + [("mxb", "v")]
ORDER += [(f"A{j}", "v") for j in range(4)]


def modulation_groups(L, c0, c1):
    names = []
    for c in range(c0, c1):
        names += [f"mr{L}{c}"] + ([f"mt{L}{c - 1}"] if c else [])
    return names + ([f"mt{L}5"] if c1 == 6 else [])


ORDER += [(n, "a") for n in modulation_groups(0, 0, MOD0_SPLIT)]
ORDER += [(f"KT{d}", "v") for d in range(2)] + [(f"QK{t}", "v") for t in range(2)]
ORDER += [(f"C{d}", "a") for d in range(2)] + [("nn", "v")] + [(f"SP{t}", "v") for t in range(2)]
ORDER += [(f"WT{j}", "a") for j in range(4)] + [("dI", "v")]
ORDER += [(f"NI{j}", "v") for j in range(4)] + [(f"CI{d}", "v") for d in range(2)]
ORDER += [(n, "a") for n in modulation_groups(0, MOD0_SPLIT, 6)]
ORDER += [(f"yT{g}", "v") for g in range(4)] + [(f"wo{g}", "v") for g in range(4)]
ORDER += [("ss3", "a")] + [(f"xq{g}", "a") for g in range(4)] + [(f"S{g}", "a") for g in range(4)]
ORDER += [(n, "a") for n in modulation_groups(1, 0, MOD1_SPLIT[0])]
ORDER += [(f"pT{h}", "a") for h in range(4)] + [(f"xo{h}", "a") for h in range(4)]
ORDER += [(f"xw{g}", "v") for g in range(4)]
ORDER += [("ss4", "a"), ("lg", "v")] + [(f"hk{g}", "a") for g in range(4)]
ORDER += [(n, "a") for n in modulation_groups(1, MOD1_SPLIT[0], MOD1_SPLIT[1])]
ORDER += [("pos", "v"), ("start", "v"), ("css", "a")]
ORDER += [(n, "a") for n in modulation_groups(1, MOD1_SPLIT[1], 6)]
ORDER += [(f"xs{k}", "a") for k in range(8)]
LOOP_AT = len(ORDER)
ORDER += [("0qkv2", "a")]
ORDER += [(f"pw{g}", "a") for g in range(2)] + [(f"yt{g}", "va"[g % 2]) for g in range(8)]
ORDER += [(f"co{g}", "v") for g in range(4)] + [("ss5", "a")]
for L in range(2):
    R = 2 - L
    if L == 0:
        ORDER += [("0qkv3", "a"), ("0ss", "a"), ("0uf1", "a"), ("0qkv0", "a"), ("0qkv1", "a")]
    else:
        ORDER += [("1ss", "a")] + [(f"1qkv{t}", "a") for t in range(4)]
    ORDER += [(f"{L}za{i}", "a") for i in range(2)] + [(f"{L}uf0", "a")]
    ORDER += [(f"{L}zf{i}", "a") for i in range(2)] + [(f"{L}b{i}", "a") for i in range(2)]
    ORDER += [(f"{L}c{i}", "a") for i in range(2)] + [(f"{L}h{i}", "v") for i in range(2)]
    ORDER += [(f"{L}zc{i}", "a") for i in range(2)] + [(f"{L}up{t}", "a") for t in range(R)]
    ORDER += [(f"{L}zp{i}", "a") for i in range(2)]
    ORDER += [(f"{L}hT{h}", "a") for h in range(6)]
    if L == 0:
        ORDER += [(f"{L}cS{g}", "a") for g in range(4)]
    ORDER += [(f"{L}xS{g}", "a") for g in range(8)]
    ORDER += [(f"{L}B{s}{i}", "a") for s in range(R) for i in range(2)]
    ORDER += [(f"{L}dT{i}", "a") for i in range(2)]
    ORDER += [(f"{L}yf{i}", "a") for i in range(2)] + [(f"{L}pl{i}", "v") for i in range(2)]
    ORDER += [(f"{L}wf{i}", "v") for i in range(2)]
    if L == 0:
        ORDER += [(f"{L}cP{h}", "a") for h in range(4)] + [(f"{L}co{i}", "v") for i in range(2)]
    ORDER += [(f"{L}xP{g}", "a") for g in range(8)] + [(f"{L}xo{i}", "v") for i in range(2)]
    ORDER += [(f"{L}out{k}", "v") for k in range(6)] + ([("fin0", "a"), ("fin1", "a")] if L == 1 else [])
    ORDER += [(f"{L}out6", "v"), (f"{L}out7", "v")]
ORDER += [("fin2", "a"), ("fin3", "a")]
INDEX = {name: n for n, (name, _) in enumerate(ORDER)}


def drained_by(name):
    n = INDEX[name]
    who = ORDER[n][1]
    return who, sum(1 for _, w in ORDER[:n + 1] if w == who)


def first_and_second_block(nc, t):
    w_in, w_in2 = t["w_in"][0], t["w_in_2"]

    def rows(w, c0, n):
        return w[:, c0:c0 + n].rearrange("(k p) n -> p k n", p=P)

    before, after = [], []
    for i, (c0, last) in enumerate([(0, "qk1"), (512, "qk3"), (1024, "v1"), (1536, "o1"), (2576, "gv1"),
                                    (2064, "gu1")]):
        before.append((f"in{i}", [(0, rows(w_in, c0, 512))], last))
    for i, last in enumerate(["km1", "km3", "vm1", "vm3"]):
        before.append((f"kv{i}", [(0, rows(t["w_kv_x"][0], 512 * i, 512))], last))

    def mod_chunks(L, c0, c1):
        return [(f"mod{L}{i}", [(0, rows(t["w_mod_2"][L], 512 * i, 512))], f"mr{L}{i}") for i in range(c0, c1)]

    before += mod_chunks(0, 0, 6)
    before += [(f"wout{i}", [(0, rows(t["w_out"][0], 512 * i, 512))], f"wo{2 * i + 1}") for i in range(2)]
    before += [(f"wq{i}", [(0, rows(t["w_q_x"][0], 512 * i, 512))], f"xq{2 * i + 1}") for i in range(2)]
    before += mod_chunks(1, 0, MOD1_SPLIT[0])
    before += [(f"wox{i}", [(0, rows(t["w_o_x"][0], 512 * i, 512))], f"xw{2 * i + 1}") for i in range(2)]
    before += mod_chunks(1, MOD1_SPLIT[0], 6)
    for L in range(2):
        lasts = [f"{L}qkv{2 * L + 1}", f"{L}uf0", f"{L}b1", f"{L}h1", f"{L}up{1 - L}", f"{L}zp1"]
        for i, last in enumerate(lasts):
            after.append((f"{L}in{i}", [(0, rows(w_in2[L], 512 * i, min(512, 2816 - 512 * i)))], last))
        after.append((f"{L}const", [(0, t["const2"]), (WF0, rows(t["w_fourier_2"][L], 0, W2))], f"{L}wf1"))
        if L == 0:
            after.append(("0pc", [], "0co1"))
        after += [(f"{L}px", [], f"{L}xP7"), (f"{L}pT", [], f"{L}xo1")]
        after += [(f"{L}wout{i}", [(0, rows(t["w_out_2"][L], 512 * i, 512))], f"{L}out{4 * i + 3}")
                  for i in range(2)]
    experts = ["G0", "U0"] + [f"{m}{e - (m == 'D')}" for e in range(1, NE) for m in "GUD"] + [f"D{NE - 1}"]

    def expert_slot(m, parity):
        return {"G": (0, 3)[parity], "U": 1, "D": 2}[m]

    place = {c[0]: n % SLOTS for n, c in enumerate(before)}
    place.update({name: expert_slot(name[0], int(name[1:]) % 2) for name in experts})
    place.update({c[0]: n % SLOTS for n, c in enumerate(after)})
    count = [0] * SLOTS
    landed = {}
    for name, pieces in [c[:2] for c in before] + [(e, [0]) for e in experts] + [c[:2] for c in after]:
        count[place[name]] += 16 * len(pieces)
        landed[name] = count[place[name]]

    with ExitStack() as ctx:
        def sb(name, shape, dt=F32):
            return ctx.enter_context(nc.sbuf_tensor(name, shape, dt))

        def sem(name):
            return ctx.enter_context(nc.semaphore(name))

        ring = sb("ring", [P, SLOTS, CW])
        c1 = sb("c1", [P, CONST1])
        w_hi = sb("w_hi", [P, 4, QW], F32R)
        w_lo = sb("w_lo", [P, 4, QW], F32R)
        x_hl = sb("x_hl", [P, KT, 2 * C], F32R)
        a_hl = sb("a_hl", [P, 4, 2 * C], F32R)
        X = sb("X", [P, 2, KT, S])
        H = sb("H", [P, 2, KT, S])
        AR = 14368
        ar = sb("ar", [P, AR])
        raw = sb("raw", [P, 2, P])
        vT = sb("vT", [P, NV1 + NV2])
        wg = sb("wg", [P, KT, 16])
        wr = sb("wr", [P, KT, NG + NE])
        gate_b = sb("gate_b", [P, 16])
        rb = sb("rb", [P, NG + NE])
        lng = sb("lng", [P, DM])
        lnb = sb("lnb", [P, DM])
        gains = sb("gains", [P, 2, 6, HD2])
        wsr = sb("wsr", [P, NH, P])
        wsT = sb("wsT", [P, NH, P])
        pwb = sb("pwb", [P, 2, 2, P])
        sd = sb("sd", [P, 2, S])
        rs = sb("rs", [P, 2, S])
        modr = sb("modr", [P, 2, 48])
        mod = sb("mod", [P, 2, 24, 2])
        gsc = sb("gsc", [P, 2, KT, 2])
        sc = sb("sc", [P, 2, KT])
        sm = sb("sm", [P, 1200])
        win = sb("win", [1, 4 * NE], I32)
        mxc = sb("mxc", [1, 1], I32)

        bank = [ctx.enter_context(nc.psum_tensor(f"bank{i}", [P, 512], F32)) for i in range(8)]

        eb = [bank[(i + LOOP_AT - 1) % 8] for i in range(8)]

        def slot(name, k=KT, n=512, c0=0):
            return ring[:, place[name], c0:c0 + k * n].rearrange("p (k n) -> p k n", k=k)

        ident, trf, trb = c1[:, ID0:ID0 + P], c1[:, TRF0:TRF0 + P], c1[:, TRB0:TRB0 + P]
        trs, ones = c1[:, TRS0:TRS0 + P], c1[:, ONE0:ONE0 + P]
        mask = [c1[:, MKF0:MKF0 + P], c1[:, MKB0:MKB0 + P]]
        iota = c1[:, IO0:IO0 + A]

        def view(at, cols, **dims):
            v = ar[:, at:at + cols]
            names = " ".join(dims)
            last = dict(list(dims.items())[:-1])
            return v.rearrange(f"p ({names}) -> p {names}", **last) if len(dims) > 1 else v

        qkp = view(0, 2080, k=8, s=260)
        W = view(0, 2048, u=16, s=128)
        num = view(0, 2048, u=16, s=128)
        qkT = view(2080, 2048, k=8, s=256)
        yT = qkT
        vs = view(4128, 1024, t=2, n=512)
        tho = view(5152, 1024, t=2, n=512)
        gu = view(6176, 1024, t=2, n=512)
        gv = view(7200, 1024, t=2, n=512)
        kmT = view(8224, 2048, k=8, s=256)
        vm = view(10272, 2048, t=2, n=1024)
        E = view(12320, 2048, u=16, s=128)
        WT = E
        Ej = view(12320, 1024, t=2, n=512)
        msq = view(4128, 2048, k=8, s=256)
        xin = view(10272, 2048, t=2, n=1024)
        memin = view(12320, 2048, t=2, n=1024)
        ctxin = view(8224, 2048, t=2, n=1024)
        h0 = H[:, 0].rearrange("p k s -> p (k s)")
        bd = h0[0:16, :].rearrange("p (u s) -> p u s", u=16)
        kw = h0[:, 0:1024].rearrange("p (d h s) -> p d h s", d=2, h=4)
        Cs = h0[:, 1024:2048].rearrange("p (d h s) -> p d h s", d=2, h=4)
        mrow = [H[0:2, 1].rearrange("p k s -> p (k s)")[:, 0:1024].rearrange("p (b n) -> p b n", b=2),
                view(9216, 1024, b=2, n=512)[0:2]]
        xqT = view(0, 2048, k=8, s=256)
        pTx = view(2080, 2048, h=4, m=2, s=256)
        oTx = view(4128, 2048, k=8, s=256)
        px = view(12320, 2048, t=2, h=4, m=256)
        hk = view(0, 2048, t=2, n=1024)
        Pm = view(2048, 1024, t=2, a=512)
        Pw = view(3072, 1024, t=2, a=512)
        xs = view(4096, 8 * AP_, k=8, a=AP_)
        ys = view(8704, 8 * AP_, k=8, a=AP_)
        gS = view(0, 512)
        uS = view(512, 512)
        yS = view(1024, 1024)
        gT = view(2048, 256, k=4, c=64)
        uT = view(13312, 256, k=4, c=64)
        th = view(2304, 256, k=4, c=64)
        aT = view(2560, 256, k=4, c=64)
        sx = view(0, 512, k=8, c=64)
        sth = view(512, 512)[0:C]
        sac = view(1024, 512)[0:C]
        sy = view(1536, 1024)[0:C]
        y_sum = h0.rearrange("p (k s) -> p k s", k=8)[:, :, 0:C]
        sacT = view(2560, 256, k=4, c=64)
        yk = [v[:, a] for v in (view(1024, 2048, a=2, n=1024), view(6144, 2048, a=2, n=1024)) for a in range(2)]
        PwT = view(0, 1024, a=4, s=256)
        oT = view(0, 4096, k=8, r=2, s=256)
        qkv = view(4096, 2048, t=4, n=512)
        uf = view(6144, 1024, t=4, n=256)
        up = view(7168, 1024, t=4, n=256)
        bs2 = view(8192, 1024, k=2, r=2, s=256)
        cs2 = view(9216, 1024, k=2, r=2, s=256)
        tp = view(10240, 1032, k=2, r=2, s=258)
        q2T = view(11296, 3072, h=6, s=512)[0:HD2]
        hf = H[:, :].rearrange("p r k s -> p (r k s)")
        B2 = hf[:, 0:2048].rearrange("p (r k s) -> p r k s", r=2, k=2)
        yf2 = hf[:, 2048:3072].rearrange("p (k r s) -> p k r s", k=2, r=2)
        dT2 = hf[:, 3072:4096].rearrange("p (k r s) -> p k r s", k=2, r=2)
        outb = view(4096, 2048, t=2, n=1024)

        ld_x, ld_mem, ld_ctx, ld_const, ld_vec1, ld_vec2, ld_gates, ld_misc = (
            sem(n) for n in ("ld_x", "ld_mem", "ld_ctx", "ld_const", "ld_vec1", "ld_vec2", "ld_gates", "ld_misc"))
        w_loaded = [sem(f"w_loaded{i}") for i in range(SLOTS)]
        psum_full = sem("psum_full")
        a_drained = sem("a_drained")
        v_drained = sem("v_drained")
        a_chain, v_chain = sem("a_chain"), sem("v_chain")
        sq_ready = sem("sq_ready")
        h_ready = sem("h_ready")
        csq_ready = sem("csq_ready")
        ctx_ready = sem("ctx_ready")
        conv_ready = sem("conv_ready")
        qk_ready = sem("qk_ready")
        nf_ready, lse_ready, lf_ready = sem("nf_ready"), sem("lse_ready"), sem("lf_ready")
        ap_ready, dmx_ready = sem("ap_ready"), sem("dmx_ready")
        em_ready, e_ready = sem("em_ready"), sem("e_ready")
        ei_ready, ee_ready = sem("ei_ready"), sem("ee_ready")
        w_ready, gvc_ready, gvs_ready, gvn_ready = (sem(n) for n in ("w_ready", "gvc_ready", "gvs_ready",
                                                                     "gvn_ready"))
        hss_ready, hsd_ready, y_ready = sem("hss_ready"), sem("hsd_ready"), sem("y_ready")
        mx_ready, pn_ready = sem("mx_ready"), sem("pn_ready")
        sc_ready = sem("sc_ready")
        ge_ready, ge_exp, me_ready, me_exp = (sem(n) for n in ("ge_ready", "ge_exp", "me_ready", "me_exp"))
        A_ready, cnt_ready, P_ready, win_ready = (sem(n) for n in ("A_ready", "cnt_ready", "P_ready",
                                                                   "win_ready"))
        qs_ready, qd_ready, rope_ready = sem("qs_ready"), sem("qd_ready"), sem("rope_ready")
        conv2_ready = sem("conv2_ready")
        stored = sem("stored")
        hi_done = [sem(f"hi_done{q}") for q in range(4)]
        lo_done = [sem(f"lo_done{q}") for q in range(4)]
        used = [sem(f"used{q}") for q in range(4)]
        (x_hi_ready, x_lo_ready, g_out, u_out, y_out, g_turned, u_turned, y_turned, g_summed, tanh_ready, act_mid,
         act_ready, a_hi_ready, a_lo_ready, ys_ready) = (sem(n) for n in (
             "x_hi_ready", "x_lo_ready", "g_out", "u_out", "y_out", "g_turned", "u_turned", "y_turned", "g_summed",
             "tanh_ready", "act_mid", "act_ready", "a_hi_ready", "a_lo_ready", "ys_ready"))
        u_summed, chain_g, chain_u, chain_y = (sem(n) for n in ("u_summed", "chain_g", "chain_u", "chain_y"))
        XE, GF, UF, TH, AC, AF, AT, YF, YB, TF, YS = range(11)
        slow = [sem(f"slow_{n}") for n in ("window", "gate", "up", "tanh", "act", "act_turned", "actT",
                                           "down", "y", "y_turned", "yT")]
        chain_s = sem("chain_s")
        s_loaded = sem("s_loaded")

        def v1(a, k=0):
            return vT[:, a + k:a + k + 1]

        def v2(a, k=0):
            return vT[:, NV1 + a + k:NV1 + a + k + 1]

        def attention_room(L):
            pc = ring[:, place["0pc"], :]
            return (pc[:, 0:2048].rearrange("p (t h m) -> p t h m", t=2, h=4),
                    pc[:, 2048:4096].rearrange("p (h m s) -> p h m s", h=4, m=2),
                    ring[:, place[f"{L}px"], :].rearrange("p (t h m) -> p t h m", t=2, h=4),
                    ring[:, place[f"{L}pT"], :].rearrange("p (h m s) -> p h m s", h=4, m=4))

        def full(eng, name):
            eng.wait_ge(psum_full, INDEX[name] + 1)
            return bank[INDEX[name] % 8]

        def emptied(eng, name):
            who, n = drained_by(name)
            eng.wait_ge(a_drained if who == "a" else v_drained, n)

        def chunk_number(m, e):
            if not isinstance(e, int):
                return e * 3 + {"G": -1, "U": 0, "D": 4}[m]
            return experts.index(f"{m}{e}")

        def quarter(m, parity, q):
            return ring[:, expert_slot(m, parity), q * QW:q * QW + QW]

        def each_expert(eng, first, last, step, **kw):
            with eng.Fori(first // 2, (last + 1) // 2) as i:
                for j in range(2):
                    step(i * 2 + j, j, **kw)

        def weights(eng, name):
            eng.wait_ge(w_loaded[place[name]], landed[name])

        def tiles(a, pat):
            return a.rearrange(pat, p=P)

        vec1_loads, vec2_loads, r0 = [], [], 0
        for a in (tiles(t["g_mix"], "o (k p) -> (o k) p"), tiles(t["conv_b"], "o (k p) -> (o k) p"),
                  tiles(t["conv_w"], "a w o (k p) -> (a w o k) p"), tiles(t["g_xattn"], "o (k p) -> (o k) p"),
                  tiles(t["g_mem"], "o (k p) -> (o k) p"), tiles(t["g_moe"], "o (k p) -> (o k) p"),
                  tiles(t["g_final"], "(k p) -> k p"), tiles(t["g_head"], "o (k p) -> (o k) p"),
                  t["b_s"][0]):
            vec1_loads.append((raw[r0:r0 + a.shape[0], 0, :], a))
            r0 += a.shape[0]
        assert r0 == NV1
        r0 = 0
        for a in (tiles(t["norm_g_2"], "l (k p) -> (l k) p"), tiles(t["b_mod_2"], "l (k p) -> (l k) p"),
                  tiles(t["c_2"], "o (k p) -> (o k) p"), tiles(t["c_ctx_2"], "(k p) -> k p"),
                  tiles(t["conv_w_2"], "l w (k p) -> (l w k) p"), tiles(t["conv_b_2"], "l (k p) -> (l k) p"),
                  tiles(t["pool_scale_2"], "l (k p) -> (l k) p")):
            vec2_loads.append((raw[r0:r0 + a.shape[0], 1, :], a))
            r0 += a.shape[0]
        assert r0 == NV2

        def everywhere(a, shape):
            return a.unsqueeze(0).broadcast_to(shape)

        gate_loads = [(wg[:, :, :], rows(w_in, 2048, 16)), (wr[:, :, 0:NG], rows(t["w_rg"][0], 0, NG)),
                        (wr[:, :, NG:NG + NE], rows(t["w_re"][0], 0, NE))]
        misc_loads = [(gate_b[:, :], everywhere(t["gate_b"][0], [P, 16])),
                      (rb[:, 0:NG], everywhere(t["b_rg"][0], [P, NG])),
                      (rb[:, NG:NG + NE], everywhere(t["b_re"][0], [P, NE])),
                      (lng[:, :], everywhere(t["ln_v_g"][0], [P, DM])),
                      (lnb[:, :], everywhere(t["ln_v_b"][0], [P, DM])),
                      (wsr[:, :, :], t["w_s"][0].rearrange("g t s -> t g s"))]
        for L in range(2):
            for name, a, b in (("q_gain_2", 0, 4), ("k_gain_2", 4, 6)):
                misc_loads += [(gains[:, L, h_, :], everywhere(t[name][L], [P, HD2])) for h_ in range(a, b)]
        for L in range(2):
            for i in range(2):
                for hf_ in range(2):
                    c = slice(64 * hf_, 64 * hf_ + 64)
                    misc_loads.append((pwb[c, L, i, c], t["pool_w_2"][L, 2 * i + hf_]))

        block = ctx.enter_context(nc.Block())

        @block.sync
        def _(sp):
            sp.dma_start(xin, t["x"][0].rearrange("(t p) n -> p t n", p=P)).then_inc(ld_x, 16)
            occupant = {}

            def load(name, pieces, release):
                old = occupant.get(place[name])
                if old and pieces:
                    if old[0] in experts:
                        split(int(old[0][1:]), old[0][0])
                    else:
                        sp.wait_ge(psum_full, INDEX[old[1]] + 1)
                for c0, src in pieces:
                    k, m = (src.shape[1], src.shape[2]) if len(src.shape) == 3 else (1, src.shape[1])
                    dst = ring[:, place[name], c0:c0 + k * m]
                    if len(src.shape) == 3:
                        dst = dst.rearrange("p (k n) -> p k n", k=k)
                    sp.dma_start(dst, src).then_inc(w_loaded[place[name]], 16)
                occupant[place[name]] = (name, release)

            def split(e, m):
                sp.wait_ge(lo_done[0], chunk_number(m, e) + 1)
                sp.wait_ge(lo_done[3], chunk_number(m, e) + 1)

            wsrc = {"G": t["w_gate"][0], "U": t["w_up"][0], "D": t["w_down"][0]}

            def expert(m, e):
                return wsrc[m][bass.ds(e, 1)].rearrange("a (k p) n -> p (a k) n", p=P)

            load(*before[0])
            sp.wait_ge(ld_vec1, 16 * len(vec1_loads))
            sp.dma_start(memin, t["mem"][0].rearrange("(t p) n -> p t n", p=P)).then_inc(ld_mem, 16)
            load(*before[1])
            sp.dma_start(ctxin, t["ctx_2"][0].rearrange("(t p) n -> p t n", p=P)).then_inc(ld_ctx, 16)
            sp.wait_ge(ld_vec2, 16 * len(vec2_loads))
            for name, pieces, release in before[2:]:
                load(name, pieces, release)
            for name in experts[:5]:
                load(name, [(0, expert(name[0], int(name[1:])))], None)

            def load_step(e, parity):
                for m, f, par in (("G", e, parity), ("U", e, parity), ("D", e - 1, 1 - parity)):
                    split(f - (2 if m == "G" else 1), m)
                    k = 4 if m == "D" else 8
                    at_ = expert_slot(m, par)
                    sp.dma_start(ring[:, at_, :].rearrange("p (k n) -> p k n", k=k), expert(m, f))\
                        .then_inc(w_loaded[at_], 16)

            each_expert(sp, 2, NE - 1, load_step)
            for name in (f"G{NE - 2}", f"G{NE - 1}", f"U{NE - 1}", f"D{NE - 2}"):
                occupant[place[name]] = (name, None)
            load(experts[-1], [(0, expert("D", NE - 1))], None)
            load(*after[0])
            load(*after[1])

            sp.wait_ge(win_ready, 2)
            rows_max = sp.value_load(mxc[0:1, 0:1], min_val=0, max_val=S)
            with sp.If(rows_max > C):
                sp.wait_ge(ys_ready, NE)
                sp.wait_ge(psum_full, INDEX["0qkv2"] + 1)
                weights(sp, "0in1")
                with sp.Fori(0, NE) as e:
                    sp.wait_ge(slow[XE], e * 4 + 1)
                    for m, k in (("G", 8), ("U", 8), ("D", 4)):
                        sp.dma_start(ring[:, "GUD".index(m), :].rearrange("p (k n) -> p k n", k=k),
                                     expert(m, e)).then_inc(s_loaded, 16)
                sp.wait_ge(slow[YS], NE * 4)
                for name, pieces, _ in after[:2]:
                    sp.dma_start(slot(name), pieces[0][1]).then_inc(s_loaded, 16)

            for name, pieces, release in after[2:]:
                load(name, pieces, release)

            for half in range(2):
                emptied(sp, f"fin{2 * half + 1}")
                c = slice(512 * half, 512 * half + 512)
                sp.dma_start(t["out"][0].rearrange("(t p) n -> p t n", p=P)[:, :, c], outb[:, :, c])\
                    .then_inc(stored, 16)
            sp.wait_ge(stored, 32)

        @block.gpsimd
        def _(gp):
            for dst, src in vec2_loads:
                gp.dma_start(dst, src).then_inc(ld_vec2, 16)
            gp.wait_ge(v_chain, 1)
            for dst, src in misc_loads:
                gp.dma_start(dst, src).then_inc(ld_misc, 16)

            def split_first(m, e, parity):
                gp.wait_ge(hi_done[0], chunk_number(m, e) + 1)
                gp.tensor_tensor(w_lo[:, 0, :], quarter(m, parity, 0), w_hi[:, 0, :].bitcast(F32), ALU.subtract)\
                    .then_inc(lo_done[0], 1)

            def split_step(e, parity):
                split_first("G", e, parity)
                split_first("U", e, parity)
                split_first("D", e - 1, 1 - parity)

            split_first("G", 0, 0)
            split_first("U", 0, 0)
            split_step(1, 1)
            each_expert(gp, 2, NE - 1, split_step)
            split_first("D", NE - 1, 1)

        @block.tensor
        def _(pe):
            at = [0]
            last = [None]

            def group(name):
                n = at[0]
                assert ORDER[n][0] == name, (ORDER[n][0], name)
                if n >= 8 and not LOOP_AT <= n < LOOP_AT + 8:
                    emptied(pe, ORDER[n - 8][0])
                at[0] += 1
                return bank[n % 8]

            def mm(o, lhsT, rhs, start=True, stop=True):
                last[0] = pe.matmul(o, lhsT, rhs, start=start, stop=stop)

            def turn(o, a):
                last[0] = pe.transpose(o, a, ident[0:a.shape[0], 0:a.shape[0]])

            def filled():
                last[0].then_inc(psum_full, 1)

            def turn_tokens(prefix, src):
                for g in range(4):
                    b = group(f"{prefix}{g}")
                    for k in range(2):
                        for tt in range(TT):
                            kk = 2 * g + k
                            turn(b[:, k * S + tt * P:k * S + tt * P + P], src[:, tt, kk * P:kk * P + P])
                    filled()

            def norm_sum(name, sq, streams=1):
                b = group(name)
                for k in range(KT):
                    if k % 2 == 0:
                        pe.wait_ge(sq_ready, SQ_BASE[name] + k // 2 + 1)
                    rhs = sq[:, k] if streams == 1 else sq[:, :, k]
                    o = b[:, 0:S] if streams == 1 else b[:, :].rearrange("p (r s) -> p r s", r=2)
                    mm(o, ones, rhs, k == 0, k == KT - 1)
                filled()

            def tile_ready(norm, k):
                pe.wait_ge(h_ready, H_BASE[norm] + k + 1)

            def to_channels(names, w, h, norm=None):
                for g, name in enumerate(names):
                    b = group(name)
                    for j in range(2):
                        m = 2 * g + j
                        for k in range(KT):
                            if norm and m == 0:
                                tile_ready(norm, k)
                            mm(b[:, j * S:j * S + S], w[:, k, m * P:m * P + P], h[:, k], k == 0, k == KT - 1)
                    filled()

            def to_tokens(names, w, h):
                for tt, name in enumerate(names):
                    b = group(name)
                    for k in range(KT):
                        mm(b[:, :], h[:, k, tt * P:tt * P + P], w[:, k], k == 0, k == KT - 1)
                    filled()

            h = H[:, 0]
            pe.wait_ge(ld_const, 16)
            pe.wait_ge(ld_x, 16)
            turn_tokens("x", xin)
            pe.wait_ge(ld_vec1, 16 * len(vec1_loads))
            b = group("vec1")
            turn(b[:, 0:NV1], raw[0:NV1, 0, :])
            filled()
            norm_sum("ss1", h)
            weights(pe, "in0")
            to_channels(["qk0", "qk1"], slot("in0"), h, "ss1")
            pe.wait_ge(ld_mem, 16)
            turn_tokens("mem", memin)
            norm_sum("ss2", msq)
            pe.wait_ge(ld_ctx, 16)
            turn_tokens("ctx", ctxin)
            pe.wait_ge(ld_vec2, 16 * len(vec2_loads))
            b = group("vec2")
            turn(b[:, 0:NV2], raw[0:NV2, 1, :])
            filled()
            weights(pe, "in1")
            to_channels(["qk2", "qk3"], slot("in1"), h)
            pe.wait_ge(ld_gates, 16 * len(gate_loads))
            pe.wait_ge(ld_misc, 16 * len(misc_loads))
            b = group("gate")
            for tt in range(TT):
                for k in range(KT):
                    mm(b[:, tt * 16:tt * 16 + 16], h[:, k, tt * P:tt * P + P], wg[:, k, :], k == 0, k == KT - 1)
            filled()
            b = group("ws")
            for g in range(NH):
                turn(b[:, g * P:g * P + P], wsr[:, g, :])
            filled()
            for c, n in ((2, "v"), (3, "o"), (4, "gv"), (5, "gu")):
                weights(pe, f"in{c}")
                to_tokens([f"{n}0", f"{n}1"], slot(f"in{c}"), h)

            for c in range(2):
                weights(pe, f"kv{c}")
                to_channels([f"km{2 * c}", f"km{2 * c + 1}"], slot(f"kv{c}"), H[:, 1], "ss2" if c == 0 else None)
            pe.wait_ge(lf_ready, 1)
            b = group("bcum")
            lf = sm[:, 64:80]
            mm(b[:, 0:8], trf, lf[:, 0:8])
            mm(b[:, 8:16], trb, lf[:, 8:16])
            mm(b[:, 16:32], ones, lf)
            filled()
            pe.wait_ge(ap_ready, 1)
            b = group("apT")
            turn(b[0:16, 0:P], sm[:, 112:128])
            filled()
            for c in range(2):
                weights(pe, f"kv{c + 2}")
                to_tokens([f"vm{2 * c}", f"vm{2 * c + 1}"], slot(f"kv{c + 2}"), H[:, 1])
            pe.wait_ge(dmx_ready, 1)
            b = group("mxb")
            mm(b[:, 0:16], ones[0:16, :], sm[0:16, 129:145])
            filled()
            for j in range(4):
                b = group(f"A{j}")
                mm(b[:, :], ones[0:16, :], bd[:, 4 * j:4 * j + 4, :])
                filled()

            def modulation(L, c0, c1):
                def turned(c):
                    emptied(pe, f"mr{L}{c}")
                    b = group(f"mt{L}{c}")
                    for m in range(4):
                        turn(b[:, 2 * m:2 * m + 2], mrow[L][:, c % 2, m * P:m * P + P])
                    filled()

                pe.wait_ge(sc_ready, 1)
                for c in range(c0, c1):
                    weights(pe, f"mod{L}{c}")
                    w = slot(f"mod{L}{c}")
                    b = group(f"mr{L}{c}")
                    for k in range(KT):
                        mm(b[0:2, :], sc[:, :, k], w[:, k], k == 0, k == KT - 1)
                    filled()
                    if c:
                        turned(c - 1)
                if c1 == 6:
                    turned(5)

            modulation(0, 0, MOD0_SPLIT)

            pe.wait_ge(qk_ready, 1)
            for d in range(2):
                b = group(f"KT{d}")
                for hh in range(NH):
                    turn(b[:, hh * P:hh * P + P], qkT[:, 4 + hh, d * P:d * P + P])
                filled()
            for tt in range(TT):
                b = group(f"QK{tt}")
                for hh in range(NH):
                    mm(b[:, hh * P:hh * P + P], qkT[:, hh, tt * P:tt * P + P],
                       qkT[:, 4 + hh, tt * P:tt * P + P])
                filled()
            emptied(pe, "KT1")
            emptied(pe, "v1")
            for d in range(2):
                b = group(f"C{d}")
                for hh in range(NH):
                    mm(b[:, hh * P:hh * P + P], kw[:, d, hh, :], vs[:, d, hh * P:hh * P + P])
                filled()
            b = group("nn")
            for d in range(2):
                for hh in range(NH):
                    mm(b[:, d * 4 + hh:d * 4 + hh + 1], kw[:, d, hh, :], ones[:, 0:1])
            filled()
            pe.wait_ge(gvn_ready, 1)
            emptied(pe, "ws")
            for tt in range(TT):
                b = group(f"SP{tt}")
                for g in range(NH):
                    mm(b[:, g * P:g * P + P], wsT[:, g, :], gv[:, tt, g * P:g * P + P])
                filled()
            pe.wait_ge(w_ready, 1)
            for j in range(4):
                b = group(f"WT{j}")
                for hh in range(NH):
                    turn(b[:, hh * P:hh * P + P], W[:, 4 * j + hh, :])
                filled()
            emptied(pe, "nn")
            b = group("dI")
            for d in range(2):
                for hh in range(NH):
                    mm(b[:, d * 4 + hh:d * 4 + hh + 1], qkT[:, hh, (1 - d) * P:(2 - d) * P],
                       sm[:, 240 + d * 4 + hh:241 + d * 4 + hh])
            filled()
            for j in range(4):
                emptied(pe, f"WT{j}")
                b = group(f"NI{j}")
                for hh in range(NH):
                    mm(b[:, hh * P:hh * P + P], WT[:, 4 * j + hh, :], vs[:, j % 2, hh * P:hh * P + P])
                filled()
            emptied(pe, "C1")
            for d in range(2):
                b = group(f"CI{d}")
                for hh in range(NH):
                    mm(b[:, hh * P:hh * P + P], qkT[:, hh, (1 - d) * P:(2 - d) * P], Cs[:, d, hh, :])
                filled()
            modulation(0, MOD0_SPLIT, 6)
            pe.wait_ge(y_ready, 1)
            emptied(pe, "SP1")
            for g in range(4):
                b = group(f"yT{g}")
                for j in range(2):
                    for tt in range(TT):
                        src = (tho if g < 2 else gu)[:, tt, ((2 * g + j) % 4) * P:((2 * g + j) % 4) * P + P]
                        turn(b[:, j * S + tt * P:j * S + tt * P + P], src)
                filled()
            emptied(pe, "yT3")
            for c in range(2):
                weights(pe, f"wout{c}")
                to_channels([f"wo{2 * c}", f"wo{2 * c + 1}"], slot(f"wout{c}"), yT)

            norm_sum("ss3", H[:, 0])
            for c in range(2):
                weights(pe, f"wq{c}")
                to_channels([f"xq{2 * c}", f"xq{2 * c + 1}"], slot(f"wq{c}"), H[:, 0],
                            "ss3" if c == 0 else None)
            emptied(pe, "xq3")
            emptied(pe, "vm3")
            for g in range(4):
                hp, tt = divmod(g, 2)
                b = group(f"S{g}")
                for j in range(2):
                    for k in range(2):
                        kk = 2 * (2 * hp + j) + k
                        mm(b[:, j * S:j * S + S], xqT[:, kk, tt * P:tt * P + P], kmT[:, kk, :], k == 0, k == 1)
                filled()
            modulation(1, 0, MOD1_SPLIT[0])
            for hh in range(NH):
                pe.wait_ge(pn_ready, 2 * (hh // 2 + 1))
                b = group(f"pT{hh}")
                for m in range(2):
                    for tt in range(TT):
                        turn(b[:, m * S + tt * P:m * S + tt * P + P], px[:, tt, hh, m * P:m * P + P])
                filled()
            for hh in range(NH):
                emptied(pe, f"pT{hh}")
                b = group(f"xo{hh}")
                for j in range(2):
                    for m in range(2):
                        c0 = hh * 256 + j * P
                        mm(b[:, j * S:j * S + S], vm[:, m, c0:c0 + P], pTx[:, hh, m, :], m == 0, m == 1)
                filled()
            emptied(pe, "xo3")
            for c in range(2):
                weights(pe, f"wox{c}")
                to_channels([f"xw{2 * c}", f"xw{2 * c + 1}"], slot(f"wox{c}"), oTx)

            norm_sum("ss4", H[:, 0])
            b = group("lg")
            for tt in range(TT):
                for k in range(KT):
                    if tt == 0:
                        tile_ready("ss4", k)
                    mm(b[:, tt * 36:tt * 36 + 36], H[:, 0, k, tt * P:tt * P + P], wr[:, k, :],
                       k == 0, k == KT - 1)
            filled()
            for g in range(4):
                tt, half = divmod(g, 2)
                b = group(f"hk{g}")
                for j in range(4):
                    turn(b[:, j * P:j * P + P], H[:, 0, 4 * half + j, tt * P:tt * P + P])
                filled()
            modulation(1, *MOD1_SPLIT)
            pe.wait_ge(A_ready, 1)
            b = group("pos")
            As = sm[:, 320:384].rearrange("p (t e) -> p t e", t=2)
            mm(b[:, 0:32], trs, As[:, 0, :])
            mm(b[:, 32:64], ones, As[:, 0, :], True, False)
            mm(b[:, 32:64], trs, As[:, 1, :], False, True)
            mm(b[:, 64:96], ones, As[:, 0, :], True, False)
            mm(b[:, 64:96], ones, As[:, 1, :], False, True)
            mm(b[0:32, 96:97], As[:, 0, :], ones[:, 0:1], True, False)
            mm(b[0:32, 96:97], As[:, 1, :], ones[:, 0:1], False, True)
            filled()
            pe.wait_ge(cnt_ready, 1)
            b = group("start")
            mm(b[:, 0:32], sm[0:32, 1000:1128], trs[0:32, 0:32])
            filled()
            pe.wait_ge(csq_ready, 1)
            b = group("css")
            for k in range(KT):
                mm(b[:, 0:S], ones, H[:, 1, k], k == 0, k == KT - 1)
            filled()
            modulation(1, MOD1_SPLIT[1], 6)
            pe.wait_ge(P_ready, 1)
            emptied(pe, "hk3")
            for k in range(KT):
                b = group(f"xs{k}")
                for tt in range(TT):
                    mm(b[:, :], hk[:, tt, k * P:k * P + P], Pm[:, tt, :], tt == 0, tt == 1)
                filled()
            emptied(pe, "xs7")
            emptied(pe, "start")

            def qkv_columns(L, r, tt, waits):
                w = slot(f"{L}in0")
                c0 = 256 if L == 1 and r == 1 else 0
                b = group(f"{L}qkv{2 * r + tt}")
                for k in range(KT):
                    if waits:
                        pe.wait_ge(h_ready, H_BASE[f"{L}ss"] + 8 * r + k + 1)
                    mm(b[:, c0:512], H[:, r, k, tt * P:tt * P + P], w[:, k, c0:512], k == 0, k == KT - 1)
                filled()

            def project(m, e, a, banks):
                n_ = chunk_number(m, e)
                k_of = 2 if m != "D" else 1
                for q in range(4):
                    pe.wait_ge(lo_done[q], n_ + 1)
                    for j in range(k_of):
                        k = q * k_of + j
                        for b_, o in enumerate(banks):
                            c0 = (j + b_) * 512
                            for part in (w_hi, w_lo):
                                ins = pe.matmul(o[:, :], a[:, k, :], part[:, q, c0:c0 + 512],
                                                start=(k == 0 and part is w_hi),
                                                stop=(k == 4 * k_of - 1 and part is w_lo))
                    ins.then_inc(used[q], 1)

            def turn_rows(src, banks, done):
                for k in range(4 * len(banks)):
                    ins = pe.transpose(banks[k // 4][:, (k % 4) * P:(k % 4) * P + P], src[:, k * P:k * P + P], ident)
                ins.then_inc(done, 1)

            def expert_step(e, parity=0, gate=True, down1=True, up1=True, y2=True, again=3):
                if gate:
                    pe.wait_ge(x_lo_ready, e + 1)
                    if up1:
                        pe.wait_ge(g_out, e)
                    project("G", e, x_hl, eb[0:1])
                if up1:
                    pe.wait_ge(u_out, e)
                    if again:
                        pe.wait_ge(u_summed, e - 1)
                    turn_rows(uS, eb[5:6], u_turned)
                if gate:
                    project("U", e, x_hl, eb[1:2])
                if y2:
                    pe.wait_ge(y_out, e - 1)
                    if again == 3:
                        pe.wait_ge(ys_ready, e - 2)
                    turn_rows(yS, eb[6:8], y_turned)
                if gate:
                    pe.wait_ge(g_out, e + 1)
                    if up1:
                        pe.wait_ge(g_summed, e)
                    turn_rows(gS, eb[4:5], g_turned)
                if down1:
                    pe.wait_ge(a_lo_ready, e)
                    project("D", e - 1, a_hl, eb[2:4])

            expert_step(0, down1=False, up1=False, y2=False)
            expert_step(1, y2=False, again=False)
            expert_step(2, again=2)
            expert_step(3)
            each_expert(pe, 4, NE - 1, expert_step)
            expert_step(NE, gate=False)
            expert_step(NE + 1, gate=False, down1=False, up1=False)

            pe.wait_ge(ctx_ready, 1)
            weights(pe, "0in0")
            qkv_columns(0, 1, 0, False)

            pe.wait_ge(win_ready, 2)
            rows_max = pe.value_load(mxc[0:1, 0:1], min_val=0, max_val=S)
            with pe.If(rows_max > C):
                def hold():
                    pe.matmul(eb[4][:, 0:1], ident, ones[:, 0:1], start=True, stop=True)

                def all_rows(bk, w, done):
                    for k in range(KT):
                        ins = pe.matmul(bk[0:C, :], sx[:, k, :], w[:, k], start=(k == 0), stop=(k == KT - 1))
                    ins.then_inc(done, 1)

                with pe.Fori(0, NE) as e:
                    for q in range(4):
                        pe.wait_ge(slow[XE], e * 4 + (q + 1))
                        if q == 0:
                            pe.wait_ge(s_loaded, e * 48 + 48)
                        all_rows(eb[0], ring[:, 0, :].rearrange("p (k n) -> p k n", k=8), slow[GF])
                        all_rows(eb[2], ring[:, 1, :].rearrange("p (k n) -> p k n", k=8), slow[UF])
                        pe.wait_ge(slow[AC], e * 4 + (q + 1))
                        hold()
                        for k in range(4):
                            ins = pe.transpose(eb[4][:, k * C:k * C + C], sac[:, k * P:k * P + P], ident[0:C, 0:C])
                        ins.then_inc(slow[AF], 1)
                        pe.wait_ge(slow[AT], e * 4 + (q + 1))
                        w = ring[:, 2, :].rearrange("p (k n) -> p k n", k=4)
                        for half in range(2):
                            for k in range(4):
                                ins = pe.matmul(eb[5 + half][0:C, :], sacT[:, k, :],
                                                w[:, k, half * 512:half * 512 + 512], start=(k == 0), stop=(k == 3))
                        ins.then_inc(slow[YF], 1)
                        pe.wait_ge(slow[YB], e * 4 + (q + 1))
                        hold()
                        for k in range(KT):
                            ins = pe.transpose(eb[7][:, k * C:k * C + C], sy[:, k * P:k * P + P], ident[0:C, 0:C])
                        ins.then_inc(slow[TF], 1)
                pe.wait_ge(slow[YS], NE * 4)
                pe.wait_ge(s_loaded, NE * 48 + 32)

            pe.wait_ge(ys_ready, NE)
            for g in range(2):
                b = group(f"pw{g}")
                for j in range(2):
                    for tt in range(TT):
                        turn(b[:, j * S + tt * P:j * S + tt * P + P], Pw[:, tt, (2 * g + j) * P:(2 * g + j) * P + P])
                filled()
            for g in range(8):
                st, half = divmod(g, 2)
                b = group(f"yt{g}")
                for j in range(4):
                    turn(b[:, j * P:j * P + P], ys[:, 4 * half + j, st * P:st * P + P])
                filled()
            emptied(pe, "pw1")
            emptied(pe, "yt6")
            emptied(pe, "yt7")
            for g in range(4):
                b = group(f"co{g}")
                for j in range(2):
                    for a in range(4):
                        kk = 2 * g + j
                        mm(b[:, j * S:j * S + S], yk[a][:, kk * P:kk * P + P], PwT[:, a, :], a == 0, a == 3)
                filled()
            norm_sum("ss5", H[:, 0])

            def turn_result(half):
                for tt in range(TT):
                    b = group(f"fin{2 * half + tt}")
                    for j in range(4):
                        turn(b[:, j * P:j * P + P], X[:, 0, 4 * half + j, tt * P:tt * P + P])
                    filled()

            for L in range(2):
                R = 2 - L
                pc2, pcT2, px2, pT2 = attention_room(L)
                def wide(name, w, m):
                    b = group(f"{L}{name}")
                    for k in range(KT):
                        if R == 2:
                            mm(b[:, :].rearrange("p (r s) -> p r s", r=2), w[:, k, m * P:m * P + P],
                               H[:, :, k], k == 0, k == KT - 1)
                        else:
                            mm(b[:, 0:S], w[:, k, m * P:m * P + P], H[:, 0, k], k == 0, k == KT - 1)
                    filled()

                def tokens2(name, w, streams):
                    for r in streams:
                        b = group(f"{L}{name}{r}")
                        for tt in range(TT):
                            for k in range(KT):
                                mm(b[:, tt * W2:tt * W2 + W2], H[:, r, k, tt * P:tt * P + P], w[:, k, :],
                                   k == 0, k == KT - 1)
                        filled()

                if L == 1:
                    weights(pe, "1in0")
                if L == 0:
                    qkv_columns(L, 1, 1, False)
                    norm_sum("0ss", H[:, 0])
                    weights(pe, "0in1")
                    tokens2("uf", slot("0in1")[:, :, 256:512], (1,))
                    qkv_columns(L, 0, 0, True)
                    qkv_columns(L, 0, 1, False)
                else:
                    norm_sum("1ss", H, 2)
                    for r in range(2):
                        qkv_columns(L, r, 0, True)
                        qkv_columns(L, r, 1, False)
                weights(pe, f"{L}in1")
                w = slot(f"{L}in1")
                wide("za0", w, 0)
                wide("za1", w, 1)
                tokens2("uf", w[:, :, 256:512], (0,))
                weights(pe, f"{L}in2")
                w = slot(f"{L}in2")
                for i, n in enumerate(("zf0", "zf1", "b0", "b1")):
                    wide(n, w, i)
                weights(pe, f"{L}in3")
                w = slot(f"{L}in3")
                for i, n in enumerate(("c0", "c1", "h0", "h1")):
                    wide(n, w, i)
                weights(pe, f"{L}in4")
                w = slot(f"{L}in4")
                wide("zc0", w, 0)
                wide("zc1", w, 1)
                tokens2("up", w[:, :, 256:512], range(R))
                weights(pe, f"{L}in5")
                w = slot(f"{L}in5", KT, 256)
                wide("zp0", w, 0)
                wide("zp1", w, 1)

                pe.wait_ge(rope_ready, L + 1)
                for hh in range(6):
                    b = group(f"{L}hT{hh}")
                    for tt in range(4):
                        if hh < 4 and tt >= 2 * R:
                            continue
                        turn(b[0:HD2, tt * P:tt * P + P], qkv[:, tt, hh * HD2:hh * HD2 + HD2])
                    filled()
                emptied(pe, f"{L}hT5")
                if L == 0:
                    for g in range(4):
                        hp, tt = divmod(g, 2)
                        b = group(f"{L}cS{g}")
                        for j in range(2):
                            mm(b[:, j * S:j * S + S], q2T[:, 2 * hp + j, S + tt * P:S + tt * P + P],
                               q2T[:, 4 + hp, S:2 * S])
                        filled()
                for g in range(8):
                    hh, tt = divmod(g, 2)
                    b = group(f"{L}xS{g}")
                    mm(b[:, :], q2T[:, hh, tt * P:tt * P + P], q2T[:, 4 + hh // 2, :])
                    filled()
                weights(pe, f"{L}const")
                cc = ring[:, place[f"{L}const"], :]
                dft = cc[:, DFT0:DFT0 + 1024].rearrange("p (t n) -> p t n", t=2)
                pool = cc[:, POOL0:POOL0 + 2048].rearrange("p (t i s) -> p t i s", t=2, i=4)
                wf = cc[:, WF0:WF0 + 512].rearrange("p (k n) -> p k n", k=2)
                for r in range(R):
                    emptied(pe, f"{L}uf{r}")
                    for i in range(2):
                        b = group(f"{L}B{r}{i}")
                        for tt in range(TT):
                            mm(b[:, :], uf[:, 2 * r + tt, i * P:i * P + P], dft[:, tt, :], tt == 0, tt == 1)
                        filled()
                emptied(pe, f"{L}up{R - 1}")
                for i in range(2):
                    b = group(f"{L}dT{i}")
                    for half in range(2):
                        g = 2 * i + half
                        for r in range(R):
                            for tt in range(TT):
                                mm(b[half * 64:half * 64 + 64, r * S:r * S + S],
                                   up[:, 2 * r + tt, g * 64:g * 64 + 64], pool[:, tt, g, :], tt == 0, tt == 1)
                    filled()
                emptied(pe, f"{L}B{R - 1}1")
                for i in range(2):
                    b = group(f"{L}yf{i}")
                    for r in range(R):
                        mm(b[:, r * S:r * S + S], cc[:, CD0:CD0 + P], B2[:, r, i, 0:S], True, False)
                        mm(b[:, r * S:r * S + S], cc[:, CD0 + P:CD0 + 2 * P], B2[:, r, i, S:2 * S], False, True)
                    filled()

                def both(b):
                    return b[:, 0:R * S]

                for i in range(2):
                    emptied(pe, f"{L}dT{i}")
                    b = group(f"{L}pl{i}")
                    mm(both(b), pwb[:, L, i, :], dT2[:, i, 0:R].rearrange("p r s -> p (r s)"))
                    filled()
                emptied(pe, f"{L}yf1")
                for i in range(2):
                    b = group(f"{L}wf{i}")
                    for k in range(2):
                        mm(both(b), wf[:, k, i * P:i * P + P], yf2[:, k, 0:R].rearrange("p r s -> p (r s)"),
                           k == 0, k == 1)
                    filled()

                if L == 0:
                    for hh in range(NH):
                        pe.wait_ge(pn_ready, 4 + 2 * (hh // 2 + 1))
                        b = group(f"{L}cP{hh}")
                        for m in range(2):
                            for tt in range(TT):
                                turn(b[:, m * S + tt * P:m * S + tt * P + P], pc2[:, tt, hh, m * P:m * P + P])
                        filled()
                    emptied(pe, f"{L}cP3")
                    for i in range(2):
                        b = group(f"{L}co{i}")
                        for j in range(2):
                            for m in range(2):
                                mm(b[j * 64:j * 64 + 64, 0:S], qkv[:, 2 + m, 384 + i * 64:384 + i * 64 + 64],
                                   pcT2[:, 2 * i + j, m, :], m == 0, m == 1)
                        filled()
                for g in range(8):
                    hh, mp = divmod(g, 2)
                    pe.wait_ge(pn_ready, 8 + 8 * L + 2 * (hh + 1))
                    b = group(f"{L}xP{g}")
                    for m in range(2):
                        for tt in range(TT):
                            mk = 2 * mp + m
                            turn(b[:, m * S + tt * P:m * S + tt * P + P], px2[:, tt, hh, mk * P:mk * P + P])
                    filled()
                emptied(pe, f"{L}xP7")
                for i in range(2):
                    b = group(f"{L}xo{i}")
                    for j in range(2):
                        for m in range(4):
                            mm(b[j * 64:j * 64 + 64, 0:S], qkv[:, m, 384 + i * 64:384 + i * 64 + 64],
                               pT2[:, 2 * i + j, m, :], m == 0, m == 3)
                    filled()
                pe.wait_ge(conv2_ready, L + 1)
                emptied(pe, f"{L}xo1")
                for c in range(2):
                    weights(pe, f"{L}wout{c}")
                    w = slot(f"{L}wout{c}")
                    for m in range(4):
                        if L == 1 and 4 * c + m == 6:
                            emptied(pe, "1out3")
                            turn_result(0)
                        b = group(f"{L}out{4 * c + m}")
                        for k in range(KT):
                            mm(both(b), w[:, k, m * P:m * P + P], oT[:, k, 0:R].rearrange("p r s -> p (r s)"),
                               k == 0, k == KT - 1)
                        filled()
            emptied(pe, "1out7")
            turn_result(1)
            assert at[0] == len(ORDER)

        @block.scalar
        def _(act):
            n = [0]

            def link(ins):
                n[0] += 1
                ins.then_inc(a_chain, 1)
                act.wait_ge(a_chain, n[0])

            act.dma_start(c1[:, :], t["const1"]).then_inc(ld_const, 16)
            for dst, src in vec1_loads:
                act.dma_start(dst, src).then_inc(ld_vec1, 16)
            for dst, src in gate_loads:
                act.dma_start(dst, src).then_inc(ld_gates, 16)

            def take(name, dst, src=None, func=ACT.Copy, **kw):
                b = full(act, name)
                src = b[:, :] if src is None else src(b)
                act.activation(dst, src, func, **kw).then_inc(a_drained, 1)

            def flat(v):
                return v.rearrange("p a b -> p (a b)")

            def root(name, n=S):
                n_ = NORMS.index(name)
                act.activation(sm[:, 1192 + n_:1193 + n_], eps, ACT.Sqrt)
                if H_BASE[name]:
                    act.wait_ge(h_ready, H_BASE[name])
                take(name, flat(sd)[:, 0:n], lambda b: b[:, 0:n], ACT.Sqrt, scale=1.0 / D, bias=eps[:, 0:1])

            eps, eps_ln = sm[:, 1190:1191], sm[:, 1191:1192]
            def take_qk(g):
                take(f"qk{g}", qkp[:, 2 * g:2 * g + 2, 2:2 + S], lambda b: b[:, :].rearrange("p (k s) -> p k s", k=2))

            for g in range(4):
                take(f"x{g}", flat(X[:, 0, 2 * g:2 * g + 2]))
            act.wait_ge(v_chain, 4)
            root("ss1")
            take_qk(0)
            take_qk(1)
            for g in range(4):
                take(f"mem{g}", flat(H[:, 1, 2 * g:2 * g + 2]))
            root("ss2")
            for g in range(4):
                take(f"ctx{g}", flat(X[:, 1, 2 * g:2 * g + 2]))
            take_qk(2)
            take_qk(3)
            take("ws", flat(wsT))
            for tt in range(TT):
                take(f"v{tt}", vs[:, tt, :])
            for tt in range(TT):
                take(f"o{tt}", tho[:, tt, :], None, ACT.Tanh, scale=0.5)
            for tt in range(TT):
                take(f"gv{tt}", gv[:, tt, :], None, ACT.Gelu_apprx_tanh)
            for tt in range(TT):
                take(f"gu{tt}", gu[:, tt, :], None, ACT.Gelu_apprx_tanh)
            emptied(act, "vec2")
            act.activation(flat(sc), vT[:, NV1 + V_C:NV1 + V_C + 16], ACT.Silu).then_inc(sc_ready, 1)
            act.wait_ge(nf_ready, 1)
            link(act.activation(sm[:, 80:96], sm[:, 32:48], ACT.Exp, scale=-1.0))
            act.activation(sm[:, 96:112], sm[:, 80:96], ACT.Ln, bias=1.0).then_inc(lse_ready, 1)
            act.wait_ge(gvc_ready, 1)
            for tt in range(TT):
                ins = act.activation(Ej[:, tt], gv[:, tt, :], ACT.Square, accum_out=sm[:, 264 + tt:265 + tt])
            ins.then_inc(gvs_ready, 1)
            act.wait_ge(gvs_ready, 1)
            act.activation(sm[:, 266:268], sm[:, 264:266], ACT.Sqrt, scale=1.0 / DM, bias=eps_ln)\
                .then_inc(gvs_ready, 1)
            for g in range(4):
                take(f"km{g}", flat(kmT[:, 2 * g:2 * g + 2]))
            for g in range(4):
                c, tt = divmod(g, 2)
                take(f"vm{g}", vm[:, tt, c * 512:c * 512 + 512])
            def take_modulation(L, c0, c1):
                for name in modulation_groups(L, c0, c1):
                    c = int(name[3])
                    if name[1] == "r":
                        if c >= 2:
                            full(act, f"mt{L}{c - 2}")
                        take(name, mrow[L][:, c % 2, :], lambda b: b[0:2, :])
                    else:
                        take(name, modr[:, L, 8 * c:8 * c + 8], lambda b: b[:, 0:8])

            act.wait_ge(conv_ready, 40)
            act.activation(qkT[:, :, :], qkT[:, :, :], ACT.Silu).then_inc(qk_ready, 1)
            act.wait_ge(ei_ready, 1)
            act.activation(sm[:, 184:224], sm[:, 144:184], ACT.Exp).then_inc(ee_ready, 1)
            act.wait_ge(em_ready, 1)
            act.activation(E[:, :, :], E[:, :, :], ACT.Exp).then_inc(e_ready, 1)
            take_modulation(0, 0, MOD0_SPLIT)
            for d in range(2):
                take(f"C{d}", Cs[:, d].rearrange("p h s -> p (h s)"))
            for j in range(4):
                take(f"WT{j}", flat(WT[:, 4 * j:4 * j + 4, :]))
            act.wait_ge(hss_ready, 1)
            act.activation(sm[:, 280:288], sm[:, 272:280], ACT.Sqrt, scale=1.0 / 128, bias=eps)\
                .then_inc(hsd_ready, 1)
            take_modulation(0, MOD0_SPLIT, 6)
            root("ss3")
            for g in range(4):
                take(f"xq{g}", flat(xqT[:, 2 * g:2 * g + 2]))

            def softmax_exp(names, heads, p, width, base, col):
                for g, name in enumerate(names):
                    b = full(act, name)
                    act.wait_ge(mx_ready, base + g + 1)
                    for j in range(heads):
                        tt, hh = g % TT, heads * (g // TT) + j
                        ins = act.activation(p[:, tt, hh, :], b[:, j * width:j * width + width], ACT.Exp,
                                             scale=col[2], bias=sm[:, col[0] + 4 * tt + hh:col[0] + 4 * tt + hh + 1],
                                             accum_out=sm[:, col[1] + 4 * tt + hh:col[1] + 4 * tt + hh + 1])
                        if j == heads - 1:
                            ins.then_inc(a_drained, 1)

            softmax_exp([f"S{g}" for g in range(4)], 2, px, 256, 0, (288, 296, X_SCALE))
            take_modulation(1, 0, MOD1_SPLIT[0])
            for hh in range(NH):
                take(f"pT{hh}", pTx[:, hh].rearrange("p m s -> p (m s)"))
            for hh in range(NH):
                take(f"xo{hh}", flat(oTx[:, 2 * hh:2 * hh + 2]))
            root("ss4")
            for g in range(4):
                tt, half = divmod(g, 2)
                take(f"hk{g}", hk[:, tt, half * 512:half * 512 + 512])
            act.activation(H[:, 1], X[:, 1], ACT.Square).then_inc(csq_ready, 1)
            act.wait_ge(ge_ready, 1)
            act.activation(sm[:, 472:480], sm[:, 464:472], ACT.Exp).then_inc(ge_exp, 1)
            act.wait_ge(me_ready, 1)
            act.activation(sm[:, 484:486], sm[:, 482:484], ACT.Exp).then_inc(me_exp, 1)
            take_modulation(1, *MOD1_SPLIT)
            take("css", sd[:, 1], lambda b: b[:, 0:S], ACT.Sqrt, scale=1.0 / D, bias=eps[:, 0:1])
            take_modulation(1, MOD1_SPLIT[1], 6)
            def split_hi(m, e, parity, between=None):
                name = None if not isinstance(e, int) else f"{m}{e}"
                at_ = expert_slot(m, parity)
                if name:
                    weights(act, name)
                elif m == "G":
                    act.wait_ge(w_loaded[at_], landed[f"G{parity}"] + (e - parity) * 8)
                else:
                    act.wait_ge(w_loaded[at_], landed[f"{m}0"] + e * 16)
                for q in range(4):
                    if between and q == 2:
                        between()
                    if name != "G0":
                        act.wait_ge(used[q], chunk_number(m, e))
                    act.activation(w_hi[:, q, :], quarter(m, parity, q), ACT.Copy).then_inc(hi_done[q], 1)

            split_hi("G", 0, 0)
            for k in range(KT):
                take(f"xs{k}", xs[:, k, 0:A])

            act.wait_ge(win_ready, 2)

            def starts_at(e, q):
                return act.value_load(win[0:1, bass.ds(e + q * NE, 1)], min_val=0, max_val=A)

            def chunk_out(m, e, dst, banks, again, turned, out):
                act.wait_ge(used[3], chunk_number(m, e) + 1)
                if again:
                    act.wait_ge(turned, e)
                for b_, o in enumerate(banks):
                    ins = act.activation(dst[:, b_ * 512:b_ * 512 + 512], o[:, :], ACT.Copy)
                ins.then_inc(out, 1)

            def rows_hi(e):
                w0 = starts_at(e, 0)
                act.activation(x_hl[:, :, 0:C], xs[:, :, bass.ds(w0, C)], ACT.Copy).then_inc(x_hi_ready, 1)

            def scalar_step(e, parity, gate=True, one=True, two=True, more=True, again=3):
                if gate and not (isinstance(e, int) and e == 0):
                    split_hi("G", e, parity)
                if two:
                    chunk_out("D", e - 2, yS, eb[2:4], again == 3, y_turned, y_out)
                if one:
                    act.wait_ge(g_summed, e)
                    if two:
                        act.wait_ge(act_mid, e - 1)
                    act.activation(th, gT, ACT.Tanh, scale=0.5).then_inc(tanh_ready, 1)
                if gate:
                    split_hi("U", e, parity)
                    chunk_out("G", e, gS, eb[0:1], one, g_turned, g_out)
                def act_hi():
                    act.wait_ge(act_ready, e)
                    if two:
                        act.wait_ge(used[3], chunk_number("D", e - 2) + 1)
                    act.activation(a_hl[:, :, 0:C], aT, ACT.Copy).then_inc(a_hi_ready, 1)

                if one:
                    split_hi("D", e - 1, 1 - parity, act_hi)
                if gate:
                    if more:
                        act.wait_ge(used[3], chunk_number("U", e) + 1)
                        rows_hi(e + 1)
                    chunk_out("U", e, uS, eb[1:2], one, u_turned, u_out)

            emptied(act, "xs7")
            rows_hi(0)
            scalar_step(0, 0, one=False, two=False)
            scalar_step(1, 1, two=False)
            scalar_step(2, 0, again=2)
            scalar_step(3, 1)
            each_expert(act, 4, NE - 3, scalar_step)
            scalar_step(NE - 2, 0)
            scalar_step(NE - 1, 1, more=False)
            scalar_step(NE, 0, gate=False)
            scalar_step(NE + 1, 1, gate=False, one=False)

            rows_max = act.value_load(mxc[0:1, 0:1], min_val=0, max_val=S)
            with act.If(rows_max > C):
                act.wait_ge(ys_ready, NE)
                with act.Fori(0, NE) as e:
                    for q in range(4):
                        w0 = starts_at(e, q)
                        act.activation(sx, xs[:, :, bass.ds(w0, C)], ACT.Copy).then_inc(slow[XE], 1)
                        act.wait_ge(slow[GF], e * 4 + (q + 1))
                        act.activation(sth, eb[0][0:C, :], ACT.Tanh, scale=0.5).then_inc(slow[TH], 1)
                        act.wait_ge(slow[AF], e * 4 + (q + 1))
                        act.activation(sacT.rearrange("p k c -> p (k c)"), eb[4][:, 0:4 * C],
                                       ACT.Copy).then_inc(slow[AT], 1)
                        act.wait_ge(slow[TF], e * 4 + (q + 1))
                        act.activation(ys[:, :, bass.ds(w0, C)], eb[7][:, :].rearrange("p (k c) -> p k c", k=KT),
                                       ACT.Copy).then_inc(slow[YS], 1)
                        act.wait_ge(slow[YS], e * 4 + (q + 1))

            def take_qkv(L, tt):
                c0 = 256 if L == 1 and tt >= 2 else 0
                take(f"{L}qkv{tt}", qkv[:, tt, c0:512], lambda b: b[:, c0:512])

            take_qkv(0, 2)
            for g in range(2):
                take(f"pw{g}", flat(PwT[:, 2 * g:2 * g + 2]))
            for g in range(1, 8, 2):
                st, half = divmod(g, 2)
                if g == 1:
                    act.wait_ge(ys_ready, NE)
                take(f"yt{g}", yk[st][:, half * 512:half * 512 + 512])
            root("ss5")

            for L in range(2):
                R = 2 - L

                def half(b):
                    return b[:, 0:R * S]

                def two(v):
                    return v.rearrange("p r s -> p (r s)")

                pc2, pcT2, px2, pT2 = attention_room(L)

                if L == 0:
                    take_qkv(L, 3)
                    root("0ss")
                    take("0uf1", flat(uf[:, 2:4]))
                    take_qkv(L, 0)
                    take_qkv(L, 1)
                else:
                    root("1ss", 2 * S)
                    for tt in range(4):
                        take_qkv(L, tt)
                for i in range(2):
                    take(f"{L}za{i}", two(oT[:, 2 + i, 0:R]), half, ACT.Silu)
                take(f"{L}uf0", flat(uf[:, 0:2]))
                for i in range(2):
                    take(f"{L}zf{i}", two(oT[:, i, 0:R]), half, ACT.Silu)
                act.wait_ge(qs_ready, L + 1)
                act.activation(sm[:, 624:648], sm[:, 600:624], ACT.Sqrt, scale=1.0 / HD2, bias=eps)\
                    .then_inc(qd_ready, 1)
                for n_, dst in (("b", bs2), ("c", cs2)):
                    for i in range(2):
                        take(f"{L}{n_}{i}", two(dst[:, i, 0:R]), half)
                for i in range(2):
                    take(f"{L}zc{i}", two(oT[:, 4 + i, 0:R]), half, ACT.Silu)
                for r in range(R):
                    take(f"{L}up{r}", flat(up[:, 2 * r:2 * r + 2]))
                for i in range(2):
                    take(f"{L}zp{i}", two(oT[:, 6 + i, 0:R]), half, ACT.Silu)
                for hh in range(6):
                    n_ = R * S if hh < 4 else 2 * S
                    take(f"{L}hT{hh}", q2T[:, hh, 0:n_], lambda b: b[0:HD2, 0:n_])
                if L == 0:
                    softmax_exp([f"0cS{g}" for g in range(4)], 2, pc2, 256, 4, (680, 688, A_SCALE))
                softmax_exp([f"{L}xS{g}" for g in range(8)], 1, px2, 512, 8 + 8 * L, (700, 708, A_SCALE))
                for r in range(R):
                    for i in range(2):
                        take(f"{L}B{r}{i}", B2[:, r, i, :])
                for i in range(2):
                    take(f"{L}dT{i}", two(dT2[:, i, 0:R]), half)
                for i in range(2):
                    take(f"{L}yf{i}", two(yf2[:, i, 0:R]), half)
                if L == 0:
                    for hh in range(NH):
                        take(f"0cP{hh}", pcT2[:, hh].rearrange("p m s -> p (m s)"))
                for g in range(8):
                    hh, mp = divmod(g, 2)
                    take(f"{L}xP{g}", pT2[:, hh, 2 * mp:2 * mp + 2].rearrange("p m s -> p (m s)"))
            for g in range(4):
                half_, tt = divmod(g, 2)
                take(f"fin{g}", outb[:, tt, half_ * 512:half_ * 512 + 512])

        @block.vector
        def _(dve):
            n = [0]

            def link(ins):
                n[0] += 1
                ins.then_inc(v_chain, 1)
                dve.wait_ge(v_chain, n[0])

            def tail(ins, s):
                tails[id(s)] = tails.get(id(s), 0) + 1
                ins.then_inc(s, 1)
                dve.wait_ge(s, tails[id(s)])

            tails = {}

            def taken(ins):
                taken_n[0] += 1
                ins.then_inc(v_drained, 1)
                dve.wait_ge(v_drained, taken_n[0])

            taken_n = [0]

            def over(v, shape, axis):
                return v.unsqueeze(axis).broadcast_to(shape)

            def tt_(o, a, b, op):
                return dve.tensor_tensor(o, a, b, op)

            def ts_(o, a, s1, s2=None, op0=ALU.mult, op1=None):
                if s2 is None:
                    return dve.tensor_scalar(o, a, s1, None, op0)
                return dve.tensor_scalar(o, a, s1, s2, op0, op1)

            def stt(o, a, s, b, op0, op1):
                return dve.scalar_tensor_tensor(out=o, in0=a, scalar=s, in1=b, op0=op0, op1=op1)

            link(dve.memset(pwb[:, :, :, :], 0.0))
            link(dve.memset(sm[:, :], 0.0))
            link(dve.memset(sm[:, 1190:1191], RMS_EPS))
            link(dve.memset(sm[:, 1191:1192], LN_EPS))
            link(dve.memset(qkp[:, :, 0:2], 0.0))
            link(dve.memset(qkp[:, :, 2 + S:4 + S], 0.0))

            def squares(src, dst):
                tt_(dst, src, src, ALU.mult).then_inc(sq_ready, 1)

            def norm(name, src, dst, gain):
                emptied(dve, name)
                link(dve.reciprocal(rs[:, 0], sd[:, 0]))
                for k in range(KT):
                    stt(dst[:, k], src[:, k], gain(k), rs[:, 0, :], ALU.mult, ALU.mult).then_inc(h_ready, 1)
                dve.wait_ge(h_ready, H_BASE[name] + KT)

            def modulation(L):
                emptied(dve, f"mt{L}5")
                o = V_BMOD + NV1 + 24 * L
                link(tt_(mod[:, L], modr[:, L].rearrange("p (m r) -> p m r", r=2),
                         over(vT[:, o:o + 24], [P, 24, 2], 2), ALU.add))
                o = V_NG + NV1 + 8 * L
                link(stt(gsc[:, L], mod[:, L, 8:16], 1.0, over(vT[:, o:o + 8], [P, 8, 2], 2), ALU.add, ALU.mult))

            def modulated_norm(L, r, ready):
                first = n[0]
                for k in range(KT + 1):
                    if k < KT:
                        n[0] += 1
                        stt(H[:, r, k], X[:, r, k], gsc[:, L, k, r:r + 1], rs[:, r], ALU.mult, ALU.mult)\
                            .then_inc(v_chain, 1)
                    if k:
                        dve.wait_ge(v_chain, first + k)
                        ins = ts_(H[:, r, k - 1], H[:, r, k - 1], mod[:, L, k - 1, r:r + 1], None, ALU.add)
                        if ready is h_ready or k == KT:
                            ins.then_inc(ready, 1)

            for g in range(4):
                emptied(dve, f"x{g}")
                squares(X[:, 0, 2 * g:2 * g + 2], H[:, 0, 2 * g:2 * g + 2])
            b = full(dve, "vec1")
            taken(dve.tensor_copy(vT[:, 0:NV1], b[:, 0:NV1]))
            norm("ss1", X[:, 0], H[:, 0], lambda k: v1(V_GMIX, k))
            for g in range(4):
                emptied(dve, f"mem{g}")
                squares(H[:, 1, 2 * g:2 * g + 2], msq[:, 2 * g:2 * g + 2])
            norm("ss2", H[:, 1], H[:, 1], lambda k: v1(V_GMEM, k))
            b = full(dve, "vec2")
            taken(dve.tensor_copy(vT[:, NV1:NV1 + NV2], b[:, 0:NV2]))
            dve.wait_ge(ld_misc, 16 * len(misc_loads))
            gsb = sm[:, 0:32].rearrange("p (t c) -> p t c", t=2)
            b = full(dve, "gate")
            taken(tt_(gsb, b[:, 0:32].rearrange("p (t c) -> p t c", t=2), over(gate_b[:, :], [P, 2, 16], 1),
                      ALU.add))
            g5 = sm[:, 0:32].rearrange("p (t d w h) -> p d t w h", t=2, d=2, w=2)

            def u16(a):
                return sm[:, a:a + 16].rearrange("p (d t h) -> p d t h", d=2, t=2)

            link(dve.tensor_copy(u16(48), g5[:, :, :, 1, :]))
            link(ts_(sm[:, 32:48], sm[:, 48:64], -1.0))
            tail(tt_(sm[:, 32:48], sm[:, 32:48], sm[:, 48:64], ALU.max), nf_ready)
            emptied(dve, "qk3")
            for w in range(5):
                for k in range(KT):
                    src = qkp[:, k, w:w + S]
                    cw = v1(V_CW, 8 * w + k)
                    if w:
                        dve.wait_ge(conv_ready, 8 * (w - 1) + k + 1)
                        stt(qkT[:, k], src, cw, qkT[:, k], ALU.mult, ALU.add).then_inc(conv_ready, 1)
                    else:
                        ts_(qkT[:, k], src, cw, v1(V_CB, k), ALU.mult, ALU.add).then_inc(conv_ready, 1)
            dve.wait_ge(lse_ready, 1)
            tail(stt(sm[:, 64:80], sm[:, 48:64], 0.0, sm[:, 96:112], ALU.min, ALU.subtract), lf_ready)
            emptied(dve, "gv1")
            link(dve.tensor_reduce(sm[:, 260:262], gv[:, :, :], AX.X, ALU.add))
            link(ts_(sm[:, 262:264], sm[:, 260:262], 1.0 / DM))
            link(ts_(gv[:, 0], gv[:, 0], sm[:, 262:263], None, ALU.subtract))
            tail(ts_(gv[:, 1], gv[:, 1], sm[:, 263:264], None, ALU.subtract), gvc_ready)
            b = full(dve, "bcum")
            taken(dve.tensor_copy(sm[:, 900:932], b[:, 0:32]))
            bb, FF = sm[:, 900:916], sm[:, 916:932]
            apc = sm[:, 112:128]
            tail(tt_(u16(112), g5[:, :, :, 0, :], u16(900), ALU.subtract), ap_ready)
            b = full(dve, "apT")
            taken(dve.tensor_copy(sm[0:16, 500:628], b[0:16, 0:P]))
            link(dve.tensor_reduce(sm[0:16, 128:129], sm[0:16, 500:628], AX.X, ALU.max))
            full(dve, "gu1")
            link(tt_(bd, over(sm[0:16, 500:628], [16, 16, P], 1), over(ident[0:16, 0:16], [16, 16, P], 2),
                     ALU.mult))
            tail(ts_(sm[0:16, 129:145], ident[0:16, 0:16], sm[0:16, 128:129]), dmx_ready)
            dve.wait_ge(gvs_ready, 2)
            link(dve.reciprocal(sm[:, 268:270], sm[:, 266:268]))
            for tt in range(TT):
                link(stt(gv[:, tt], gv[:, tt], sm[:, 268 + tt:269 + tt], lng[:, :], ALU.mult, ALU.mult))
            tail(tt_(gv[:, :, :], gv[:, :, :], over(lnb[:, :], [P, 2, DM], 1), ALU.add), gvn_ready)

            b = full(dve, "mxb")
            mxb, ml, M = sm[:, 932:948], sm[:, 948:964], sm[:, 964:980]
            taken(dve.tensor_copy(mxb, b[:, 0:16]))
            link(tt_(ml, FF, mxb, ALU.add))
            for j in range(4):
                b = full(dve, f"A{j}")
                taken(tt_(E[:, 4 * j:4 * j + 4, :], b[:, :].rearrange("p (h s) -> p h s", h=4),
                          over(mask[j // 2], [P, 4, P], 1), ALU.add))
            link(dve.tensor_reduce(M, E[:, :, :], AX.X, ALU.max))
            M2 = M[:, 4:12].rearrange("p (d h) -> p d h", d=2)
            mlp = sm[:, 948:964].rearrange("p (u h) -> p u h", u=4)[:, 0:4:3, :]
            link(tt_(M2, M2, mlp, ALU.max))
            exi, exo = sm[:, 144:184], sm[:, 184:224]
            link(stt(exi[:, 0:16], bb, -1.0, M, ALU.mult, ALU.subtract))
            link(tt_(exi[:, 16:24].rearrange("p (d h) -> p d h", d=2), mlp, M2, ALU.subtract))
            tail(tt_(exi[:, 24:40], apc, mxb, ALU.subtract), ei_ready)
            tail(tt_(E[:, :, :], E[:, :, :], over(M, [P, 16, P], 2), ALU.subtract), em_ready)
            dve.wait_ge(ee_ready, 1)
            link(ts_(sm[:, 224:240], exo[:, 24:40], QK_SCALE))
            for d in range(2):
                b = full(dve, f"KT{d}")
                taken(tt_(kw[:, d], b[:, :].rearrange("p (h s) -> p h s", h=4),
                          over(sm[:, 224 + 12 * d:228 + 12 * d], [P, 4, P], 2), ALU.mult))
            dve.wait_ge(e_ready, 1)
            for tt in range(TT):
                b = full(dve, f"QK{tt}")
                for d in range(2):
                    u = 4 * (2 * d + tt)
                    ins = stt(W[:, u:u + 4, :], E[:, u:u + 4, :], QK_SCALE,
                              b[:, :].rearrange("p (h s) -> p h s", h=4), ALU.mult, ALU.mult)
                    if d:
                        taken(ins)
            dve.wait_ge(v_chain, n[0])
            tail(dve.tensor_reduce(sm[:, 980:996], W[:, :, :], AX.X, ALU.add), w_ready)
            b = full(dve, "nn")
            taken(dve.tensor_copy(sm[:, 240:248], b[:, 0:8]))
            emptied(dve, "gu1")
            for tt in range(TT):
                b = full(dve, f"SP{tt}")
                for g in range(NH):
                    c = slice(g * P, g * P + P)
                    ins = stt(gu[:, tt, c], b[:, c], v1(V_BS, g), gu[:, tt, c], ALU.add, ALU.mult)
                taken(ins)
            b = full(dve, "dI")
            den, r = sm[:, 980:996], sm[:, 248:264]
            taken(tt_(sm[:, 300:308], b[:, 0:8], exo[:, 16:24], ALU.mult))
            link(tt_(den[:, 4:12], den[:, 4:12], sm[:, 300:308], ALU.add))
            link(stt(r, den, -1.0, den, ALU.mult, ALU.max))
            link(tt_(r, r, exo[:, 0:16], ALU.max))
            link(dve.reciprocal(r, r))
            link(tt_(sm[:, 300:308], exo[:, 16:24], r[:, 4:12], ALU.mult))
            for j in range(4):
                b = full(dve, f"NI{j}")
                taken(tt_(num[:, 4 * j:4 * j + 4, :], b[:, :].rearrange("p (h s) -> p h s", h=4),
                          over(r[:, 4 * j:4 * j + 4], [P, 4, P], 2), ALU.mult))
            for d in range(2):
                b = full(dve, f"CI{d}")
                for hh in range(NH):
                    u = 4 + 4 * d + hh
                    ins = stt(num[:, u], b[:, hh * P:hh * P + P], sm[:, 300 + 4 * d + hh:301 + 4 * d + hh],
                              num[:, u], ALU.mult, ALU.add)
                taken(ins)
            hs, hq = num[:, 0:8], num[:, 8:16]
            link(tt_(hs, hs, hq, ALU.add))
            link(tt_(hq, hs, hs, ALU.mult))
            tail(dve.tensor_reduce(sm[:, 272:280], hq, AX.X, ALU.add), hss_ready)
            dve.wait_ge(hsd_ready, 1)
            link(dve.reciprocal(sm[:, 280:288], sm[:, 280:288]))
            link(tt_(hs, hs, over(sm[:, 280:288], [P, 8, P], 2), ALU.mult))
            tho2 = tho[:, :, :].rearrange("p t n -> p (t n)")
            tail(stt(tho2, tho2, 1.0, hs.rearrange("p u s -> p (u s)"), ALU.add, ALU.mult), y_ready)
            for g in range(4):
                b = full(dve, f"yT{g}")
                if g < 2:
                    for j in range(2):
                        k = 2 * g + j
                        ins = ts_(yT[:, k], b[:, j * S:j * S + S], v1(V_GHEAD, k), 0.5, ALU.mult, ALU.mult)
                    taken(ins)
                else:
                    taken(dve.tensor_copy(yT[:, 2 * g:2 * g + 2].rearrange("p k s -> p (k s)"), b[:, :]))

            def residual(prefix):
                for g in range(4):
                    b = full(dve, f"{prefix}{g}")
                    v = X[:, 0, 2 * g:2 * g + 2].rearrange("p k s -> p (k s)")
                    taken(tt_(v, v, b[:, :], ALU.add))
                    squares(X[:, 0, 2 * g:2 * g + 2], H[:, 0, 2 * g:2 * g + 2])

            residual("wo")
            norm("ss3", X[:, 0], H[:, 0], lambda k: v1(V_GX, k))

            def softmax(names, heads, p, width, base, col, scale):
                def columns(c, g):
                    c += 4 * (g % TT) + heads * (g // TT)
                    return sm[:, c:c + heads]

                for g in range(len(names) + 1):
                    if g < len(names):
                        b = full(dve, names[g])
                        m = columns(col[0], g)
                        link(dve.tensor_reduce(m, b[:, :].rearrange("p (h m) -> p h m", h=heads), AX.X, ALU.max))
                        ts_(m, m, -scale).then_inc(mx_ready, 1)
                    if g:
                        emptied(dve, names[g - 1])
                        d = columns(col[1], g - 1)
                        link(dve.reciprocal(d, d))
                        h0_ = heads * ((g - 1) // TT)
                        v = p[:, (g - 1) % TT, h0_:h0_ + heads, :]
                        tt_(v, v, over(d, [P, heads, width], 2), ALU.mult).then_inc(pn_ready, 1)

            softmax([f"S{g}" for g in range(4)], 2, px, 256, 0, (288, 296), X_SCALE)
            residual("xw")
            norm("ss4", X[:, 0], H[:, 0], lambda k: v1(V_GMOE, k))

            b = full(dve, "lg")
            lg = sm[:, 392:464].rearrange("p (t e) -> p t e", t=2)
            taken(tt_(lg, b[:, 0:72].rearrange("p (t e) -> p t e", t=2), over(rb[:, :], [P, 2, 36], 1), ALU.add))
            scr = sm[:, 500:564].rearrange("p (t e) -> p t e", t=2)

            def first_max(vals, w, mx, one):
                s = scr[:, :, 0:w]
                link(dve.tensor_reduce(mx, vals, AX.X, ALU.max))
                link(tt_(s, vals, over(mx, [P, 2, w], 2), ALU.is_equal))
                link(ts_(s, s, -64.0, 64.0, ALU.mult, ALU.add))
                link(tt_(s, s, over(iota[:, 0:w], [P, 2, w], 1), ALU.add))
                link(dve.tensor_reduce(sm[:, 570:572], s, AX.X, ALU.min))
                link(tt_(one, over(iota[:, 0:w], [P, 2, w], 1), over(sm[:, 570:572], [P, 2, w], 2), ALU.is_equal))

            gl, el = lg[:, :, 0:NG], lg[:, :, NG:NG + NE]
            gmax, m1, m2 = sm[:, 572:574], sm[:, 574:576], sm[:, 576:578]
            og = sm[:, 580:588].rearrange("p (t g) -> p t g", t=2)
            first_max(gl, NG, gmax, og)
            tail(tt_(sm[:, 464:472].rearrange("p (t g) -> p t g", t=2), gl, over(gmax, [P, 2, NG], 2),
                     ALU.subtract), ge_ready)
            em = sm[:, 588:652]
            em4 = em.rearrange("p (q e) -> p q e", q=8)
            em3 = em.rearrange("p (t e) -> p t e", t=2)
            link(dve.tensor_copy(em3, el))
            link(tt_(em4, em4, over(sm[:, 580:588], [P, 8, EPG], 2), ALU.mult))
            link(ts_(sm[:, 652:660], sm[:, 580:588], BIG, -BIG, ALU.mult, ALU.add))
            link(tt_(em4, em4, over(sm[:, 652:660], [P, 8, EPG], 2), ALU.add))
            o1 = sm[:, 664:728].rearrange("p (t e) -> p t e", t=2)
            o2 = sm[:, 728:792].rearrange("p (t e) -> p t e", t=2)
            first_max(em3, NE, m1, o1)
            link(stt(em, sm[:, 664:728], -2.0 * BIG, em, ALU.mult, ALU.add))
            first_max(em3, NE, m2, o2)
            tail(tt_(sm[:, 482:484], m2, m1, ALU.subtract), me_ready)
            tail(tt_(sm[:, 320:384], sm[:, 664:728], sm[:, 728:792], ALU.add), A_ready)
            dve.wait_ge(ge_exp, 1)
            link(dve.tensor_reduce(sm[:, 486:488], sm[:, 472:480].rearrange("p (t g) -> p t g", t=2), AX.X, ALU.add))
            dve.wait_ge(me_exp, 1)
            w1_, w2_ = sm[:, 488:490], sm[:, 490:492]
            link(stt(sm[:, 486:488], sm[:, 484:486], 1.0, sm[:, 486:488], ALU.add, ALU.mult))
            link(dve.reciprocal(w1_, sm[:, 486:488]))
            link(tt_(w2_, w1_, sm[:, 484:486], ALU.mult))
            b = full(dve, "pos")
            posn = sm[:, 792:888]
            link(dve.tensor_copy(sm[0:32, 888:889], b[0:32, 96:97]))
            taken(dve.tensor_copy(posn, b[:, 0:96]))
            tail(ts_(sm[0:32, 1000:1128], ones[0:32, :], sm[0:32, 888:889]), cnt_ready)
            b = full(dve, "start")
            taken(dve.tensor_copy(sm[:, 1034 - 134:1034 - 134 + 32], b[:, 0:32]))
            strt = sm[:, 900:932]
            slt = sm[:, 792:856].rearrange("p (t e) -> p t e", t=2)
            for q in range(4):
                ins = ts_(win[0:1, q * NE:q * NE + NE], strt[0:1, :], float(C * q), float(A), ALU.add, ALU.min)
                link(ins) if q < 3 else tail(ins, win_ready)
            link(dve.tensor_reduce(sm[0:1, 889:890], sm[0:1, 856:888], AX.X, ALU.max))
            tail(dve.tensor_copy(mxc[:, :], sm[0:1, 889:890]), win_ready)
            link(tt_(slt, slt, over(strt, [P, 2, NE], 1), ALU.add))
            for o, c in ((664, 478), (728, 480)):
                link(tt_(sm[:, 500:564], sm[:, o:o + 64], sm[:, 792:856], ALU.mult))
                link(dve.tensor_reduce(sm[:, c:c + 2], scr, AX.X, ALU.add))
            for tt in range(TT):
                s1, s2 = sm[:, 478 + tt:479 + tt], sm[:, 480 + tt:481 + tt]
                link(ts_(Pw[:, tt], iota, s1, None, ALU.is_equal))
                ins = stt(Pm[:, tt], iota, s2, Pw[:, tt], ALU.is_equal, ALU.add)
                link(ins)
            tail(dve.memset(xs[:, :, A:AP_], 0.0), P_ready)

            def split_lo(m, e, parity, between=None):
                for q in range(1, 4):
                    if between and q == 2:
                        between()
                    dve.wait_ge(hi_done[q], chunk_number(m, e) + 1)
                    tt_(w_lo[:, q, :], quarter(m, parity, q), w_hi[:, q, :].bitcast(F32), ALU.subtract)\
                        .then_inc(lo_done[q], 1)

            split_lo("G", 0, 0)
            for tt in range(TT):
                s1, s2 = sm[:, 478 + tt:479 + tt], sm[:, 480 + tt:481 + tt]
                link(ts_(Pw[:, tt], iota, s1, w1_[:, tt:tt + 1], ALU.is_equal, ALU.mult))
                link(ts_(ys[:, 0, 0:A], iota, s2, w2_[:, tt:tt + 1], ALU.is_equal, ALU.mult))
                link(tt_(Pw[:, tt], Pw[:, tt], ys[:, 0, 0:A], ALU.add))
            modulation(0)
            modulation(1)
            emptied(dve, "css")
            link(dve.reciprocal(rs[:, 1], sd[:, 1]))
            modulated_norm(0, 1, ctx_ready)

            full(dve, "xs7")

            def starts_at(e):
                return dve.value_load(win[0:1, bass.ds(e, 1)], min_val=0, max_val=A)

            def rows_lo(e):
                w0 = starts_at(e)
                dve.wait_ge(x_hi_ready, e + 1)
                tt_(x_hl[:, :, C:2 * C], xs[:, :, bass.ds(w0, C)], x_hl[:, :, 0:C].bitcast(F32), ALU.subtract)\
                    .then_inc(x_lo_ready, 1)

            def both(b):
                v = b[:, :].rearrange("p (k h c) -> p k h c", k=4, h=2)
                return v[:, :, 0, :], v[:, :, 1, :]

            def vector_step(e, parity, gate=True, one=True, two=True, more=True):
                if gate and not (isinstance(e, int) and e == 0):
                    split_lo("G", e, parity)
                if one:
                    dve.wait_ge(tanh_ready, e)
                    stt(th, th, 1.0, gT, ALU.add, ALU.mult).then_inc(act_mid, 1)
                if gate:
                    split_lo("U", e, parity)
                if one:
                    dve.wait_ge(u_turned, e)
                    dve.tensor_copy(uT, both(eb[5])[0]).then_inc(chain_u, 1)
                    dve.wait_ge(chain_u, e)
                    tt_(uT, uT, both(eb[5])[1], ALU.add).then_inc(u_summed, 1)
                    dve.wait_ge(u_summed, e)
                    if two:
                        dve.wait_ge(a_lo_ready, e - 1)
                    stt(aT, th, 0.5, uT, ALU.mult, ALU.mult).then_inc(act_ready, 1)

                    def act_lo():
                        dve.wait_ge(a_hi_ready, e)
                        tt_(a_hl[:, :, C:2 * C], aT, a_hl[:, :, 0:C].bitcast(F32), ALU.subtract)\
                            .then_inc(a_lo_ready, 1)

                    split_lo("D", e - 1, 1 - parity, act_lo)
                if gate:
                    if more:
                        rows_lo(e + 1)
                    dve.wait_ge(g_turned, e + 1)
                    dve.tensor_copy(gT, both(eb[4])[0]).then_inc(chain_g, 1)
                    dve.wait_ge(chain_g, e + 1)
                    tt_(gT, gT, both(eb[4])[1], ALU.add).then_inc(g_summed, 1)
                if two:
                    w0 = starts_at(e - 2)
                    dve.wait_ge(y_turned, e - 1)
                    for b_ in range(2):
                        hi, lo = both(eb[6 + b_])
                        o = ys[:, 4 * b_:4 * b_ + 4, bass.ds(w0, C)]
                        dve.tensor_copy(y_sum[:, 4 * b_:4 * b_ + 4], hi).then_inc(chain_y, 1)
                        dve.wait_ge(chain_y, (e - 2) * 2 + (b_ + 1))
                        ins = tt_(o, y_sum[:, 4 * b_:4 * b_ + 4], lo, ALU.add)
                    ins.then_inc(ys_ready, 1)

            rows_lo(0)
            vector_step(0, 0, one=False, two=False)
            vector_step(1, 1, two=False)
            each_expert(dve, 2, NE - 3, vector_step)
            vector_step(NE - 2, 0)
            vector_step(NE - 1, 1, more=False)
            vector_step(NE, 0, gate=False)
            vector_step(NE + 1, 1, gate=False, one=False)

            rows_max = dve.value_load(mxc[0:1, 0:1], min_val=0, max_val=S)
            with dve.If(rows_max > C):
                with dve.Fori(0, NE) as e:
                    for q in range(4):
                        dve.wait_ge(slow[TH], e * 4 + (q + 1))
                        dve.wait_ge(slow[UF], e * 4 + (q + 1))
                        stt(sth, sth, 1.0, eb[0][0:C, :], ALU.add, ALU.mult).then_inc(chain_s, 1)
                        dve.wait_ge(chain_s, e * 4 + (q + 1))
                        stt(sac, sth, 0.5, eb[2][0:C, :], ALU.mult, ALU.mult).then_inc(slow[AC], 1)
                        dve.wait_ge(slow[YF], e * 4 + (q + 1))
                        dve.tensor_copy(sy[:, 0:512], eb[5][0:C, :])
                        dve.tensor_copy(sy[:, 512:1024], eb[6][0:C, :]).then_inc(slow[YB], 1)

            for g in range(0, 8, 2):
                st, half = divmod(g, 2)
                b = full(dve, f"yt{g}")
                taken(dve.tensor_copy(yk[st][:, half * 512:half * 512 + 512], b[:, :]))
            residual("co")
            norm("ss5", X[:, 0], X[:, 0], lambda k: v1(V_GFIN, k))
            for g in range(4):
                squares(X[:, 0, 2 * g:2 * g + 2], H[:, 0, 2 * g:2 * g + 2])

            for L in range(2):
                R = 2 - L
                pc2, pcT2, px2, pT2 = attention_room(L)

                def two(v):
                    return v.rearrange("p r s -> p (r s)")

                emptied(dve, f"{L}ss")
                for r in range(1 + L):
                    link(dve.reciprocal(rs[:, r], sd[:, r]))
                    modulated_norm(L, r, h_ready)
                emptied(dve, f"{L}qkv{2 * L + 1}")
                qsq = view(11296, 1536, t=4, n=384)

                def heads(v, t0, t1, h0_, h1_):
                    return v[:, t0:t1, h0_ * HD2:h1_ * HD2].rearrange("p t (h e) -> p t h e", e=HD2)

                parts = [(0, 4, 0, 6)] if L == 0 else [(0, 2, 0, 6), (2, 4, 4, 6)]
                for a0, a1, b0, b1 in parts:
                    link(tt_(heads(qsq, a0, a1, b0, b1), heads(qkv, a0, a1, b0, b1),
                             heads(qkv, a0, a1, b0, b1), ALU.mult))
                ssq = sm[:, 600:624].rearrange("p (t h) -> p t h", t=4)
                link(dve.memset(sm[:, 600:624], 1.0))
                for n_, (a0, a1, b0, b1) in enumerate(parts):
                    ins = dve.tensor_reduce(ssq[:, a0:a1, b0:b1], heads(qsq, a0, a1, b0, b1), AX.X, ALU.add)
                    tail(ins, qs_ready) if n_ == len(parts) - 1 else link(ins)
                dve.wait_ge(qd_ready, L + 1)
                link(dve.reciprocal(sm[:, 648:672], sm[:, 624:648]))
                rq = sm[:, 648:672].rearrange("p (t h) -> p t h", t=4)
                for a0, a1, b0, b1 in parts:
                    for ta in range(a0, a1):
                        v = heads(qkv, ta, ta + 1, b0, b1)[:, 0]
                        link(tt_(v, v, over(rq[:, ta, b0:b1], [P, b1 - b0, HD2], 2), ALU.mult))
                        ins = tt_(v, v, gains[:, L, b0:b1, :], ALU.mult)
                        link(ins)
                weights(dve, f"{L}const")
                rope = ring[:, place[f"{L}const"], ROPE0:ROPE0 + 128].rearrange("p (t c a f) -> p t c a f", t=2, c=2, a=2)
                for tt in range(TT):
                    v = qkv[:, tt, 0:384].rearrange("p (h a w f) -> p h a w f", h=6, a=2, w=2)
                    for a in range(2):
                        x1, x2 = v[:, :, a, 0, :], v[:, :, a, 1, :]
                        cos = over(rope[:, tt, 0, a, :], [P, 6, 16], 1)
                        sin = over(rope[:, tt, 1, a, :], [P, 6, 16], 1)
                        T = [sm[:, 500 + 96 * 0:596], sm[:, 1000:1096], sm[:, 792:888], sm[:, 392:488]]
                        T = [x.rearrange("p (h f) -> p h f", h=6) for x in T]
                        for o, p1, p2 in ((T[0], x1, cos), (T[1], x2, sin), (T[2], x2, cos), (T[3], x1, sin)):
                            ins = tt_(o, p1, p2, ALU.mult)
                        link(ins)
                        tt_(x1, T[0], T[1], ALU.subtract)
                        ins = tt_(x2, T[2], T[3], ALU.add)
                        tail(ins, rope_ready) if tt == 1 and a == 1 else link(ins)
                link(dve.memset(tp[:, :, :, 0:1], 0.0))
                link(dve.memset(tp[:, :, :, 1 + S:2 + S], 0.0))
                for i in range(2):
                    emptied(dve, f"{L}c{i}")
                    b = full(dve, f"{L}h{i}")
                    taken(tt_(tp[:, i, 0:R, 1:1 + S], b[:, 0:R * S].rearrange("p (r s) -> p r s", r=R),
                              cs2[:, i, 0:R], ALU.mult))
                for i in range(2):
                    o = cs2[:, i, 0:R]

                    def cw2(w):
                        return v2(V_CW2, (L * 3 + w) * 2 + i)

                    link(ts_(o, tp[:, i, 0:R, 0:S], cw2(0), v2(V_CB2, 2 * L + i), ALU.mult, ALU.add))
                    for w in (1, 2):
                        link(stt(o, tp[:, i, 0:R, w:w + S], cw2(w), o, ALU.mult, ALU.add))
                    link(tt_(o, o, bs2[:, i, 0:R], ALU.mult))
                emptied(dve, f"{L}zc1")
                link(tt_(oT[:, 4, 0:R], oT[:, 4, 0:R], cs2[:, 0, 0:R], ALU.mult))
                tail(tt_(oT[:, 5, 0:R], oT[:, 5, 0:R], cs2[:, 1, 0:R], ALU.mult), conv2_ready)
                if L == 0:
                    softmax([f"0cS{g}" for g in range(4)], 2, pc2, 256, 4, (680, 688), A_SCALE)
                softmax([f"{L}xS{g}" for g in range(8)], 1, px2, 512, 8 + 8 * L, (700, 708), A_SCALE)
                for i in range(2):
                    b = full(dve, f"{L}pl{i}")
                    emptied(dve, f"{L}zp{i}")
                    o = two(oT[:, 6 + i, 0:R])
                    taken(stt(o, b[:, 0:R * S], v2(V_PS, 2 * L + i), o, ALU.mult, ALU.mult))
                for i in range(2):
                    b = full(dve, f"{L}wf{i}")
                    emptied(dve, f"{L}zf{i}")
                    o = two(oT[:, i, 0:R])
                    taken(tt_(o, o, b[:, 0:R * S], ALU.mult))
                if L == 0:
                    for i in range(2):
                        b = full(dve, f"0co{i}")
                        o = oT[:, 2 + i, 1]
                        taken(tt_(o, o, b[:, 0:S], ALU.mult))
                for i in range(2):
                    b = full(dve, f"{L}xo{i}")
                    o = oT[:, 2 + i, 0]
                    taken(tt_(o, o, b[:, 0:S], ALU.mult))
                for k in range(KT):
                    b = full(dve, f"{L}out{k}")
                    for r in range(R):
                        ins = stt(X[:, r, k], b[:, r * S:r * S + S], mod[:, L, 16 + k, r:r + 1], X[:, r, k],
                                  ALU.mult, ALU.add)
                    taken(ins)
                    if L == 0:
                        for r in range(2):
                            ins = tt_(H[:, r, k], X[:, r, k], X[:, r, k], ALU.mult)
                        if k % 2:
                            ins.then_inc(sq_ready, 1)


def constants():
    import numpy as np

    i, j = np.arange(P)[:, None], np.arange(P)[None, :]
    one = np.zeros((P, CONST1), np.float32)
    for at, m in ((ID0, i == j), (TRF0, i <= j), (TRB0, i >= j), (TRS0, i < j), (ONE0, i == i + 0 * j),
                  (MKF0, np.where(j <= i, 0.0, -BIG)), (MKB0, np.where(j >= i, 0.0, -BIG))):
        one[:, at:at + P] = m
    one[:, IO0:] = np.arange(A)[None, :]

    def by_tile(m):
        return m.reshape(TT, P, -1).transpose(1, 0, 2).reshape(P, -1)

    two = np.zeros((P, CONST2), np.float32)
    a = 2 * np.pi * (np.outer(np.arange(S), np.arange(S)) % S) / S
    two[:, DFT0:CD0] = by_tile(np.concatenate([np.cos(a), np.sin(a)], 1) / np.sqrt(S))
    a = 2 * np.pi * (np.outer(np.arange(64), np.arange(64)) % 64) / 64
    for h in range(2):
        c = slice(64 * h, 64 * h + 64)
        two[c, CD0 + 64 * h:CD0 + 64 * h + 64] = np.cos(a) / 8
        two[c, CD0 + P + 64 * h:CD0 + P + 64 * h + 64] = -np.sin(a) / 8
    pool = np.zeros((S, 4, S))
    tok = np.arange(S)
    for n, w in enumerate((2, 4, 8, 16)):
        lo, hi = np.clip(tok - w // 2, 0, S), np.clip(tok + w - w // 2, 0, S)
        inside = (tok[:, None] >= lo[None, :]) & (tok[:, None] < hi[None, :])
        pool[:, n, :] = inside / (hi - lo)[None, :] - np.eye(S)
    two[:, POOL0:ROPE0] = by_tile(pool)
    inv = 10000.0 ** (-np.arange(16) / 16)
    ang = np.stack([(tok // 64)[:, None] * inv, (tok % 64)[:, None] * inv], 1)
    two[:, ROPE0:] = by_tile(np.stack([np.cos(ang), np.sin(ang)], 1))
    return one, two


_INS = ['x', 'mem', 'g_mix', 'w_in', 'conv_w', 'conv_b', 'gate_b', 'g_head', 'ln_v_g', 'ln_v_b', 'w_s', 'b_s',
        'w_out', 'g_xattn', 'g_mem', 'w_q_x', 'w_kv_x', 'w_o_x', 'g_moe', 'w_rg', 'b_rg', 'w_re', 'b_re',
        'w_gate', 'w_up', 'w_down', 'g_final', 'c_2', 'ctx_2', 'c_ctx_2', 'w_mod_2', 'b_mod_2', 'norm_g_2',
        'w_in_2', 'q_gain_2', 'k_gain_2', 'w_fourier_2', 'conv_w_2', 'conv_b_2', 'pool_w_2', 'pool_scale_2',
        'w_out_2']


def kernel(**inputs):
    import numpy as _np
    import concourse.bacc as _bacc
    from concourse import mybir as _mybir
    from concourse.bass_utils import run_bass_kernel_spmd as _run

    nc = _bacc.Bacc("TRN2", target_bir_lowering=False, num_devices=1, dynamic_dma_scratch_size=1024)
    arrays, tensors = {}, {}
    one, two = constants()
    for name, a in [(n, inputs[n]) for n in _INS] + [("const1", one), ("const2", two)]:
        a = _np.ascontiguousarray(a)
        arrays[f"in_{name}_dram"] = a
        tensors[name] = nc.dram_tensor(f"in_{name}_dram", a.shape, _mybir.dt.from_np(a.dtype),
                                       kind="ExternalInput").ap()
    tensors["out"] = nc.dram_tensor("out_0_dram", (1, S, D), F32, kind="ExternalOutput").ap()
    first_and_second_block(nc, tensors)
    r = _run(nc, [arrays], core_ids=[0])
    return r.results[0]["out_0_dram"]
```
